# Optimizing a Trainium2 kernel written in Bass

```python
import jax
import jax.numpy as jnp
from jax import lax
import numpy as np
import math

D_MODEL = 1024
BATCH = 1
SEQ = 1024
DEPTH = 1

GRID_W = 64
CTX_LEN = 256
MLSTM_HEADS = 4
MLSTM_DH = 128
MLSTM_W = MLSTM_HEADS * MLSTM_DH
MLSTM_CHUNK = 64
QK_CONV = 3
N_GATES = 4 * MLSTM_HEADS
ATTN_HEADS = 8
KV_HEADS = 2
ATTN_DH = 64
ATTN_W = ATTN_HEADS * ATTN_DH
KV_W = KV_HEADS * ATTN_DH
GQA_GROUP = ATTN_HEADS // KV_HEADS
WINDOW = 128
ATTN_BLOCK = 128
ROPE_BASE = 10000.0
ROPE_AXIS_PAIRS = ATTN_DH // 4
MIX_W = MLSTM_W + ATTN_W
IN_SPLITS = (2 * MLSTM_W, 3 * MLSTM_W, 4 * MLSTM_W, 4 * MLSTM_W + N_GATES,
             4 * MLSTM_W + N_GATES + ATTN_W, 4 * MLSTM_W + N_GATES + ATTN_W + KV_W)
IN_COLS = 4 * MLSTM_W + N_GATES + ATTN_W + 2 * KV_W
D_FF = 2816
FFN_CONV = 3
EPS = 1e-6


def rmsnorm(x, g):
    xf = x.astype(jnp.float32)
    y = xf * lax.rsqrt(jnp.mean(xf * xf, axis=-1, keepdims=True) + EPS)
    return (y * g.astype(jnp.float32)).astype(x.dtype)

def modulate(h, shift, scale):
    return h * (1 + scale) + shift

def dwconv(x, w, b):
    k = w.shape[0]
    y = lax.conv_general_dilated(x, w[:, None, :], window_strides=(1,), padding=[(k // 2, k // 2)],
                                 dimension_numbers=('NWC', 'WIO', 'NWC'),
                                 feature_group_count=x.shape[-1])
    return y + b

def heads_first(t, n_heads):
    b, l, _ = t.shape
    return t.reshape(b, l, n_heads, -1).transpose(0, 2, 1, 3)

def axial_rope(n_tokens):
    rows = n_tokens // GRID_W
    r, col = jnp.meshgrid(jnp.arange(rows, dtype=jnp.float32), jnp.arange(GRID_W, dtype=jnp.float32),
                          indexing='ij')
    inv = ROPE_BASE ** (-jnp.arange(ROPE_AXIS_PAIRS, dtype=jnp.float32) / ROPE_AXIS_PAIRS)
    ang = jnp.stack([r.reshape(-1)[:, None] * inv, col.reshape(-1)[:, None] * inv], axis=1)
    return jnp.cos(ang), jnp.sin(ang)

def apply_rope(x, cos, sin):
    b, l, h, _ = x.shape
    xr = x.astype(jnp.float32).reshape(b, l, h, 2, 2, ROPE_AXIS_PAIRS)
    x0, x1 = xr[..., 0, :], xr[..., 1, :]
    cs, sn = cos[:, None], sin[:, None]
    y = jnp.stack([x0 * cs - x1 * sn, x0 * sn + x1 * cs], axis=-2)
    return y.reshape(b, l, h, ATTN_DH).astype(x.dtype)

def project_tokens(h, w_in, qk_conv_w, qk_conv_b, gate_b):
    b, l, _ = h.shape
    u = h @ w_in
    qk, v_m, o_m, gates, q_a, k_a, v_a = jnp.split(u, IN_SPLITS, axis=-1)
    q_m, k_m = jnp.split(jax.nn.silu(dwconv(qk, qk_conv_w, qk_conv_b)), 2, axis=-1)
    q_m = heads_first(q_m, MLSTM_HEADS).astype(jnp.float32)
    k_m = heads_first(k_m, MLSTM_HEADS).astype(jnp.float32) * (MLSTM_DH ** -0.5)
    v_m = heads_first(v_m, MLSTM_HEADS).astype(jnp.float32)
    g = (gates + gate_b).astype(jnp.float32).reshape(b, l, 4, MLSTM_HEADS).transpose(2, 0, 3, 1)
    gates = (g[0], jax.nn.log_sigmoid(g[1]), g[2], jax.nn.log_sigmoid(g[3]))
    q_a = q_a.reshape(b, l, ATTN_HEADS, ATTN_DH)
    k_a = k_a.reshape(b, l, KV_HEADS, ATTN_DH)
    v_a = v_a.reshape(b, l, KV_HEADS, ATTN_DH)
    return q_m, k_m, v_m, o_m, gates, q_a, k_a, v_a

def init_state(b):
    return (jnp.zeros((b, MLSTM_HEADS, MLSTM_DH, MLSTM_DH), jnp.float32),
            jnp.zeros((b, MLSTM_HEADS, MLSTM_DH), jnp.float32),
            jnp.zeros((b, MLSTM_HEADS), jnp.float32))

def mlstm_scan(q, k, v, log_i, log_f, init, return_h):
    b, h, l, dh = k.shape
    nc = l // MLSTM_CHUNK
    chunk = lambda t: t.reshape((b, h, nc, MLSTM_CHUNK) + t.shape[3:])
    k, v, li, lf = chunk(k), chunk(v), chunk(log_i), chunk(log_f)
    cum = jnp.cumsum(lf, axis=-1)
    cum_end = cum[..., -1]
    g = cum_end[..., None] - cum + li
    m_loc = jnp.max(g, axis=-1)
    w = jnp.exp(g - m_loc[..., None])
    c_loc = jnp.einsum('bhnsd,bhnse->bhnde', w[..., None] * k, v)
    n_loc = jnp.einsum('bhns,bhnsd->bhnd', w, k)

    def step(carry, inp):
        c_st, n_st, m_st = carry
        c_l, n_l, m_l, bt = inp
        m_new = jnp.maximum(bt + m_st, m_l)
        a = jnp.exp(bt + m_st - m_new)
        s = jnp.exp(m_l - m_new)
        return (a[..., None, None] * c_st + s[..., None, None] * c_l,
                a[..., None] * n_st + s[..., None] * n_l, m_new), (c_st, n_st, m_st)

    final, starts = lax.scan(step, init, tuple(jnp.moveaxis(t, 2, 0) for t in (c_loc, n_loc, m_loc, cum_end)))
    if not return_h:
        return None, final
    c0, n0, m0 = (jnp.moveaxis(t, 0, 2) for t in starts)
    q = chunk(q)
    a_log = cum + m0[..., None]
    d_log = cum[..., :, None] - cum[..., None, :] + li[..., None, :]
    order = jnp.tril(jnp.ones((MLSTM_CHUNK, MLSTM_CHUNK), dtype=bool))
    d_log = jnp.where(order, d_log, -jnp.inf)
    m_t = jnp.maximum(a_log, jnp.max(d_log, axis=-1))
    dec = jnp.exp(d_log - m_t[..., None])
    inter = jnp.exp(a_log - m_t)
    s = jnp.einsum('bhntd,bhnsd->bhnts', q, k) * dec
    num = jnp.einsum('bhnts,bhnse->bhnte', s, v) + inter[..., None] * jnp.einsum('bhntd,bhnde->bhnte', q, c0)
    den = jnp.sum(s, axis=-1) + inter * jnp.einsum('bhntd,bhnd->bhnt', q, n0)
    hid = num / jnp.maximum(jnp.abs(den), jnp.exp(-m_t))[..., None]
    return hid.reshape(b, h, l, dh), final

def mlstm_bidirectional(q, k, v, gates, init_f, init_b, return_h):
    li_f, lf_f, li_b, lf_b = gates
    flip = lambda t: jnp.flip(t, axis=2)
    h_f, st_f = mlstm_scan(q, k, v, li_f, lf_f, init_f, return_h)
    h_b, st_b = mlstm_scan(flip(q), flip(k), flip(v), flip(li_b), flip(lf_b), init_b, return_h)
    hid = h_f + flip(h_b) if return_h else None
    return hid, st_f, st_b

def mlstm_merge(h, o, gain):
    b, _, l, _ = h.shape
    hn = h * lax.rsqrt(jnp.mean(h * h, axis=-1, keepdims=True) + EPS)
    hn = hn.transpose(0, 2, 1, 3).reshape(b, l, MLSTM_W) * gain.astype(jnp.float32)
    return (hn * jax.nn.sigmoid(o.astype(jnp.float32))).astype(o.dtype)

def window_attention(q, k, v, k_ctx, v_ctx, sink):
    b, l = q.shape[:2]
    nb = l // ATTN_BLOCK
    qb = q.reshape(b, nb, ATTN_BLOCK, KV_HEADS, GQA_GROUP, ATTN_DH)

    def band(t):
        tb = jnp.pad(t.reshape(b, nb, ATTN_BLOCK, KV_HEADS, ATTN_DH), ((0, 0), (1, 1), (0, 0), (0, 0), (0, 0)))
        return jnp.concatenate([tb[:, :-2], tb[:, 1:-1], tb[:, 2:]], axis=2)

    kb, vb = band(k), band(v)
    n_band = 3 * ATTN_BLOCK
    qpos = jnp.arange(l).reshape(nb, ATTN_BLOCK)
    kpos = qpos[:, :1] - ATTN_BLOCK + jnp.arange(n_band)
    valid = ((jnp.abs(kpos[:, None, :] - qpos[:, :, None]) <= WINDOW)
             & (kpos >= 0)[:, None, :] & (kpos < l)[:, None, :])
    s_band = jnp.einsum('bnqhgd,bnkhd->bnhgqk', qb, kb).astype(jnp.float32)
    s_band = jnp.where(valid[None, :, None, None], s_band, -jnp.inf)
    s_ctx = jnp.einsum('bnqhgd,bchd->bnhgqc', qb, k_ctx).astype(jnp.float32)
    s_sink = jnp.broadcast_to(sink.astype(jnp.float32).reshape(KV_HEADS, GQA_GROUP, 1, 1),
                              s_band.shape[:-1] + (1,))
    p = jax.nn.softmax(jnp.concatenate([s_band, s_ctx, s_sink], axis=-1), axis=-1).astype(v.dtype)
    out = (jnp.einsum('bnhgqk,bnkhd->bnqhgd', p[..., :n_band], vb)
           + jnp.einsum('bnhgqc,bchd->bnqhgd', p[..., n_band:n_band + k_ctx.shape[1]], v_ctx))
    return out.reshape(b, l, ATTN_W)

def context_attention(q, k, v, sink):
    b, n = q.shape[:2]
    qg = q.reshape(b, n, KV_HEADS, GQA_GROUP, ATTN_DH)
    s = jnp.einsum('bqhgd,bkhd->bhgqk', qg, k).astype(jnp.float32)
    s_sink = jnp.broadcast_to(sink.astype(jnp.float32).reshape(KV_HEADS, GQA_GROUP, 1, 1), s.shape[:-1] + (1,))
    p = jax.nn.softmax(jnp.concatenate([s, s_sink], axis=-1), axis=-1)[..., :-1].astype(v.dtype)
    return jnp.einsum('bhgqk,bkhd->bqhgd', p, v).reshape(b, n, ATTN_W)

def conv_glu(h, w_up, conv_w, conv_b, w_down):
    a, val = jnp.split(h @ w_up, 2, axis=-1)
    a = jax.nn.gelu(dwconv(a, conv_w, conv_b))
    return (a * val) @ w_down

def first_inputs(seed: int = 0) -> dict:
    key = jax.random.key(seed)
    ks = jax.random.split(key, 20)
    nrm = lambda k, shape, s: jax.random.normal(k, shape, jnp.float32) * s
    f_bias = jnp.linspace(3.0, 6.0, MLSTM_HEADS, dtype=jnp.float32)
    zero_h = jnp.zeros((MLSTM_HEADS,), jnp.float32)
    gate_base = jnp.stack([zero_h, f_bias, zero_h, f_bias]).reshape(-1)
    return {
        'x': nrm(ks[0], (BATCH, SEQ, D_MODEL), 1.0),
        'c': nrm(ks[1], (BATCH, D_MODEL), 1.0),
        'ctx': nrm(ks[2], (BATCH, CTX_LEN, D_MODEL), 1.0),
        'c_ctx': nrm(ks[3], (D_MODEL,), 1.0),
        'w_ada': nrm(ks[4], (DEPTH, D_MODEL, 6 * D_MODEL), 0.5 * D_MODEL ** -0.5),
        'b_ada': nrm(ks[5], (DEPTH, 6 * D_MODEL), 0.02),
        'norm_mix': 1.0 + nrm(ks[6], (DEPTH, D_MODEL), 0.02),
        'norm_ffn': 1.0 + nrm(ks[7], (DEPTH, D_MODEL), 0.02),
        'w_in': nrm(ks[8], (DEPTH, D_MODEL, IN_COLS), D_MODEL ** -0.5),
        'gate_b': gate_base[None, :] + nrm(ks[9], (DEPTH, N_GATES), 0.1),
        'qk_conv_w': nrm(ks[10], (DEPTH, QK_CONV, 2 * MLSTM_W), QK_CONV ** -0.5),
        'qk_conv_b': nrm(ks[11], (DEPTH, 2 * MLSTM_W), 0.02),
        'mlstm_norm': 1.0 + nrm(ks[12], (DEPTH, MLSTM_W), 0.02),
        'attn_sink': nrm(ks[13], (DEPTH, ATTN_HEADS), 0.5),
        'w_out': nrm(ks[14], (DEPTH, MIX_W, D_MODEL), MIX_W ** -0.5),
        'w_up': nrm(ks[15], (DEPTH, D_MODEL, 2 * D_FF), D_MODEL ** -0.5),
        'ffn_conv_w': nrm(ks[16], (DEPTH, FFN_CONV, D_FF), FFN_CONV ** -0.5),
        'ffn_conv_b': nrm(ks[17], (DEPTH, D_FF), 0.02),
        'w_down': nrm(ks[18], (DEPTH, D_FF, D_MODEL), D_FF ** -0.5),
        'final_norm': 1.0 + nrm(ks[19], (D_MODEL,), 0.02),
    }

def first_block(x, c, ctx, c_ctx, w_ada, b_ada, norm_mix, norm_ffn, w_in, gate_b, qk_conv_w, qk_conv_b,
              mlstm_norm, attn_sink, w_out, w_up, ffn_conv_w, ffn_conv_b, w_down, final_norm):
    cos, sin = axial_rope(x.shape[1])
    attn_scale = ATTN_DH ** -0.5
    for l in range(DEPTH):
        last = l == DEPTH - 1
        sh_a, sc_a, g_a, sh_f, sc_f, g_f = jnp.split(
            (jax.nn.silu(c) @ w_ada[l] + b_ada[l])[:, None, :], 6, axis=-1)
        csh_a, csc_a, cg_a, csh_f, csc_f, cg_f = jnp.split(
            jax.nn.silu(c_ctx) @ w_ada[l] + b_ada[l], 6, axis=-1)

        hc = modulate(rmsnorm(ctx, norm_mix[l]), csh_a, csc_a)
        qm_c, km_c, vm_c, om_c, gates_c, qa_c, ka_c, va_c = project_tokens(
            hc, w_in[l], qk_conv_w[l], qk_conv_b[l], gate_b[l])
        zero = init_state(ctx.shape[0])
        hm_c, st_f, st_b = mlstm_bidirectional(qm_c, km_c, vm_c, gates_c, zero, zero, not last)

        hx = modulate(rmsnorm(x, norm_mix[l]), sh_a, sc_a)
        qm, km, vm, om, gates_x, qa, ka, va = project_tokens(hx, w_in[l], qk_conv_w[l], qk_conv_b[l], gate_b[l])
        hm, _, _ = mlstm_bidirectional(qm, km, vm, gates_x, st_f, st_b, True)
        y_m = mlstm_merge(hm, om, mlstm_norm[l])
        y_a = window_attention(apply_rope(qa, cos, sin) * attn_scale, apply_rope(ka, cos, sin), va,
                               ka_c, va_c, attn_sink[l])
        x = x + g_a * (jnp.concatenate([y_m, y_a], axis=-1) @ w_out[l])
        x = x + g_f * conv_glu(modulate(rmsnorm(x, norm_ffn[l]), sh_f, sc_f),
                               w_up[l], ffn_conv_w[l], ffn_conv_b[l], w_down[l])

        if not last:
            y_mc = mlstm_merge(hm_c, om_c, mlstm_norm[l])
            y_ac = context_attention(qa_c * attn_scale, ka_c, va_c, attn_sink[l])
            ctx = ctx + cg_a * (jnp.concatenate([y_mc, y_ac], axis=-1) @ w_out[l])
            ctx = ctx + cg_f * conv_glu(modulate(rmsnorm(ctx, norm_ffn[l]), csh_f, csc_f),
                                        w_up[l], ffn_conv_w[l], ffn_conv_b[l], w_down[l])
    return rmsnorm(x, final_norm)


POOL_WINDOWS = (2, 4, 8, 16)
POOL_GROUP = D_MODEL // 8
POOL_WIDTH = len(POOL_WINDOWS) * POOL_GROUP
DIL_PAIRS = ((128, 1), (512, 4), (2048, 16))
DIL_HEADS_PER_GROUP = 4
DIL_HEADS = len(DIL_PAIRS) * DIL_HEADS_PER_GROUP
DIL_HEAD_DIM = 64
DIL_QKV_WIDTH = DIL_HEADS * DIL_HEAD_DIM
DIL_OUT_WIDTH = DIL_HEADS_PER_GROUP * DIL_HEAD_DIM
REL_BUCKETS = 32
REL_MAX_DIST = 2048
SB_HEADS = 4
SB_HEAD_DIM = 128
SB_WIDTH = SB_HEADS * SB_HEAD_DIM
SB_BLOCK = 128
S5_WIDTH = D_MODEL // 2
S5_CH = 16
S5_GROUPS = S5_WIDTH // S5_CH
S5_STATE = 64
FFN_HIDDEN = ((8 * D_MODEL + 3 * 256 - 1) // (3 * 256)) * 256
N_BRANCHES = 4
IN_WIDTH = POOL_WIDTH + 3 * DIL_QKV_WIDTH + 3 * SB_WIDTH + S5_WIDTH
BRANCH_WIDTHS = (POOL_WIDTH, DIL_OUT_WIDTH, SB_WIDTH, S5_WIDTH)
BRANCH_WIDTH = sum(BRANCH_WIDTHS)


def rmsnorm_2(x, g):
    xf = x.astype(jnp.float32)
    y = xf * lax.rsqrt(jnp.mean(xf * xf, axis=-1, keepdims=True) + EPS)
    return (y * g.astype(jnp.float32)).astype(x.dtype)

def pool_mixer(u, w_grp, scale):
    B_, S_, _ = u.shape
    uf = u.astype(jnp.float32)
    cs = jnp.concatenate([jnp.zeros_like(uf[:, :1]), jnp.cumsum(uf, axis=1)], axis=1)
    t = jnp.arange(S_)
    outs = []
    for gi, w in enumerate(POOL_WINDOWS):
        sl = slice(gi * POOL_GROUP, (gi + 1) * POOL_GROUP)
        lo = jnp.maximum(t + 1 - w, 0)
        cnt = (t + 1 - lo).astype(jnp.float32)
        mean = (cs[:, 1:, sl] - cs[:, lo, sl]) / cnt[None, :, None]
        outs.append(mean - uf[:, :, sl])
    p = jnp.stack(outs, axis=2)
    y = jnp.einsum('bsgc,gcd->bsgd', p, w_grp.astype(jnp.float32)).reshape(B_, S_, POOL_WIDTH)
    return (y * scale.astype(jnp.float32)).astype(u.dtype)

def t5_bucket(dist):
    exact = REL_BUCKETS // 2
    df = jnp.maximum(dist, 1).astype(jnp.float32)
    large = exact + (jnp.log(df / exact) / math.log(REL_MAX_DIST / exact)
                     * (REL_BUCKETS - exact)).astype(jnp.int32)
    large = jnp.minimum(large, REL_BUCKETS - 1)
    return jnp.where(dist < exact, dist, large)

def dilated_group(q, k, v, bias_tab, window, dil):
    B_, S_, H, E = q.shape
    band = window // dil
    L = S_ // dil
    nb = -(-L // band)
    Lp = nb * band

    def to_sub(a):
        a = a.reshape(B_, L, dil, H, E).transpose(0, 2, 3, 1, 4)
        return jnp.pad(a, ((0, 0), (0, 0), (0, 0), (0, Lp - L), (0, 0)))

    def band_keys(a):
        a = jnp.pad(a, ((0, 0), (0, 0), (0, 0), (band, 0), (0, 0))).reshape(B_, dil, H, nb + 1, band, E)
        return jnp.concatenate([a[:, :, :, :-1], a[:, :, :, 1:]], axis=4)

    qb = to_sub(q).reshape(B_, dil, H, nb, band, E)
    kb = band_keys(to_sub(k))
    vb = band_keys(to_sub(v))
    i = jnp.arange(band)[:, None]
    c = jnp.arange(2 * band)[None, :]
    dist_sub = band + i - c
    in_band = (dist_sub >= 0) & (dist_sub <= band)
    n = jnp.arange(nb)[:, None, None]
    mask = in_band[None] & ((n > 0) | (c[None] >= band))
    buckets = t5_bucket(jnp.clip(dist_sub, 0, band) * dil)
    bias = bias_tab.astype(jnp.float32)[buckets].transpose(2, 0, 1)
    s = jnp.einsum('bdhnqe,bdhnke->bdhnqk', qb, kb, preferred_element_type=jnp.float32) / math.sqrt(E)
    s = jnp.where(mask[None, None, None], s + bias[None, None, :, None], -1e30)
    m = jnp.max(s, axis=-1, keepdims=True)
    p = jnp.exp(s - m)
    den = jnp.sum(p, axis=-1, keepdims=True)
    o = jnp.einsum('bdhnqk,bdhnke->bdhnqe', p, vb.astype(jnp.float32)) / den
    lse = (m + jnp.log(den))[..., 0]
    o = o.reshape(B_, dil, H, Lp, E)[:, :, :, :L].transpose(0, 3, 1, 2, 4).reshape(B_, S_, H, E)
    lse = lse.reshape(B_, dil, H, Lp)[:, :, :, :L].transpose(0, 3, 1, 2).reshape(B_, S_, H)
    return o, lse

def dilated_attention(qkv, rel_bias):
    B_, S_ = qkv.shape[:2]
    outs, lses = [], []
    for g, (window, dil) in enumerate(DIL_PAIRS):
        hs = slice(g * DIL_HEADS_PER_GROUP, (g + 1) * DIL_HEADS_PER_GROUP)
        o, lse = dilated_group(qkv[:, :, 0, hs], qkv[:, :, 1, hs], qkv[:, :, 2, hs],
                               rel_bias[:, hs], window, dil)
        outs.append(o)
        lses.append(lse)
    o = jnp.stack(outs, axis=0)
    alpha = jax.nn.softmax(jnp.stack(lses, axis=0), axis=0)
    y = jnp.sum(alpha[..., None] * o, axis=0)
    return y.reshape(B_, S_, DIL_OUT_WIDTH).astype(qkv.dtype)

def stick_breaking_attention(qkv):
    B_, S_, _, H, E = qkv.shape
    nb = S_ // SB_BLOCK
    qh = qkv[:, :, 0].transpose(0, 2, 1, 3)
    kh = qkv[:, :, 1].transpose(0, 2, 1, 3)
    vh = qkv[:, :, 2].transpose(0, 2, 1, 3).astype(jnp.float32)
    qblk = qh.reshape(B_, H, nb, SB_BLOCK, E).transpose(2, 0, 1, 3, 4)
    key_pos = jnp.arange(S_)

    def one_block(args):
        qb, bi = args
        z = jnp.einsum('bhqe,bhke->bhqk', qb, kh, preferred_element_type=jnp.float32) / math.sqrt(E)
        q_pos = bi * SB_BLOCK + jnp.arange(SB_BLOCK)
        mask = key_pos[None, :] < q_pos[:, None]
        log_not = jnp.where(mask, jax.nn.log_sigmoid(-z), 0.0)
        excl = lax.cumsum(log_not, axis=3, reverse=True) - log_not
        w = jnp.where(mask, jnp.exp(jax.nn.log_sigmoid(z) + excl), 0.0)
        return jnp.einsum('bhqk,bhke->bhqe', w, vh)

    o = lax.map(one_block, (qblk, jnp.arange(nb)))
    return o.transpose(1, 0, 3, 2, 4).reshape(B_, S_, SB_WIDTH).astype(qkv.dtype)

def s5_mixer(u, a_re, a_im, log_dt, b_re, b_im, c_re, c_im, d_skip, w_glu):
    B_, S_, _ = u.shape
    f32 = jnp.float32
    uf = u.astype(f32).reshape(B_, S_, S5_GROUPS, S5_CH)
    lam = lax.complex(a_re.astype(f32), a_im.astype(f32))
    dt = jnp.exp(log_dt.astype(f32))[:, None]
    lam_bar = jnp.exp(lam * dt)
    b_t = lax.complex(b_re.astype(f32), b_im.astype(f32))
    b_bar = ((lam_bar - 1.0) / lam)[:, :, None] * b_t
    bu = jnp.einsum('gpc,bsgc->bsgp', b_bar, uf.astype(jnp.complex64))
    a = jnp.broadcast_to(lam_bar, (1, S_) + lam_bar.shape)

    def combine(left, right):
        a_l, b_l = left
        a_r, b_r = right
        return a_r * a_l, a_r * b_l + b_r

    _, h = lax.associative_scan(combine, (a, bu), axis=1)
    c_t = lax.complex(c_re.astype(f32), c_im.astype(f32))
    y = jnp.real(jnp.einsum('gcp,bsgp->bsgc', c_t, h)) + d_skip.astype(f32).reshape(S5_GROUPS, S5_CH) * uf
    y = jax.nn.gelu(y.reshape(B_, S_, S5_WIDTH))
    gl = y @ w_glu.astype(f32)
    y = gl[..., :S5_WIDTH] * jax.nn.sigmoid(gl[..., S5_WIDTH:])
    return y.astype(u.dtype)

def second_inputs(seed: int = 0) -> dict:
    key = jax.random.key(seed)
    ks = jax.random.split(key, 22)
    nrm = jax.random.normal
    f32 = jnp.float32
    x = nrm(ks[0], (BATCH, SEQ, D_MODEL), f32)
    attn_norm_g = 1.0 + 0.02 * nrm(ks[1], (DEPTH, D_MODEL), f32)
    w_in = nrm(ks[2], (DEPTH, D_MODEL, IN_WIDTH), f32) * D_MODEL ** -0.5
    pool_w = nrm(ks[3], (DEPTH, len(POOL_WINDOWS), POOL_GROUP, POOL_GROUP), f32) * POOL_GROUP ** -0.5
    pool_scale = 1.0 + 0.02 * nrm(ks[4], (DEPTH, POOL_WIDTH), f32)
    rel_bias = 0.5 * nrm(ks[5], (REL_BUCKETS, DIL_HEADS), f32)
    s5_a_re = -0.5 + 0.01 * nrm(ks[6], (DEPTH, S5_GROUPS, S5_STATE), f32)
    s5_a_im = jnp.pi * jnp.arange(S5_STATE, dtype=f32)[None, None, :] + 0.01 * nrm(ks[7], (DEPTH, S5_GROUPS, S5_STATE), f32)
    s5_log_dt = jax.random.uniform(ks[8], (DEPTH, S5_GROUPS), f32, minval=math.log(1e-3), maxval=math.log(1e-1))
    s5_b_re = nrm(ks[9], (DEPTH, S5_GROUPS, S5_STATE, S5_CH), f32) * (2 * S5_CH) ** -0.5
    s5_b_im = nrm(ks[10], (DEPTH, S5_GROUPS, S5_STATE, S5_CH), f32) * (2 * S5_CH) ** -0.5
    s5_c_re = nrm(ks[11], (DEPTH, S5_GROUPS, S5_CH, S5_STATE), f32) * S5_STATE ** -0.5
    s5_c_im = nrm(ks[12], (DEPTH, S5_GROUPS, S5_CH, S5_STATE), f32) * S5_STATE ** -0.5
    s5_d = nrm(ks[13], (DEPTH, S5_WIDTH), f32)
    s5_w_glu = nrm(ks[14], (DEPTH, S5_WIDTH, 2 * S5_WIDTH), f32) * S5_WIDTH ** -0.5
    row_scale = jnp.concatenate([jnp.full((w,), w ** -0.5, f32) for w in BRANCH_WIDTHS])
    w_branch = nrm(ks[15], (DEPTH, BRANCH_WIDTH, D_MODEL), f32) * row_scale[None, :, None]
    w_gate = nrm(ks[16], (DEPTH, N_BRANCHES, D_MODEL, D_MODEL), f32) * D_MODEL ** -0.5
    w_out = nrm(ks[17], (DEPTH, D_MODEL, D_MODEL), f32) * D_MODEL ** -0.5
    ffn_norm_g = 1.0 + 0.02 * nrm(ks[18], (DEPTH, D_MODEL), f32)
    w_up = nrm(ks[19], (DEPTH, D_MODEL, 2 * FFN_HIDDEN), f32) * D_MODEL ** -0.5
    w_down = nrm(ks[20], (DEPTH, FFN_HIDDEN, D_MODEL), f32) * FFN_HIDDEN ** -0.5
    final_norm_g = 1.0 + 0.02 * nrm(ks[21], (D_MODEL,), f32)
    return {'x': x, 'attn_norm_g': attn_norm_g, 'w_in': w_in, 'pool_w': pool_w,
            'pool_scale': pool_scale, 'rel_bias': rel_bias, 's5_a_re': s5_a_re,
            's5_a_im': s5_a_im, 's5_log_dt': s5_log_dt, 's5_b_re': s5_b_re, 's5_b_im': s5_b_im,
            's5_c_re': s5_c_re, 's5_c_im': s5_c_im, 's5_d': s5_d, 's5_w_glu': s5_w_glu,
            'w_branch': w_branch, 'w_gate': w_gate, 'w_out': w_out, 'ffn_norm_g': ffn_norm_g,
            'w_up': w_up, 'w_down': w_down, 'final_norm_g': final_norm_g}

def second_block(x, attn_norm_g, w_in, pool_w, pool_scale, rel_bias, s5_a_re, s5_a_im, s5_log_dt,
              s5_b_re, s5_b_im, s5_c_re, s5_c_im, s5_d, s5_w_glu, w_branch, w_gate, w_out,
              ffn_norm_g, w_up, w_down, final_norm_g):
    B_, S_, _ = x.shape
    o1 = POOL_WIDTH
    o2 = o1 + 3 * DIL_QKV_WIDTH
    o3 = o2 + 3 * SB_WIDTH
    for l in range(DEPTH):
        xn = rmsnorm_2(x, attn_norm_g[l])
        proj = xn @ w_in[l]
        u_pool = proj[..., :o1]
        qkv_dil = proj[..., o1:o2].reshape(B_, S_, 3, DIL_HEADS, DIL_HEAD_DIM)
        qkv_sb = proj[..., o2:o3].reshape(B_, S_, 3, SB_HEADS, SB_HEAD_DIM)
        u_s5 = proj[..., o3:]
        y_pool = pool_mixer(u_pool, pool_w[l], pool_scale[l])
        y_dil = dilated_attention(qkv_dil, rel_bias)
        y_sb = stick_breaking_attention(qkv_sb)
        y_s5 = s5_mixer(u_s5, s5_a_re[l], s5_a_im[l], s5_log_dt[l], s5_b_re[l], s5_b_im[l],
                        s5_c_re[l], s5_c_im[l], s5_d[l], s5_w_glu[l])
        merged = jnp.zeros_like(x)
        row = 0
        for bi, yb in enumerate((y_pool, y_dil, y_sb, y_s5)):
            width = BRANCH_WIDTHS[bi]
            gate = jax.nn.sigmoid(xn @ w_gate[l, bi])
            merged = merged + gate * (yb @ w_branch[l, row:row + width])
            row += width
        x = x + merged @ w_out[l]
        hn = rmsnorm_2(x, ffn_norm_g[l])
        gu = hn @ w_up[l]
        h = jax.nn.silu(gu[..., :FFN_HIDDEN]) * gu[..., FFN_HIDDEN:]
        x = x + h @ w_down[l]
    return rmsnorm_2(x, final_norm_g)


def setup_inputs(seed=0):
    out = dict(first_inputs(seed))
    for name, value in second_inputs(seed + 1).items():
        if name != "x":
            out[name + "_2"] = value
    return out


def reference(
    x, c, ctx, c_ctx, w_ada, b_ada, norm_mix, norm_ffn, w_in, gate_b, qk_conv_w, qk_conv_b,
    mlstm_norm, attn_sink, w_out, w_up, ffn_conv_w, ffn_conv_b, w_down, final_norm,
    attn_norm_g_2, w_in_2, pool_w_2, pool_scale_2, rel_bias_2, s5_a_re_2, s5_a_im_2,
    s5_log_dt_2, s5_b_re_2, s5_b_im_2, s5_c_re_2, s5_c_im_2, s5_d_2, s5_w_glu_2, w_branch_2,
    w_gate_2, w_out_2, ffn_norm_g_2, w_up_2, w_down_2, final_norm_g_2,
):
    x = first_block(
        x, c, ctx, c_ctx, w_ada, b_ada, norm_mix, norm_ffn, w_in, gate_b, qk_conv_w, qk_conv_b,
        mlstm_norm, attn_sink, w_out, w_up, ffn_conv_w, ffn_conv_b, w_down, final_norm,
    )
    return second_block(
        x, attn_norm_g_2, w_in_2, pool_w_2, pool_scale_2, rel_bias_2, s5_a_re_2, s5_a_im_2,
        s5_log_dt_2, s5_b_re_2, s5_b_im_2, s5_c_re_2, s5_c_im_2, s5_d_2, s5_w_glu_2, w_branch_2,
        w_gate_2, w_out_2, ffn_norm_g_2, w_up_2, w_down_2, final_norm_g_2,
    )


_drawn_inputs = setup_inputs


def setup_inputs(seed=0):
    import zlib

    import numpy as np

    out = dict(_drawn_inputs(seed))
    spreads = {}
    factors = {'ctx': 2.746,
     'norm_mix': 8.0,
     'norm_ffn': 7.132,
     'qk_conv_b': 64.0,
     'mlstm_norm': 8.0,
     'attn_sink': 8.0,
     'ffn_conv_b': 8.0,
     'attn_norm_g_2': 4.157,
     'pool_scale_2': 6.547,
     's5_a_re_2': 64.0,
     's5_a_im_2': 28.352,
     's5_log_dt_2': 30.144,
     's5_b_re_2': 40.448,
     's5_b_im_2': 39.688,
     's5_c_re_2': 40.776,
     's5_c_im_2': 39.776,
     'ffn_norm_g_2': 13.094,
     'final_norm_g_2': 8.019,
     'rel_bias_2': 3.092}
    for name, (base, spread) in spreads.items():
        noise = np.random.default_rng([zlib.crc32(name.encode()), seed]).standard_normal(out[name].shape)
        drawn = base * np.exp(spread * noise) if base else spread * noise
        out[name] = jnp.asarray(drawn.astype(out[name].dtype))
    for name, factor in factors.items():
        out[name] = (out[name] * factor).astype(out[name].dtype)
    return out
```

```python
from contextlib import ExitStack

import numpy as np

import concourse.bass as bass
from concourse import mybir

F32 = mybir.dt.float32
ALU = mybir.AluOpType
ACT = mybir.ActivationFunctionType
AX = mybir.AxisListType

P = 128
D = 1024
DK = D // P
T = 1024
TC = 256
TA = T + TC
NB = T // P
NBA = TA // P
BANK = 512
EPS = 1e-6
NEG = -1e30
FF = 2816
FK = FF // P
MH, AH, KVH, GRP = 4, 8, 2, 4
OFF_QK, OFF_V, OFF_O, OFF_G, OFF_QA, OFF_KA, OFF_VA = 0, 1024, 1536, 2048, 2064, 2576, 2704
NG = 16
HALVES = [(0, BANK), (BANK, BANK)]
XCHUNKS = HALVES + [(T, TC)]
STOP = 99


class Count:

    def __init__(self, sem):
        self.sem, self.base = sem, 0


class Chain:

    def __init__(self, sem):
        self.sem, self.eng, self.base, self.n = sem, None, 0, 0

    def on(self, eng):
        self.eng = eng
        return self

    def __call__(self, ins):
        self.n += 1
        ins.then_inc(self.sem, 1)
        self.eng.wait_ge(self.sem, self.base + self.n)

    def loop(self, count, per, body):
        start = self.base + self.n
        with self.eng.Fori(0, count) as i:
            self.base, self.n = start + i * per, 0
            body(i)
            assert self.n == per, (self.n, per)
        self.base, self.n = start + count * per, 0


class Core:

    def __init__(self, nc, ctx):
        self.nc, self.ctx, self.names, self.lasting = nc, ctx, {}, True
        self.dve, self.act, self.pool, self.pe = (Chain(self.sem(n)) for n in
                                        ("dve_steps", "act_steps", "pool_steps", "pe_steps"))
        self.ps = ctx.enter_context(nc.psum_tensor("ps", [P, 8, BANK], F32))
        self.w_loaded = [Count(self.sem(f"w_loaded{s}")) for s in range(2)]
        self.w_used = [Count(self.sem(f"w_used{s}")) for s in range(2)]
        self.acc_ready = [Count(self.sem(f"acc_ready{s}")) for s in range(2)]
        self.act_emptied = [Count(self.sem(f"act_emptied{s}")) for s in range(2)]
        self.dve_emptied = [Count(self.sem(f"dve_emptied{s}")) for s in range(2)]

        self.lasting, self.stage_sems = False, []

    def sem(self, name):
        sem = self.nc.alloc_semaphore(name=name)
        if not self.lasting:
            self.stage_sems.append(sem)
        return sem

    def end_stage(self):
        self.nc.clear_and_free_semaphores(self.stage_sems)
        self.nc.all_engine_barrier()
        self.stage_sems = []

    def sb(self, name, shape, ctx=None):
        self.names[name] = self.names.get(name, 0) + 1
        if self.names[name] > 1:
            name = f"{name}_{self.names[name]}"
        return (ctx or self.ctx).enter_context(self.nc.sbuf_tensor(name, shape, F32))


def project(c, tiles, parts, k_tiles, w_cols, rhs, chunks, bank_of, act_part, dve_part, act_steps,
            dve_steps, wbuf, extra_load=None):
    nc = c.nc
    half = tiles // 2
    n_loads = sum(1 for _ in range(parts))

    with nc.Block() as block:

        def both_slots(eng, body):
            with eng.Fori(0, half) as i:
                for s in range(2):
                    body(i * 2 + s, s, i)

        @block.sync
        def _(sp):
            def load(tile, s, i):
                sp.wait_ge(c.w_used[s].sem, c.w_used[s].base + i)
                for part in range(parts):
                    sp.dma_start(wbuf[:, s, part, 0:k_tiles, :], w_cols(part, tile)).then_inc(c.w_loaded[s].sem, 16)
            both_slots(sp, load)

        @block.tensor
        def _(pe):
            def products(tile, s, i):
                pe.wait_ge(c.w_loaded[s].sem, c.w_loaded[s].base + (i + 1) * (16 * n_loads))
                pe.wait_ge(c.act_emptied[s].sem, c.act_emptied[s].base + i)
                pe.wait_ge(c.dve_emptied[s].sem, c.dve_emptied[s].base + i)
                for part in range(parts):
                    for n, (at, size) in enumerate(chunks):
                        for k in range(k_tiles):
                            last = nc.tensor.matmul(bank_of(s, part, n)[:, 0:size], wbuf[:, s, part, k, :],
                                                    rhs(part)[:, k, at:at + size],
                                                    start=(k == 0), stop=(k == k_tiles - 1))
                            if n == len(chunks) - 1 and k == k_tiles - 1:
                                if part == parts - 1:
                                    last.then_inc(c.w_used[s].sem, 1)
                pe.wait_ge(c.w_used[s].sem, c.w_used[s].base + i + 1)
                pe.nop().then_inc(c.acc_ready[s].sem, 1)
            both_slots(pe, products)

        @block.scalar
        def _(eng):
            def empty(i):
                for s in range(2):
                    eng.wait_ge(c.acc_ready[s].sem, c.acc_ready[s].base + i + 1)
                    act_part(eng, i * 2 + s, s, i)
                    eng.nop().then_inc(c.act_emptied[s].sem, 1)
            c.act.on(eng).loop(half, 2 * act_steps, empty)

        @block.vector
        def _(eng):
            def empty(i):
                for s in range(2):
                    eng.wait_ge(c.acc_ready[s].sem, c.acc_ready[s].base + i + 1)
                    dve_part(eng, i * 2 + s, s, i)
                    eng.nop().then_inc(c.dve_emptied[s].sem, 1)
            c.dve.on(eng).loop(half, 2 * dve_steps, empty)

    for s in range(2):
        c.w_loaded[s].base += half * 16 * n_loads
        c.w_used[s].base += half
        c.acc_ready[s].base += half
        c.act_emptied[s].base += half
        c.dve_emptied[s].base += half


def modulation(c, io, ada, ident):
    nc = c.nc
    with ExitStack() as tmp:
        cc = c.sb("cc", [P, DK, 2], tmp)
        sc = c.sb("sc", [P, DK, 2], tmp)
        b = c.sb("b_ada_t", [P, 48], tmp)
        wa = c.sb("wa", [P, 3, DK, BANK], tmp)
        c_loaded, sc_ready, ada_sum = c.sem("c_loaded"), c.sem("sc_ready"), c.sem("ada_sum")
        wa_loaded = [c.sem(f"wa_loaded{s}") for s in range(3)]
        wa_used = [c.sem(f"wa_used{s}") for s in range(3)]
        acc = c.ps[:, 0, 0:96].rearrange("p (m j) -> p m j", j=2)
        w = io["w_ada"][0].rearrange("(k p) n -> p k n", p=P)
        with nc.Block() as block:
            @block.sync
            def _(sp):
                with nc.allow_non_contiguous_dma("small"):
                    sp.dma_start(cc[:, :, 0], io["c"].rearrange("o (k p) -> p (o k)", p=P)).then_inc(c_loaded, 16)
                    sp.dma_start(cc[:, :, 1], io["c_ctx"].rearrange("(k p) -> p k", p=P)).then_inc(c_loaded, 16)
                    sp.dma_start(b[:, :], io["b_ada"].rearrange("o (m p) -> p (o m)", p=P)).then_inc(c_loaded, 16)
                with sp.Fori(0, 4) as i:
                    for s in range(3):
                        sp.wait_ge(wa_used[s], i + 1)
                        sp.dma_start(wa[:, s], w[:, :, bass.ds((i * 3 + s) * BANK, BANK)]).then_inc(wa_loaded[s], 16)

            @block.scalar
            def _(act):
                act.wait_ge(c_loaded, 48)
                nc.scalar.activation(sc[:, :, :], cc[:, :, :], ACT.Silu).then_inc(sc_ready, 1)

            @block.tensor
            def _(pe):
                for s in range(3):
                    pe.nop().then_inc(wa_used[s], 1)
                pe.wait_ge(sc_ready, 1)
                for i in range(4):
                    for s in range(3):
                        pe.wait_ge(wa_loaded[s], 16 * (i + 1))
                        for m in range(4):
                            for k in range(DK):
                                last = nc.tensor.matmul(acc[:, 4 * (3 * i + s) + m, :],
                                                        wa[:, s, k, m * P:(m + 1) * P], sc[:, k, :],
                                                        start=(k == 0), stop=(k == DK - 1))
                        last.then_inc(wa_used[s], 1)

            @block.vector
            def _(dve):
                for s in range(3):
                    dve.wait_ge(wa_used[s], 5)
                nc.vector.tensor_tensor(ada[:, :, :], acc, b[:, :].unsqueeze(2).to_broadcast([P, 48, 2]),
                                        ALU.add).then_inc(ada_sum, 1)


def turn_in(c, io, xT, cT, ident):
    nc = c.nc
    with ExitStack() as tmp:
        rows = c.sb("rows", [P, 2, D], tmp)
        loaded = [c.sem(f"rows_loaded{s}") for s in range(2)]
        turned, dve_copied, act_copied = c.sem("turned"), c.sem("turned_dve_copied"), c.sem("turned_act_copied")
        src = [io["x"][0, b * P:(b + 1) * P, :] for b in range(NB)] + \
              [io["ctx"][0, b * P:(b + 1) * P, :] for b in range(TC // P)]
        dst = [xT[:, :, b * P:(b + 1) * P] for b in range(NB)] + \
              [cT[:, :, b * P:(b + 1) * P] for b in range(TC // P)]
        with nc.Block() as block:
            @block.sync
            def _(sp):
                for b in range(NBA):
                    if b >= 2:
                        sp.wait_ge(turned, b - 1)
                    sp.dma_start(rows[:, b % 2, :], src[b]).then_inc(loaded[b % 2], 16)

            @block.tensor
            def _(pe):
                for b in range(NBA):
                    pe.wait_ge(loaded[b % 2], 16 * (b // 2 + 1))
                    if b >= 2:
                        pe.wait_ge(dve_copied, b - 1)
                        pe.wait_ge(act_copied, b - 1)
                    for k in range(DK):
                        last = nc.tensor.transpose(c.ps[:, 2 * (b % 2) + k // 4, (k % 4) * P:(k % 4 + 1) * P],
                                                   rows[:, b % 2, k * P:(k + 1) * P], ident[:, :])
                    last.then_inc(turned, 1)

            @block.vector
            def _(dve):
                for b in range(NBA):
                    dve.wait_ge(turned, b + 1)
                    nc.vector.tensor_copy(dst[b][:, 0:4, :], c.ps[:, 2 * (b % 2), :].rearrange("p (k t) -> p k t", k=4)).then_inc(dve_copied, 1)

            @block.scalar
            def _(act):
                for b in range(NBA):
                    act.wait_ge(turned, b + 1)
                    nc.scalar.copy(dst[b][:, 4:8, :], c.ps[:, 2 * (b % 2) + 1, :].rearrange("p (k t) -> p k t", k=4)).then_inc(act_copied, 1)


def norm(c, name, parts, ones, out, shift=True):
    nc = c.nc
    with ExitStack() as tmp:
        sq = c.sb("sq", [P, 2, BANK], tmp)
        rs = c.sb("rs", [P, 2, BANK], tmp)
        squared, sq_used = c.sem(name + "_squared"), c.sem(name + "_sq_used")
        mean_ready, root_ready, scaled = c.sem(name + "_mean"), c.sem(name + "_root"), c.sem(name + "_scaled")
        done = c.sem(name + "_done")
        with nc.Block() as block:
            @block.scalar
            def _(act):
                for n, (src, at, size, g, b, to) in enumerate(parts):
                    for k in range(DK):
                        j = n * DK + k
                        if j >= 2:
                            act.wait_ge(sq_used, j - 1)
                        nc.scalar.activation(sq[:, j % 2, 0:size], src[:, k, at:at + size], ACT.Square).then_inc(squared, 1)
                for n, (src, at, size, g, b, to) in enumerate(parts):
                    act.wait_ge(mean_ready, n + 1)
                    nc.scalar.activation(rs[:, n % 2, 0:size], rs[:, n % 2, 0:size], ACT.Sqrt).then_inc(root_ready, 1)
                    if shift:
                        for k in range(DK):
                            act.wait_ge(scaled, n * DK + k + 1)
                            nc.scalar.activation(out[:, k, to:to + size], out[:, k, to:to + size], ACT.Identity,
                                                 bias=b(k), scale=1.0).then_inc(done, 1)

            @block.tensor
            def _(pe):
                for n, (src, at, size, g, b, to) in enumerate(parts):
                    for k in range(DK):
                        pe.wait_ge(squared, n * DK + k + 1)
                        nc.tensor.matmul(c.ps[:, n, 0:size], ones[:, :], sq[:, (n * DK + k) % 2, 0:size],
                                         start=(k == 0), stop=(k == DK - 1)).then_inc(sq_used, 1)

            @block.vector
            def _(dve):
                step = c.dve.on(dve)
                for n, (src, at, size, g, b, to) in enumerate(parts):
                    dve.wait_ge(sq_used, DK * (n + 1))
                    if n >= 2:
                        dve.wait_ge(scaled, DK * (n - 1))
                    nc.vector.tensor_scalar(rs[:, n % 2, 0:size], c.ps[:, n, 0:size], 1.0 / D, EPS,
                                            ALU.mult, ALU.add).then_inc(mean_ready, 1)
                    dve.wait_ge(root_ready, n + 1)
                    step(nc.vector.reciprocal(rs[:, n % 2, 0:size], rs[:, n % 2, 0:size]))
                    for k in range(DK):
                        nc.vector.scalar_tensor_tensor(out[:, k, to:to + size], src[:, k, at:at + size], g(k),
                                                       rs[:, n % 2, 0:size], ALU.mult, ALU.mult).then_inc(scaled, 1)


def load_all(c, name, pairs):
    nc = c.nc
    loaded = c.sem(name)
    with nc.Block() as block:
        @block.sync
        def _(sp):
            with nc.allow_non_contiguous_dma("small vectors, one element to a partition"):
                for dst, src in pairs:
                    sp.dma_start(dst, src).then_inc(loaded, 16)
            sp.wait_ge(loaded, 16 * len(pairs))


def col(ap):
    return ap.rearrange("(k p) -> p k", p=P)


def build(nc, io):
    with ExitStack() as ctx:
        c = Core(nc, ctx)
        c.io = io
        c.eps = c.sb("eps", [P, 1])
        xT = c.sb("xT", [P, DK, T])
        ident, ones = c.sb("ident", [P, P]), c.sb("ones", [P, P])
        ada = c.sb("ada", [P, 48, 2])
        gains = c.sb("gains", [P, 5, DK])
        gainx = c.sb("gainx", [P, 3, DK])
        final2 = c.sb("final2", [P, DK])
        load_all(c, "consts_loaded", [
            (ident[:, :], io["k_ident"]), (ones[:, :], io["k_ones"]),
            (gains[:, 0], col(io["norm_mix"][0])), (gains[:, 1], col(io["norm_ffn"][0])),
            (gains[:, 2], col(io["final_norm"])), (gains[:, 3], col(io["attn_norm_g_2"][0])),
            (gains[:, 4], col(io["ffn_norm_g_2"][0])), (final2[:, :], col(io["final_norm_g_2"]))])
        with nc.Block() as block:
            @block.vector
            def _(dve):
                c.dve.on(dve)(nc.vector.memset(c.eps[:, :], EPS))
                for emptied in c.dve_emptied:
                    dve.nop().then_inc(emptied.sem, 1)

            @block.scalar
            def _(act):
                for emptied in c.act_emptied:
                    act.nop().then_inc(emptied.sem, 1)

            @block.tensor
            def _(pe):
                for used in c.w_used:
                    pe.nop().then_inc(used.sem, 1)
        for count in c.w_used + c.act_emptied + c.dve_emptied:
            count.base += 1
        modulation(c, io, ada, ident)
        first_block(c, io, xT, ident, ones, ada, gains, gainx)
        if STOP > 20:
            second_block(c, io, xT, ident, ones, gains, final2)


def first_block(c, io, xT, ident, ones, ada, gains, gainx):
    nc = c.nc
    mix_ctx = ExitStack()
    with mix_ctx:
        mixT = c.sb("mixT", [P, DK, T], mix_ctx)
        with ExitStack() as s1:
            mixer(c, io, xT, ident, ones, ada, gains, gainx, mixT, s1)
        if STOP <= 8:
            return
        residual(c, io["w_out"][0], DK, mixT, xT, lambda k: ada[:, bass.ds(16 + k, 1), 0], "mix")
    if STOP <= 9:
        return
    c.end_stage()
    feed_forward_1(c, io, xT, ones, ada, gainx)
    norm(c, "final1", [(xT, at, n, lambda k: gains[:, 2, k:k + 1], None, at) for at, n in HALVES],
         ones, xT, shift=False)


def residual(c, w, k_tiles, src, xT, gate, name):
    nc = c.nc
    wv = w.rearrange("(k p) n -> p k n", p=P)
    with ExitStack() as tmp:
        wbuf = c.sb("wbuf", [P, 2, 1, k_tiles, P], tmp)

        def add(eng, tile, s, i):
            for n, (at, size) in enumerate(HALVES):
                dst = xT[:, bass.ds(tile, 1), at:at + size].rearrange("p o t -> p (o t)")
                acc = c.ps[:, 2 * s + n, :]
                if gate is None:
                    c.dve(nc.vector.tensor_tensor(dst, acc, dst, ALU.add))
                else:
                    c.dve(nc.vector.scalar_tensor_tensor(dst, acc, gate(tile), dst, ALU.mult, ALU.add))
        project(c, DK, 1, k_tiles, lambda part, t: wv[:, :, bass.ds(t * P, P)], lambda part: src, HALVES,
                lambda s, part, n: c.ps[:, 2 * s + n, :], lambda *a: None, add, 0, 2, wbuf)


def feed_forward_1(c, io, xT, ones, ada, gainx):
    nc = c.nc
    with ExitStack() as s2:
        hid = c.sb("hid", [P, FK, T], s2)
        with ExitStack() as s3:
            hT = c.sb("hT_ffn", [P, DK, T], s3)
            wbuf = c.sb("wbuf", [P, 2, 2, DK, P], s3)
            a_pad = c.sb("a_pad", [P, 2, T + 2], s3)
            tap = c.sb("tap", [P, 2, T], s3)
            cw = c.sb("cw", [P, 4, FK], s3)
            load_all(c, "ffn_conv_loaded", [(cw[:, j], col(io["ffn_conv_w"][0, j])) for j in range(3)]
                     + [(cw[:, 3], col(io["ffn_conv_b"][0]))])
            norm(c, "norm_ffn1", [(xT, at, n, lambda k: gainx[:, 2, k:k + 1], lambda k: ada[:, 24 + k, 0:1], at)
                                  for at, n in HALVES], ones, hT)
            with nc.Block() as block:
                @block.vector
                def _(dve):
                    c.dve.on(dve)(nc.vector.memset(a_pad[:, :, :], 0.0))
            a_copied, conv_ready, gelu_ready = c.sem("a_copied"), c.sem("conv_ready"), c.sem("gelu_ready")
            wv = io["w_up"][0].rearrange("(k p) n -> p k n", p=P)

            def act_part(eng, tile, s, i):
                n = i * 2 + s + 1
                c.act(nc.scalar.copy(a_pad[:, s, 1:T + 1], c.ps[:, 4 * s:4 * s + 2, :].rearrange("p b t -> p (b t)")))
                eng.nop().then_inc(a_copied, 1)
                eng.wait_ge(conv_ready, n)
                c.act(nc.scalar.activation(tap[:, s, :], tap[:, s, :], ACT.Gelu_apprx_tanh))
                eng.nop().then_inc(gelu_ready, 1)

            def dve_part(eng, tile, s, i):
                n = i * 2 + s + 1
                w = [cw[:, j, bass.ds(tile, 1)] for j in range(4)]
                eng.wait_ge(a_copied, n)
                c.dve(nc.vector.tensor_scalar(tap[:, s, :], a_pad[:, s, 1:T + 1], w[1], w[3], ALU.mult, ALU.add))
                c.dve(nc.vector.scalar_tensor_tensor(tap[:, s, :], a_pad[:, s, 0:T], w[0], tap[:, s, :], ALU.mult, ALU.add))
                c.dve(nc.vector.scalar_tensor_tensor(tap[:, s, :], a_pad[:, s, 2:T + 2], w[2], tap[:, s, :], ALU.mult, ALU.add))
                eng.nop().then_inc(conv_ready, 1)
                eng.wait_ge(gelu_ready, n)
                c.dve(nc.vector.tensor_tensor(hid[:, bass.ds(tile, 1), :].rearrange("p o t -> p (o t)"),
                                              c.ps[:, 4 * s + 2:4 * s + 4, :].rearrange("p b t -> p (b t)"),
                                              tap[:, s, :], ALU.mult))
            project(c, FK, 2, DK, lambda part, t: wv[:, :, bass.ds(t * P + part * FF, P)], lambda part: hT, HALVES,
                    lambda s, part, n: c.ps[:, 4 * s + 2 * part + n, :], act_part, dve_part, 2, 4, wbuf)
        residual(c, io["w_down"][0], FK, hid, xT, lambda k: ada[:, bass.ds(40 + k, 1), 0], "down1")


def token_major(c, name, w, cols, src, lhs_cols, dst):
    nc = c.nc
    blocks = len(lhs_cols)
    with ExitStack() as tmp:
        wbuf = c.sb("w_tok", [P, DK, cols], tmp)
        loaded, summed, emptied = c.sem(name + "_w"), c.sem(name + "_sum"), c.sem(name + "_out")
        with nc.Block() as block:
            @block.sync
            def _(sp):
                for i, (at, view) in enumerate(w):
                    sp.dma_start(wbuf[:, :, at:at + view.shape[2]], view).then_inc(loaded, 16)

            @block.tensor
            def _(pe):
                pe.wait_ge(loaded, 16 * len(w))
                for b in range(blocks):
                    if b >= 8:
                        pe.wait_ge(emptied, b - 7)
                    for k in range(DK):
                        last = nc.tensor.matmul(c.ps[:, b % 8, 0:cols], lhs_cols[b](src, k), wbuf[:, k, :],
                                                start=(k == 0), stop=(k == DK - 1))
                    last.then_inc(summed, 1)

            @block.vector
            def _(dve):
                for b in range(blocks):
                    dve.wait_ge(summed, b + 1)
                    nc.vector.tensor_copy(dst(b), c.ps[:, b % 8, 0:cols]).then_inc(emptied, 1)


def mixer(c, io, xT, ident, ones, ada, gains, gainx, mixT, s1):
    nc = c.nc
    hT = c.sb("hT", [P, DK, TA], s1)
    with ExitStack() as s2:
        cT = c.sb("cT", [P, DK, TC], s2)
        turn_in(c, io, xT, cT, ident)
        with nc.Block() as block:
            @block.vector
            def _(dve):
                for j, (at, who, g) in enumerate([(8, 0, 0), (8, 1, 0), (32, 0, 1)]):
                    c.dve.on(dve)(nc.vector.scalar_tensor_tensor(gainx[:, j, :], ada[:, at:at + DK, who], 1.0,
                                                                 gains[:, g, :], ALU.add, ALU.mult))
        norm(c, "norm_mix", [(xT, at, n, lambda k: gainx[:, 0, k:k + 1], lambda k: ada[:, k, 0:1], at) for at, n in HALVES]
             + [(cT, 0, TC, lambda k: gainx[:, 1, k:k + 1], lambda k: ada[:, k, 1:2], T)], ones, hT)
    w_in = io["w_in"][0].rearrange("(k p) n -> p k n", p=P)
    with ExitStack() as s2:
        window(c, io, w_in, hT, ident, mixT, s2)
    if STOP <= 3:
        return
    c.end_stage()
    with ExitStack() as s2:
        mlstm(c, io, w_in, hT, ident, ones, mixT, s2)


def plain_blocks(n):
    return [lambda src, k, b=b: src[:, k, b * P:(b + 1) * P] for b in range(n)]


def mlstm(c, io, w_in, hT, ident, ones, mixT, s2):
    nc = c.nc
    qkT = c.sb("qkT", [P, 2 * MH, TA], s2)
    between = c.sb("between", [MH, 2, NBA, NBA], s2)
    keyw = c.sb("keyw", [P, 2, 2, NBA, MH], s2)
    sel = c.sb("sel", [MH, MH, P], s2)
    mgain = c.sb("mgain", [P, MH], s2)

    with ExitStack() as tmp:
        PADW = TA + 3
        wbuf = c.sb("wbuf", [P, 2, 1, DK, P], tmp)
        pad = c.sb("pad", [P, 2, PADW], tmp)
        tap = c.sb("tap", [P, 2, PADW], tmp)
        cw = c.sb("cw", [P, 4, DK], tmp)
        load_all(c, "qk_conv_loaded", [(cw[:, j], col(io["qk_conv_w"][0, j])) for j in range(3)]
                 + [(cw[:, 3], col(io["qk_conv_b"][0])), (sel[:, :, :], io["k_sel"]),
                    (mgain[:, :], col(io["mlstm_norm"][0]))])
        with nc.Block() as block:
            @block.vector
            def _(dve):
                c.dve.on(dve)(nc.vector.memset(pad[:, :, :], 0.0))
        copied, conv_ready = c.sem("qk_copied"), c.sem("qk_conv")
        W3 = PADW - 2

        def act_part(eng, tile, s, i):
            c.act(nc.scalar.copy(pad[:, s, 1:T + 1], c.ps[:, 4 * s:4 * s + 2, :].rearrange("p b t -> p (b t)")))
            c.act(nc.scalar.copy(pad[:, s, T + 2:TA + 2], c.ps[:, 4 * s + 2, 0:TC]))
            eng.nop().then_inc(copied, 1)
            eng.wait_ge(conv_ready, i * 2 + s + 1)
            c.act(nc.scalar.activation(qkT[:, bass.ds(tile, 1), 0:T].rearrange("p o t -> p (o t)"), tap[:, s, 0:T], ACT.Silu))
            c.act(nc.scalar.activation(qkT[:, bass.ds(tile, 1), T:TA].rearrange("p o t -> p (o t)"), tap[:, s, T + 1:TA + 1], ACT.Silu))

        def dve_part(eng, tile, s, i):
            w = [cw[:, j, bass.ds(tile, 1)] for j in range(4)]
            eng.wait_ge(copied, i * 2 + s + 1)
            c.dve(nc.vector.tensor_scalar(tap[:, s, 0:W3], pad[:, s, 1:W3 + 1], w[1], w[3], ALU.mult, ALU.add))
            c.dve(nc.vector.scalar_tensor_tensor(tap[:, s, 0:W3], pad[:, s, 0:W3], w[0], tap[:, s, 0:W3], ALU.mult, ALU.add))
            c.dve(nc.vector.scalar_tensor_tensor(tap[:, s, 0:W3], pad[:, s, 2:W3 + 2], w[2], tap[:, s, 0:W3], ALU.mult, ALU.add))
            eng.nop().then_inc(conv_ready, 1)
        project(c, 2 * MH, 1, DK, lambda part, t: w_in[:, :, bass.ds(t * P, P)], lambda part: hT, XCHUNKS,
                lambda s, part, n: c.ps[:, 4 * s + n, :], act_part, dve_part, 4, 3, wbuf)

    oT = c.sb("oT", [P, MH, T], s2)
    v = c.sb("v_m", [P, NBA, 512], s2)
    with ExitStack() as tmp:
        wbuf = c.sb("wbuf", [P, 2, 1, DK, P], tmp)

        def o_part(eng, tile, s, i):
            c.act(nc.scalar.activation(oT[:, bass.ds(tile, 1), :].rearrange("p o t -> p (o t)"),
                                       c.ps[:, 4 * s:4 * s + 2, :].rearrange("p b t -> p (b t)"), ACT.Sigmoid))
        project(c, MH, 1, DK, lambda part, t: w_in[:, :, bass.ds(t * P + OFF_O, P)], lambda part: hT, HALVES,
                lambda s, part, n: c.ps[:, 4 * s + n, :], o_part, lambda *a: None, 1, 0, wbuf)
    token_major(c, "v_m", [(0, w_in[:, :, OFF_V:OFF_V + 512])], 512, hT, plain_blocks(NBA), lambda b: v[:, b, :])
    negM = c.sb("negM", [MH, 2, T], s2)
    floor = c.sb("floor", [MH, 2, T], s2)
    with ExitStack() as s3:
        g = c.sb("g", [P, NBA, NG], s3)
        token_major(c, "gates", [(0, w_in[:, :, OFF_G:OFF_G + NG])], NG, hT, plain_blocks(NBA), lambda b: g[:, b, :])
        gates(c, io, g, hT, ident, negM, floor, between, keyw)
    if STOP <= 4:
        return
    mlstm_heads(c, hT, qkT, oT, v, negM, floor, between, keyw, sel, mgain, ones, mixT)


def carve(tile, parts, sizes):
    flat = tile[0:parts].rearrange("p k t -> p (k t)")
    at, views = 0, []
    for n in sizes:
        views.append(flat[:, at:at + n])
        at += n
    assert at <= flat.shape[1]
    return views


def gates(c, io, g, hT, ident, negM, floor, between, keyw):
    nc = c.nc
    with ExitStack() as s3:
        rows, reset, t1, t2 = carve(hT, MH, [4 * TA, 2 * TA, TA, TA])
        rows = rows.rearrange("p (k t) -> p k t", k=4)
        reset = reset.rearrange("p (k t) -> p k t", k=2)
        gb = c.sb("gb", [MH, 4], s3)
        later = c.sb("later", [MH, 2, NBA, NBA], s3)
        t3 = c.sb("t3", [MH, TA], s3)
        nat = rows.rearrange("p (d w) t -> p d w t", d=2)
        small = c.sb("small", [MH, 4, NBA], s3)
        grid = g[0:MH].rearrange("p b n -> p (b n)")[:, 0:NBA * NBA].rearrange("p (j i) -> p j i", j=NBA)
        load_all(c, "gate_consts", [(gb[:, :], io["gate_b"][0].rearrange("(k h) -> h k", h=MH)),
                                    (reset[:, :, :], io["k_reset"]), (later[:, :, :, :], io["k_later"])])
        turned, taken = c.sem("gates_turned"), c.sem("gates_taken")
        spans = [(slice(T, TA), slice(0, TC)), (slice(0, T), slice(TC, TA))]

        def rev(ap, d):
            return ap[:, ::-1] if d else ap

        with nc.Block() as block:
            @block.tensor
            def _(pe):
                for kind in range(4):
                    if kind >= 2:
                        pe.wait_ge(taken, kind - 1)
                    for b in range(NBA):
                        last = nc.tensor.transpose(c.ps[0:MH, 4 * (kind % 2) + b // 4, (b % 4) * P:(b % 4 + 1) * P],
                                                   g[:, b, kind * MH:(kind + 1) * MH], ident[:, :])
                    last.then_inc(turned, 1)

            @block.vector
            def _(dve):
                step = c.dve.on(dve)
                for kind in range(4):
                    dve.wait_ge(turned, kind + 1)
                    flat = c.ps[0:MH, 4 * (kind % 2):4 * (kind % 2) + 3, :].rearrange("p b t -> p (b t)")
                    for nat_s, proc_s in spans:
                        step(nc.vector.tensor_scalar(rows[:, kind, proc_s], rev(flat[:, nat_s], kind // 2),
                                                     gb[:, kind:kind + 1], None, ALU.add))
                    dve.nop().then_inc(taken, 1)

        with nc.Block() as block:
            abs_ready, soft_ready = c.sem("gate_abs"), c.sem("gate_soft")

            @block.scalar
            def _(act):
                step = c.act.on(act)
                for d in range(2):
                    t = (t1, t2)[d]
                    step(nc.scalar.activation(t[:, :], rows[:, 2 * d + 1, :], ACT.Abs))
                    step(nc.scalar.activation(t[:, :], t[:, :], ACT.Exp, scale=-1.0))
                    nc.scalar.activation(t[:, :], t[:, :], ACT.Ln, bias=1.0).then_inc(soft_ready, 1)

            @block.vector
            def _(dve):
                step = c.dve.on(dve)
                for d in range(2):
                    dve.wait_ge(soft_ready, d + 1)
                    step(nc.vector.scalar_tensor_tensor(rows[:, 2 * d + 1, :], rows[:, 2 * d + 1, :], 0.0,
                                                        (t1, t2)[d][:, :], ALU.min, ALU.subtract))

        with nc.Block() as block:
            m_ready = c.sem("gate_m")

            @block.vector
            def _(dve):
                step = c.dve.on(dve)
                blk = lambda ap: ap.rearrange("p (b t) -> p b t", t=P)
                for d in range(2):
                    li, lf = rows[:, 2 * d, :], rows[:, 2 * d + 1, :]
                    L, U, C = t1[:, :], t2[:, :], t3[:, :]
                    step(nc.vector.tensor_tensor_scan(L, reset[:, 0, :], lf, 0.0, ALU.mult, ALU.add))
                    step(nc.vector.tensor_tensor(U, li, L, ALU.subtract))
                    step(nc.vector.tensor_tensor_scan(C, reset[:, 1, :], U, NEG, ALU.add, ALU.max))
                    step(nc.vector.tensor_copy(small[:, 0, :], blk(L)[:, :, P - 1]))
                    step(nc.vector.tensor_tensor(small[:, 1, :], blk(C)[:, :, P - 1], small[:, 0, :], ALU.add))
                    step(nc.vector.tensor_tensor_scan(small[:, 2, :], small[:, 0, :], small[:, 1, :], NEG, ALU.add, ALU.max))
                    step(nc.vector.memset(grid[:, :, :], 0.0))
                    step(nc.vector.tensor_tensor(grid[:, :, 1:NBA], later[:, 0, :, 1:NBA],
                                                 small[:, 0, 0:NBA - 1].unsqueeze(1).to_broadcast([MH, NBA, NBA - 1]), ALU.mult))
                    step(nc.vector.tensor_tensor_scan(between[:, d].rearrange("p j i -> p (j i)"),
                                                      later[:, 1].rearrange("p j i -> p (j i)"),
                                                      grid[:, :, :].rearrange("p j i -> p (j i)"), 0.0, ALU.mult, ALU.add))
                    step(nc.vector.tensor_tensor(blk(C)[:, 2:NBA, :], blk(C)[:, 2:NBA, :],
                                                 small[:, 2, 1:NBA - 1].unsqueeze(2).to_broadcast([MH, NB, P]), ALU.max))
                    step(nc.vector.tensor_tensor(L[:, TC:TA], L[:, TC:TA], C[:, TC:TA], ALU.add))
                    for nat_s, proc_s in spans:
                        step(nc.vector.tensor_copy(nat[:, d, 1, nat_s], rev(U[:, proc_s], d)))
                    step(nc.vector.tensor_tensor(blk(U), blk(U), small[:, 0, :].unsqueeze(2).to_broadcast([MH, NBA, P]), ALU.add))
                    for nat_s, proc_s in spans:
                        step(nc.vector.tensor_copy(nat[:, d, 0, nat_s], rev(U[:, proc_s], d)))
                    step(nc.vector.tensor_scalar(negM[:, d, :], rev(C[:, TC:TA], d), -1.0, None, ALU.mult))
                    step(nc.vector.tensor_scalar(floor[:, d, :], rev(L[:, TC:TA], d), -1.0, 88.0, ALU.mult, ALU.min))
                    dve.nop().then_inc(m_ready, 1)

            @block.scalar
            def _(act):
                step = c.act.on(act)
                for d in range(2):
                    act.wait_ge(m_ready, d + 1)
                    step(nc.scalar.activation(floor[:, d, :], floor[:, d, :], ACT.Exp))

        with nc.Block() as block:
            cols_ready = c.sem("gate_cols")
            flat = c.ps[:, 0, 0:2 * 2 * NBA * MH].rearrange("p (d w b h) -> p d w b h", d=2, w=2, b=NBA)

            @block.tensor
            def _(pe):
                for d in range(2):
                    for w in range(2):
                        for b in range(NBA):
                            last = nc.tensor.transpose(flat[:, d, w, b, :], nat[:, d, w, b * P:(b + 1) * P], ident[0:MH, 0:MH])
                last.then_inc(cols_ready, 1)

            @block.vector
            def _(dve):
                dve.wait_ge(cols_ready, 1)
                c.dve.on(dve)(nc.vector.tensor_copy(keyw[:, :, :, :, :].rearrange("p d w b h -> p (d w b h)"),
                                                    c.ps[:, 0, 0:2 * 2 * NBA * MH]))


def mlstm_heads(c, hT, qkT, oT, v, negM, floor, between, keyw, sel, mgain, ones, mixT):
    nc = c.nc
    SCALE = float(P) ** -0.5
    units = []
    for h in range(MH):
        for d in range(2):
            units += [("negM", h, d, None), ("floor", h, d, None)]
            for j in range(NBA):
                if j < 2:
                    b, t0, t1, diag = (NB + j, NB + 1 - j)[d], 0, T, None
                else:
                    b = (j - 2, NBA - 1 - j)[d]
                    t0, t1 = ((b * P, T), (0, (b + 1) * P))[d]
                    diag = b * P
                units.append(("key", h, d, (j, b, t0, t1, diag)))
        units.append(("norm", h, None, None))
    with ExitStack() as tmp:
        bias, low, S, mask, w, h_sum = carve(hT, P, [2 * T, 2 * T, MH * 2 * NBA * NBA, 2 * P, 2 * T, T])
        bias = bias.rearrange("p (d t) -> p d t", d=2)
        low = low.rearrange("p (d t) -> p d t", d=2)
        S = S.rearrange("p (h d x) -> p h d x", h=MH, d=2)
        mask = mask.rearrange("p (d t) -> p d t", d=2)
        w = w.rearrange("p (s t) -> p s t", s=2)
        load_all(c, "tri_loaded", [(mask[:, :, :], c.io["k_tri"])])
        scores_ready, args_ready = c.sem("scores_ready"), c.sem("args_ready")
        weights_ready, probs_ready, summed = c.sem("weights_ready"), c.sem("probs_ready"), c.sem("summed")
        pair_summed, den_copied, pair_done = c.sem("pair_summed"), c.sem("den_copied"), c.sem("pair_done")
        sq_ready, root_ready = c.sem("hn_squared"), c.sem("hn_root")

        def slices(t0, t1):
            return [(b, max(t0, b * BANK), min(t1, (b + 1) * BANK)) for b in range(2)
                    if max(t0, b * BANK) < min(t1, (b + 1) * BANK)]

        with nc.Block() as block:
            bet_ready = c.sem("between_ready")

            @block.tensor
            def _(pe):
                for h in range(MH):
                    last = nc.tensor.matmul(c.ps[:, h, 0:200], sel[:, h, :], between[:, :, :, :].rearrange("p d j i -> p (d j i)"),
                                            start=True, stop=True)
                last.then_inc(bet_ready, 1)

            @block.vector
            def _(dve):
                dve.wait_ge(bet_ready, 1)
                c.dve.on(dve)(nc.vector.tensor_copy(S[:, :, :, :].rearrange("p h d x -> p h (d x)"), c.ps[:, 0:MH, 0:200]))
        S4 = S[:, :, :, :].rearrange("p h d (j i) -> p h d j i", j=NBA)

        key_no, pair_no, n, m = [], [], 0, 0
        for kind, h, d, x in units:
            key_no.append(n)
            n += kind == "key"
            if kind == "negM":
                m += 1
            pair_no.append(m)

        with nc.Block() as block:
            num = lambda b: c.ps[:, 4 + b, :]
            den = lambda b: c.ps[:, 6 + b, :]

            @block.tensor
            def _(pe):
                def first(u):
                    kind, h, d, x = units[u]
                    if u >= 2:
                        pe.wait_ge(probs_ready, u - 1)
                    for b, lo, hi in (slices(x[2], x[3]) if kind == "key" else slices(0, T)):
                        dst = c.ps[:, 2 * (u % 2) + b, lo - b * BANK:hi - b * BANK]
                        if kind == "key":
                            last = nc.tensor.matmul(dst, qkT[:, MH + h, x[1] * P:(x[1] + 1) * P], qkT[:, h, lo:hi],
                                                    start=True, stop=True)
                        elif kind == "norm":
                            if b == 0:
                                pe.wait_ge(sq_ready, h + 1)
                            last = nc.tensor.matmul(dst, ones[:, :], w[:, u % 2, lo:hi], start=True, stop=True)
                        else:
                            last = nc.tensor.matmul(dst, sel[:, h, :], (negM if kind == "negM" else floor)[:, d, lo:hi],
                                                    start=True, stop=True)
                    last.then_inc(scores_ready, 1)

                def second(u):
                    kind, h, d, x = units[u]
                    if kind != "key":
                        return
                    j, kb, t0, t1, diag = x
                    if j == 0 and pair_no[u] > 1:
                        pe.wait_ge(pair_done, pair_no[u] - 1)
                    pe.wait_ge(probs_ready, u + 1)
                    for b, lo, hi in slices(t0, t1):
                        cols = slice(lo - b * BANK, hi - b * BANK)
                        nc.tensor.matmul(num(b)[:, cols], v[:, kb, h * P:(h + 1) * P], w[:, u % 2, lo:hi],
                                         start=(j == 0), stop=False, skip_group_check=True)
                        last = nc.tensor.matmul(den(b)[:, cols], ones[:, :], w[:, u % 2, lo:hi],
                                                start=(j == 0), stop=False, skip_group_check=True)
                    last.then_inc(summed, 1)
                    if j == NBA - 1:
                        pe.wait_ge(summed, key_no[u] + 1)
                        pe.nop().then_inc(pair_summed, 1)
                first(0)
                for u in range(len(units)):
                    if u + 1 < len(units) and units[u + 1][0] != "norm":
                        first(u + 1)
                    second(u)
                    if u + 1 < len(units) and units[u + 1][0] == "norm":
                        first(u + 1)

            @block.gpsimd
            def _(pool):
                step = c.pool.on(pool)
                for u, (kind, h, d, x) in enumerate(units):
                    if kind != "key":
                        continue
                    j, kb, t0, t1, diag = x
                    if j == 0:
                        pool.wait_ge(probs_ready, u - 1)
                    if u >= 2:
                        prev = [p for p in range(u - 1) if (u - p) % 2 == 0 and units[p][0] != "negM" and units[p][0] != "floor"]
                        if prev and units[prev[-1]][0] == "key":
                            pool.wait_ge(summed, key_no[prev[-1]] + 1)
                        elif prev:
                            pool.wait_ge(probs_ready, prev[-1] + 1)
                            if key_no[prev[-1]]:
                                pool.wait_ge(summed, key_no[prev[-1]])
                    B = bias[:, d, :]
                    far = (t0, t1) if diag is None else ((diag + P, t1) if d == 0 else (t0, diag))
                    if diag is not None:
                        nc.gpsimd.tensor_tensor(w[:, u % 2, diag:diag + P], B[:, diag:diag + P], mask[:, d, :], ALU.add).then_inc(args_ready, 1)
                    if far[0] < far[1]:
                        q0, q1 = far[0] // P, far[1] // P
                        i0 = (q0 + 2, NBA - 1 - q0)[d]
                        i1 = i0 + (q1 - q0) * (1, -1)[d]
                        s = S4[:, h, d, j, i0:i1] if d == 0 else S4[:, h, d, j, i0:(i1 if i1 >= 0 else None):-1]
                        nc.gpsimd.tensor_tensor(w[:, u % 2, far[0]:far[1]].rearrange("p (q t) -> p q t", t=P),
                                                B[:, far[0]:far[1]].rearrange("p (q t) -> p q t", t=P),
                                                s.unsqueeze(2).to_broadcast([P, q1 - q0, P]), ALU.add).then_inc(args_ready, 1)

            @block.scalar
            def _(act):
                step = c.act.on(act)
                n = 0
                for u, (kind, h, d, x) in enumerate(units):
                    if kind == "norm":
                        act.wait_ge(pair_done, pair_no[u])
                        prev = [p for p in range(u) if (u - p) % 2 == 0 and units[p][0] == "key"]
                        act.wait_ge(summed, key_no[prev[-1]] + 1)
                        nc.scalar.activation(w[:, u % 2, :], h_sum[:, :], ACT.Square).then_inc(sq_ready, 1)
                        act.wait_ge(args_ready, n)
                        act.wait_ge(scores_ready, u + 1)
                        step(nc.scalar.activation(low[:, 0, :], c.ps[:, 2 * (u % 2):2 * (u % 2) + 2, :].rearrange("p b t -> p (b t)"),
                                                  ACT.Sqrt, scale=1.0 / P, bias=c.eps[:, 0:1]))
                        act.nop().then_inc(root_ready, 1)
                        continue
                    if kind != "key":
                        continue
                    j, kb, t0, t1, diag = x
                    far = (t0, t1) if diag is None else ((diag + P, t1) if d == 0 else (t0, diag))
                    if diag is not None:
                        n += 1
                        act.wait_ge(args_ready, n)
                        last = step(nc.scalar.activation(w[:, u % 2, diag:diag + P], w[:, u % 2, diag:diag + P], ACT.Exp,
                                                         bias=keyw[:, d, 1, kb, h:h + 1]))
                    if far[0] < far[1]:
                        n += 1
                        act.wait_ge(args_ready, n)
                        step(nc.scalar.activation(w[:, u % 2, far[0]:far[1]], w[:, u % 2, far[0]:far[1]], ACT.Exp,
                                                  bias=keyw[:, d, 0, kb, h:h + 1]))
                    act.nop().then_inc(weights_ready, 1)
                    if j == NBA - 1:
                        act.wait_ge(pair_summed, pair_no[u])
                        nc.scalar.activation(bias[:, d, :], c.ps[:, 6:8, :].rearrange("p b t -> p (b t)"), ACT.Abs).then_inc(den_copied, 1)

            @block.vector
            def _(dve):
                step = c.dve.on(dve)
                for u, (kind, h, d, x) in enumerate(units):
                    dve.wait_ge(scores_ready, u + 1)
                    flat = c.ps[:, 2 * (u % 2):2 * (u % 2) + 2, :].rearrange("p b t -> p (b t)")
                    if kind in ("negM", "floor"):
                        dst = (bias if kind == "negM" else low)[:, d, :]
                        nc.vector.tensor_copy(dst, flat).then_inc(probs_ready, 1)
                    elif kind == "key":
                        j, kb, t0, t1, diag = x
                        dve.wait_ge(weights_ready, key_no[u] + 1)
                        nc.vector.scalar_tensor_tensor(w[:, u % 2, t0:t1], flat[:, t0:t1], SCALE, w[:, u % 2, t0:t1],
                                                       ALU.mult, ALU.mult).then_inc(probs_ready, 1)
                        if j == NBA - 1:
                            dve.wait_ge(den_copied, pair_no[u])
                            step(nc.vector.tensor_tensor(bias[:, d, :], bias[:, d, :], low[:, d, :], ALU.max))
                            step(nc.vector.reciprocal(bias[:, d, :], bias[:, d, :]))
                            both = c.ps[:, 4:6, :].rearrange("p b t -> p (b t)")
                            if d == 0:
                                step(nc.vector.tensor_tensor(h_sum[:, :], both, bias[:, d, :], ALU.mult))
                            else:
                                step(nc.vector.tensor_tensor(bias[:, d, :], both, bias[:, d, :], ALU.mult))
                                step(nc.vector.tensor_tensor(h_sum[:, :], h_sum[:, :], bias[:, d, :], ALU.add))
                            dve.nop().then_inc(pair_done, 1)
                    else:
                        dve.wait_ge(root_ready, h + 1)
                        step(nc.vector.reciprocal(low[:, 0, :], low[:, 0, :]))
                        step(nc.vector.scalar_tensor_tensor(h_sum[:, :], h_sum[:, :], mgain[:, h:h + 1], low[:, 0, :], ALU.mult, ALU.mult))
                        step(nc.vector.tensor_tensor(mixT[:, h, :], h_sum[:, :], oT[:, h, :], ALU.mult))
                        dve.nop().then_inc(probs_ready, 1)


def window(c, io, w_in, hT, ident, mixT, s2):
    nc = c.nc
    AT = AH // 2
    qT = c.sb("qaT", [P, AT, T], s2)
    kT = c.sb("kaT", [P, KVH, TA], s2)
    va = c.sb("v_a", [P, NBA, P], s2)
    with ExitStack() as tmp:
        rope = c.sb("rope", [P, 2, T], tmp)
        swap = c.sb("swap", [P, P], tmp)
        wq = c.sb("w_qa", [P, DK, 5 * P], tmp)
        raw = c.sb("raw", [P, 2, TA], tmp)
        loaded, summed, raw_ready, swapped, roped = (c.sem("rope_" + n) for n in ("w", "sum", "raw", "swap", "done"))
        dup = c.sem("k_dup")
        with nc.Block() as block:
            @block.sync
            def _(sp):
                sp.dma_start(wq[:, :, :], w_in[:, :, OFF_QA:OFF_VA]).then_inc(loaded, 16)
                sp.dma_start(rope[:, :, :], io["k_rope"]).then_inc(loaded, 16)
                sp.dma_start(swap[:, :], io["k_swap"]).then_inc(loaded, 16)
                sp.wait_ge(roped, 5)
                sp.dma_start(kT[64:128, 0, :], kT[0:64, 0, :]).then_inc(dup, 16)
                sp.dma_start(kT[0:64, 1, :], kT[64:128, 1, :]).then_inc(dup, 16)
                sp.wait_ge(dup, 32)

            @block.tensor
            def _(pe):
                pe.wait_ge(loaded, 48)
                for m in range(5):
                    if m >= 1:
                        pe.wait_ge(raw_ready, m)
                    for n, (at, size) in enumerate(HALVES if m < 4 else XCHUNKS):
                        for k in range(DK):
                            last = nc.tensor.matmul(c.ps[:, n, 0:size], wq[:, k, m * P:(m + 1) * P], hT[:, k, at:at + size],
                                                    start=(k == 0), stop=(k == DK - 1))
                    last.then_inc(summed, 1)
                    pe.wait_ge(raw_ready, m + 1)
                    if m >= 2:
                        pe.wait_ge(roped, m - 1)
                    for n in range(2):
                        last = nc.tensor.matmul(c.ps[:, 4 + 2 * (m % 2) + n, :], swap[:, :], raw[:, m % 2, n * BANK:(n + 1) * BANK],
                                                start=True, stop=True)
                    last.then_inc(swapped, 1)

            @block.scalar
            def _(act):
                step = c.act.on(act)
                for m in range(5):
                    act.wait_ge(summed, m + 1)
                    if m >= 2:
                        act.wait_ge(roped, m - 1)
                    step(nc.scalar.copy(raw[:, m % 2, 0:T], c.ps[:, 0:2, :].rearrange("p b t -> p (b t)")))
                    if m == 4:
                        step(nc.scalar.mul(kT[0:64, 0, T:TA], c.ps[0:64, 2, 0:TC], 0.125))
                        step(nc.scalar.mul(kT[64:128, 1, T:TA], c.ps[64:128, 2, 0:TC], 0.125))
                    act.nop().then_inc(raw_ready, 1)

            @block.vector
            def _(dve):
                step = c.dve.on(dve)
                for m in range(5):
                    dve.wait_ge(swapped, m + 1)
                    sw = c.ps[:, 4 + 2 * (m % 2):6 + 2 * (m % 2), :].rearrange("p b t -> p (b t)")
                    for lo, hi, dst, s in ([(0, P, qT[:, m, :], 1.0)] if m < 4 else
                                           [(0, 64, kT[0:64, 0, 0:T], 0.125), (64, P, kT[64:128, 1, 0:T], 0.125)]):
                        step(nc.vector.scalar_tensor_tensor(dst, sw[lo:hi, :], s, rope[lo:hi, 1, :], ALU.mult, ALU.mult))
                        step(nc.vector.scalar_tensor_tensor(raw[lo:hi, m % 2, 0:T], raw[lo:hi, m % 2, 0:T], s, rope[lo:hi, 0, :],
                                                            ALU.mult, ALU.mult))
                        step(nc.vector.tensor_tensor(dst, dst, raw[lo:hi, m % 2, 0:T], ALU.add))
                    dve.nop().then_inc(roped, 1)
    token_major(c, "v_a", [(0, w_in[:, :, OFF_VA:OFF_VA + P])], P, hT, plain_blocks(NBA), lambda b: va[:, b, :])
    if STOP <= 2:
        return
    with ExitStack() as tmp:
        W = 3 * P
        mask = c.sb("band", [P, W], tmp)
        sink = c.sb("sink", [P, AH], tmp)
        lg = c.sb("lg", [P, 2, 2, W + TC + 1], tmp)
        st = c.sb("st", [P, 2, 3, 2], tmp)
        pt = c.sb("pt", [P, 2, 2, 5, P], tmp)
        load_all(c, "band_loaded", [(mask[:, :], io["k_band"]), (sink[:, :], io["attn_sink"].partition_broadcast(P)[:, 0, :] if False else bass.AP(io["attn_sink"].tensor, 0, [[0, P], [1, AH]]))])
        units = [(n, g) for n in range(NB) for g in range(AH // 2)]
        sc_ready, sc_band_read, sc_ctx_read = c.sem("aw_scores"), c.sem("aw_band_read"), c.sem("aw_ctx_read")
        max_ready, exp_ready, p_ready, t_ready = c.sem("aw_max"), c.sem("aw_exp"), c.sem("aw_p"), c.sem("aw_t")
        t_dve, t_act, pv_ready, y_ready = c.sem("aw_t_dve"), c.sem("aw_t_act"), c.sem("aw_pv"), c.sem("aw_y")

        def band(n):
            lo, hi = max(0, (n - 1) * P), min(T, (n + 2) * P)
            return lo, hi, lo - (n - 1) * P

        with nc.Block() as block:
            @block.tensor
            def _(pe):
                def scores(u):
                    n, g = units[u]
                    lo, hi, off = band(n)
                    if u >= 1:
                        pe.wait_ge(sc_band_read, u)
                        pe.wait_ge(sc_ctx_read, u)
                    for h in range(2):
                        r = slice(64 * h, 64 * h + 64)
                        q = qT[r, g, n * P:(n + 1) * P]
                        nc.tensor.matmul(c.ps[:, h, 0:hi - lo], q, kT[r, g // 2, lo:hi], start=True, stop=True)
                        last = nc.tensor.matmul(c.ps[:, 2 + h, 0:TC], q, kT[r, g // 2, T:TA], start=True, stop=True)
                    last.then_inc(sc_ready, 1)
                scores(0)
                for u, (n, g) in enumerate(units):
                    if u + 1 < len(units):
                        scores(u + 1)
                    lo, hi, off = band(n)
                    nk = (hi - lo) // P + 2
                    pe.wait_ge(p_ready, u + 1)
                    if u >= 1:
                        pe.wait_ge(t_dve, u)
                        pe.wait_ge(t_act, u)
                    for x in range(2 * nk):
                        last = nc.tensor.transpose(c.ps[:, 4 + x // 4, (x % 4) * P:(x % 4 + 1) * P],
                                                   lg[:, u % 2, x // nk, (x % nk) * P:(x % nk + 1) * P], ident[:, :])
                    last.then_inc(t_ready, 1)
                    pe.wait_ge(t_dve, u + 1)
                    pe.wait_ge(t_act, u + 1)
                    if u >= 1:
                        pe.wait_ge(y_ready, u)
                    for h in range(2):
                        for x in range(nk):
                            kb = lo // P + x if x < nk - 2 else NB + x - (nk - 2)
                            last = nc.tensor.matmul(c.ps[64 * h:64 * h + 64, 7, 0:P], va[:, kb, (g // 2) * 64:(g // 2) * 64 + 64],
                                                    pt[:, u % 2].rearrange("p h x q -> p (h x) q")[:, h * nk + x, :],
                                                    start=(x == 0), stop=(x == nk - 1))
                    last.then_inc(pv_ready, 1)

            @block.vector
            def _(dve):
                step = c.dve.on(dve)
                for u, (n, g) in enumerate(units):
                    lo, hi, off = band(n)
                    bw = hi - lo
                    nk = bw // P + 2
                    s = u % 2
                    dve.wait_ge(sc_ready, u + 1)
                    if u >= 2:
                        dve.wait_ge(t_ready, u - 1)
                    step(nc.vector.tensor_tensor(lg[:, s, :, 0:bw], c.ps[:, 0:2, 0:bw],
                                                 mask[:, off:off + bw].unsqueeze(1).to_broadcast([P, 2, bw]), ALU.add))
                    dve.nop().then_inc(sc_band_read, 1)
                    step(nc.vector.tensor_copy(lg[:, s, :, bw + TC], sink[:, 2 * g:2 * g + 2]))
                    dve.wait_ge(sc_ctx_read, u + 1)
                    step(nc.vector.tensor_reduce(st[:, s, 0, :], lg[:, s, :, 0:bw + TC + 1], AX.X, ALU.max))
                    step(nc.vector.tensor_scalar(st[:, s, 0, :], st[:, s, 0, :], -1.0, None, ALU.mult))
                    dve.nop().then_inc(max_ready, 1)
                    dve.wait_ge(exp_ready, u + 1)
                    step(nc.vector.reciprocal(st[:, s, 2, :], st[:, s, 1, :]))
                    for h in range(2):
                        step(nc.vector.tensor_scalar(lg[:, s, h, 0:bw + TC], lg[:, s, h, 0:bw + TC], st[:, s, 2, h:h + 1], None, ALU.mult))
                    dve.nop().then_inc(p_ready, 1)
                    dve.wait_ge(t_ready, u + 1)
                    if u >= 2:
                        dve.wait_ge(pv_ready, u - 1)
                    flat = pt[:, s].rearrange("p h x q -> p (h x q)")
                    step(nc.vector.tensor_copy(flat[:, 0:BANK], c.ps[:, 4, :]))
                    dve.nop().then_inc(t_dve, 1)
                    dve.wait_ge(pv_ready, u + 1)
                    step(nc.vector.tensor_copy(mixT[:, 4 + g, n * P:(n + 1) * P], c.ps[:, 7, 0:P]))
                    dve.nop().then_inc(y_ready, 1)

            @block.scalar
            def _(act):
                step = c.act.on(act)
                for u, (n, g) in enumerate(units):
                    lo, hi, off = band(n)
                    bw = hi - lo
                    nk = bw // P + 2
                    s = u % 2
                    act.wait_ge(sc_ready, u + 1)
                    if u >= 2:
                        act.wait_ge(t_ready, u - 1)
                    step(nc.scalar.copy(lg[:, s, :, bw:bw + TC], c.ps[:, 2:4, 0:TC]))
                    act.nop().then_inc(sc_ctx_read, 1)
                    act.wait_ge(max_ready, u + 1)
                    for h in range(2):
                        step(nc.scalar.activation(lg[:, s, h, 0:bw + TC + 1], lg[:, s, h, 0:bw + TC + 1], ACT.Exp,
                                                  bias=st[:, s, 0, h:h + 1], accum_out=st[:, s, 1, h:h + 1]))
                    act.nop().then_inc(exp_ready, 1)
                    act.wait_ge(t_ready, u + 1)
                    if u >= 2:
                        act.wait_ge(pv_ready, u - 1)
                    flat = pt[:, s].rearrange("p h x q -> p (h x q)")
                    rest = 2 * nk * P - BANK
                    step(nc.scalar.copy(flat[:, BANK:BANK + rest], c.ps[:, 5:7, :].rearrange("p b t -> p (b t)")[:, 0:rest]))
                    act.nop().then_inc(t_act, 1)


POOLS = (2, 4, 8, 16)
DIL, DH, DE = (1, 4, 16), 4, 64
SB_E = 128
O_POOL, O_DIL, O_SB, O_S5 = 0, 512, 2816, 4352
Y_POOL, Y_DIL, Y_SB, Y_S5, Y_TILES = 0, 4, 6, 10, 14
BRANCH_TILES = (4, 2, 4, 4)
SKEW = 384
ROUND = 1.5 * 2.0 ** 23
QT = 16
SC = 16


def second_block(c, io, xT, ident, ones, gains, final2):
    nc = c.nc
    with ExitStack() as s1:
        merged = None
        xnT = c.sb("xnT", [P, DK, T], s1)
        norm(c, "norm2", [(xT, at, n, lambda k: gains[:, 3, k:k + 1], None, at) for at, n in HALVES],
             ones, xnT, shift=False)
        yT = c.sb("yT", [P, Y_TILES, T], s1)
        w_in = io["w_in_2"][0].rearrange("(k p) n -> p k n", p=P)
        with ExitStack() as s2:
            pool_branch(c, io, w_in, xnT, yT, s2)
        if STOP <= 21:
            return
        c.end_stage()
        with ExitStack() as s2:
            dilated_branch(c, io, w_in, xnT, yT, ident, s2)
        if STOP <= 22:
            return
        c.end_stage()
        with ExitStack() as s2:
            stick_branch(c, io, w_in, xnT, yT, ones, s2)
        if STOP <= 23:
            return
        c.end_stage()
        with ExitStack() as s2:
            s5_branch(c, io, w_in, xnT, yT, ident, s2)
        if STOP <= 24:
            return
        c.end_stage()
        with ExitStack() as s2:
            merged = c.sb("merged", [P, DK, T], s2)
            merge(c, io, xnT, yT, merged, s2)
            residual(c, io["w_out_2"][0], DK, merged, xT, None, "out2")
    if STOP <= 25:
        return
    with ExitStack() as s2:
        hid = c.sb("hid2", [P, FK, T], s2)
        with ExitStack() as s3:
            hT = c.sb("hT2", [P, DK, T], s3)
            wbuf = c.sb("wbuf", [P, 2, 2, DK, P], s3)
            act_out = c.sb("silu", [P, 2, T], s3)
            norm(c, "norm_ffn2", [(xT, at, n, lambda k: gains[:, 4, k:k + 1], None, at) for at, n in HALVES],
                 ones, hT, shift=False)
            silu_ready = c.sem("silu_ready")
            wv = io["w_up_2"][0].rearrange("(k p) n -> p k n", p=P)

            def act_part(eng, tile, s, i):
                c.act(nc.scalar.activation(act_out[:, s, :], c.ps[:, 4 * s:4 * s + 2, :].rearrange("p b t -> p (b t)"), ACT.Silu))
                eng.nop().then_inc(silu_ready, 1)

            def dve_part(eng, tile, s, i):
                eng.wait_ge(silu_ready, i * 2 + s + 1)
                c.dve(nc.vector.tensor_tensor(hid[:, bass.ds(tile, 1), :].rearrange("p o t -> p (o t)"),
                                              c.ps[:, 4 * s + 2:4 * s + 4, :].rearrange("p b t -> p (b t)"),
                                              act_out[:, s, :], ALU.mult))
            project(c, FK, 2, DK, lambda part, t: wv[:, :, bass.ds(t * P + part * FF, P)], lambda part: hT, HALVES,
                    lambda s, part, n: c.ps[:, 4 * s + 2 * part + n, :], act_part, dve_part, 1, 1, wbuf)
        residual(c, io["w_down_2"][0], FK, hid, xT, None, "down2")
    norm(c, "final2", [(xT, at, n, lambda k: final2[:, k:k + 1], None, at) for at, n in HALVES],
         ones, xT, shift=False)
    turn_out(c, io, xT, ident)


def turn_out(c, io, xT, ident):
    nc = c.nc
    with ExitStack() as tmp:
        rows = c.sb("out_rows", [P, 2, D], tmp)
        turned, dve_copied, act_copied = c.sem("out_turned"), c.sem("out_dve"), c.sem("out_act")
        stored = [c.sem(f"out_stored{s}") for s in range(2)]
        with nc.Block() as block:
            @block.tensor
            def _(pe):
                for b in range(NB):
                    if b >= 2:
                        pe.wait_ge(dve_copied, b - 1)
                        pe.wait_ge(act_copied, b - 1)
                    for k in range(DK):
                        last = nc.tensor.transpose(c.ps[:, 2 * (b % 2) + k // 4, (k % 4) * P:(k % 4 + 1) * P],
                                                   xT[:, k, b * P:(b + 1) * P], ident[:, :])
                    last.then_inc(turned, 1)

            @block.vector
            def _(dve):
                for b in range(NB):
                    dve.wait_ge(turned, b + 1)
                    if b >= 2:
                        dve.wait_ge(stored[b % 2], 16 * (b // 2))
                    nc.vector.tensor_copy(rows[:, b % 2, 0:BANK], c.ps[:, 2 * (b % 2), :]).then_inc(dve_copied, 1)

            @block.scalar
            def _(act):
                for b in range(NB):
                    act.wait_ge(turned, b + 1)
                    if b >= 2:
                        act.wait_ge(stored[b % 2], 16 * (b // 2))
                    nc.scalar.copy(rows[:, b % 2, BANK:D], c.ps[:, 2 * (b % 2) + 1, :]).then_inc(act_copied, 1)

            @block.sync
            def _(sp):
                for b in range(NB):
                    sp.wait_ge(dve_copied, b + 1)
                    sp.wait_ge(act_copied, b + 1)
                    sp.dma_start(io["out"][0, b * P:(b + 1) * P, :], rows[:, b % 2, :]).then_inc(stored[b % 2], 16)
                for s in range(2):
                    sp.wait_ge(stored[s], 16 * (NB // 2))


def copy_tiles(c, w_in, col0, tiles, src, dst, scale=1.0):
    nc = c.nc
    with ExitStack() as tmp:
        wbuf = c.sb("wbuf", [P, 2, 1, DK, P], tmp)

        def act_part(eng, tile, s, i):
            c.act(nc.scalar.mul(dst[:, bass.ds(tile, 1), :].rearrange("p o t -> p (o t)"),
                                c.ps[:, 2 * s:2 * s + 2, :].rearrange("p b t -> p (b t)"), scale))
        project(c, tiles, 1, DK, lambda part, t: w_in[:, :, bass.ds(t * P + col0, P)], lambda part: src, HALVES,
                lambda s, part, n: c.ps[:, 2 * s + n, :], act_part, lambda *a: None, 1, 0, wbuf)


def pool_branch(c, io, w_in, xnT, yT, s2):
    nc = c.nc
    G = len(POOLS)
    u = c.sb("u_pool", [P, NB, G * P], s2)
    token_major(c, "u_pool", [(0, w_in[:, :, O_POOL:O_POOL + G * P])], G * P, xnT, plain_blocks(NB), lambda b: u[:, b, :])
    band, wg, sc = c.sb("pool_band", [P, G, 3, P], s2), c.sb("pool_w", [P, G, P], s2), c.sb("pool_sc", [P, G], s2)
    p = c.sb("pool_p", [P, 2, T], s2)
    load_all(c, "pool_loaded", [(band[:, :, :, :], io["k_pool"]), (wg[:, :, :], io["pool_w_2"][0].rearrange("g c d -> c g d")),
                                (sc[:, :], col(io["pool_scale_2"][0]))])
    meaned, p_ready, mixed, y_ready = (c.sem("pool_" + n) for n in ("mean", "p", "mix", "y"))
    flat = lambda b: c.ps[:, b:b + 2, :].rearrange("p b t -> p (b t)")
    with nc.Block() as block:
        @block.tensor
        def _(pe):
            def means(g):
                if g >= 2:
                    pe.wait_ge(p_ready, g - 1)
                for b in range(NB):
                    dst = c.ps[:, 2 * (g % 2) + b // 4, (b % 4) * P:(b % 4 + 1) * P]
                    last = nc.tensor.matmul(dst, u[:, b, g * P:(g + 1) * P], band[:, g, 0 if b == 0 else 1, :],
                                            start=True, stop=(b == 0))
                    if b:
                        last = nc.tensor.matmul(dst, u[:, b - 1, g * P:(g + 1) * P], band[:, g, 2, :], start=False, stop=True)
                last.then_inc(meaned, 1)
            means(0)
            for g in range(G):
                if g + 1 < G:
                    means(g + 1)
                pe.wait_ge(p_ready, g + 1)
                if g >= 2:
                    pe.wait_ge(y_ready, g - 1)
                for n in range(2):
                    last = nc.tensor.matmul(c.ps[:, 4 + 2 * (g % 2) + n, :], wg[:, g, :], p[:, g % 2, n * BANK:(n + 1) * BANK],
                                            start=True, stop=True)
                last.then_inc(mixed, 1)

        @block.vector
        def _(dve):
            for g in range(G):
                dve.wait_ge(meaned, g + 1)
                if g >= 2:
                    dve.wait_ge(mixed, g - 1)
                nc.vector.tensor_copy(p[:, g % 2, :], flat(2 * (g % 2))).then_inc(p_ready, 1)

        @block.scalar
        def _(act):
            for g in range(G):
                act.wait_ge(mixed, g + 1)
                nc.scalar.activation(yT[:, Y_POOL + g, :], flat(4 + 2 * (g % 2)), ACT.Copy, scale=sc[:, g:g + 1]).then_inc(y_ready, 1)


def dilated_branch(c, io, w_in, xnT, yT, ident, s2):
    nc = c.nc
    ROW = DH * DE + DH
    o = c.sb("o_dil", [P, 3, NB, ROW], s2)
    stat = c.sb("stat", [P, 3, NB, 3, DH], s2)
    scratch = nc.dram_tensor("dil_scratch", (2, T, ROW), F32, kind="Internal").ap()
    skewed = nc.dram_tensor("bias_scratch", (3, DH, P, SKEW), F32, kind="Internal").ap()
    with ExitStack() as tmp:
        rel, oh = c.sb("rel", [32, 3 * DH], tmp), c.sb("onehot", [32, 3, SKEW], tmp)
        off = c.sb("bias_off", [DH, 3, SKEW], tmp)
        load_all(c, "rel_loaded", [(rel[:, :], io["rel_bias_2"]), (oh[:, :, :], io["k_onehot"]), (off[:, :, :], io["k_skewmask"])])
        summed, ready, stored = c.sem("rel_sum"), c.sem("rel_ready"), c.sem("rel_stored")
        with nc.Block() as block:
            @block.tensor
            def _(pe):
                for g in range(3):
                    last = nc.tensor.matmul(c.ps[0:DH, g, 0:SKEW], rel[:, g * DH:(g + 1) * DH], oh[:, g, :], start=True, stop=True)
                last.then_inc(summed, 1)

            @block.vector
            def _(dve):
                dve.wait_ge(summed, 1)
                nc.vector.tensor_tensor(off[:, :, :], off[:, :, :], c.ps[0:DH, 0:3, 0:SKEW], ALU.add).then_inc(ready, 1)

            @block.sync
            def _(sp):
                sp.wait_ge(ready, 1)
                for g in range(3):
                    sp.dma_start(skewed[g], off[:, g, :].unsqueeze(1).to_broadcast([DH, P, SKEW])).then_inc(stored, 16)
                sp.wait_ge(stored, 48)

    for g, dil in enumerate(DIL):
        c.end_stage()
        with ExitStack() as tmp:
            dilated_group(c, w_in, xnT, ident, o, stat, skewed, g, dil, tmp)

    c.end_stage()
    lse = o[:, :, :, DH * DE:ROW]
    with nc.Block() as block:
        ln_ready, lse_ready, stored, back = (c.sem("dil_" + n) for n in ("ln", "lse", "stored", "back"))

        @block.scalar
        def _(act):
            nc.scalar.activation(stat[:, :, :, 1, :], stat[:, :, :, 1, :], ACT.Ln).then_inc(ln_ready, 1)

        @block.vector
        def _(dve):
            step = c.dve.on(dve)
            dve.wait_ge(ln_ready, 1)
            for g in range(3):
                for par in range(2):
                    step(nc.vector.tensor_tensor(lse[:, g].rearrange("p b (h r) -> p b r h", r=2)[:, :, par, :],
                                                 stat[:, g, :, 1, 2 * par:2 * par + 2], stat[:, g, :, 0, 2 * par:2 * par + 2], ALU.subtract))
            dve.nop().then_inc(lse_ready, 1)

        @block.sync
        def _(sp):
            sp.wait_ge(lse_ready, 1)
            for r in range(4):
                sp.dma_start(scratch[0].rearrange("(b l r) x -> r l b x", b=2, r=4)[r], o[:, 1, 2 * r:2 * r + 2, :]).then_inc(stored, 16)
            sp.dma_start(scratch[1].rearrange("(l a) x -> l a x", a=NB), o[:, 2, :, :]).then_inc(stored, 16)
            sp.wait_ge(stored, 80)
            for g in range(2):
                sp.dma_start(o[:, 1 + g, :, :], scratch[g].rearrange("(b p) x -> p b x", p=P)).then_inc(back, 16)
            sp.wait_ge(back, 32)

    with ExitStack() as tmp:
        top = c.sb("dil_top", [P, NB, DH], tmp)
        with nc.Block() as block:
            sub_ready, e_ready, y_ready, turned = (c.sem("dily_" + n) for n in ("sub", "exp", "y", "turned"))

            @block.vector
            def _(dve):
                step = c.dve.on(dve)
                step(nc.vector.tensor_tensor(top[:, :, :], lse[:, 0], lse[:, 1], ALU.max))
                step(nc.vector.tensor_tensor(top[:, :, :], top[:, :, :], lse[:, 2], ALU.max))
                for g in range(3):
                    step(nc.vector.tensor_tensor(lse[:, g], lse[:, g], top[:, :, :], ALU.subtract))
                dve.nop().then_inc(sub_ready, 1)
                dve.wait_ge(e_ready, 1)
                step(nc.vector.tensor_tensor(top[:, :, :], lse[:, 0], lse[:, 1], ALU.add))
                step(nc.vector.tensor_tensor(top[:, :, :], top[:, :, :], lse[:, 2], ALU.add))
                step(nc.vector.reciprocal(top[:, :, :], top[:, :, :]))
                for b in range(NB):
                    for g in range(3):
                        v = o[:, g, b, 0:DH * DE].rearrange("p (h e) -> p h e", h=DH)
                        step(nc.vector.tensor_tensor(v, v, lse[:, g, b, :].unsqueeze(2).to_broadcast([P, DH, DE]), ALU.mult))
                        if g:
                            step(nc.vector.tensor_tensor(o[:, 0, b, 0:DH * DE], o[:, 0, b, 0:DH * DE], o[:, g, b, 0:DH * DE], ALU.add))
                    v = o[:, 0, b, 0:DH * DE].rearrange("p (h e) -> p h e", h=DH)
                    step(nc.vector.tensor_tensor(v, v, top[:, b, :].unsqueeze(2).to_broadcast([P, DH, DE]), ALU.mult))
                    dve.nop().then_inc(y_ready, 1)

            @block.tensor
            def _(pe):
                for b in range(NB):
                    pe.wait_ge(y_ready, b + 1)
                    for m in range(2):
                        last = nc.tensor.transpose(c.ps[:, 2 * m + b // 4, (b % 4) * P:(b % 4 + 1) * P],
                                                   o[:, 0, b, m * P:(m + 1) * P], ident[:, :])
                last.then_inc(turned, 1)

            @block.scalar
            def _(act):
                step = c.act.on(act)
                act.wait_ge(sub_ready, 1)
                for g in range(3):
                    step(nc.scalar.activation(lse[:, g], lse[:, g], ACT.Exp))
                act.nop().then_inc(e_ready, 1)
                act.wait_ge(turned, 1)
                for m in range(2):
                    step(nc.scalar.copy(yT[:, Y_DIL + m, :], c.ps[:, 2 * m:2 * m + 2, :].rearrange("p b t -> p (b t)")))


def dilated_group(c, w_in, xnT, ident, o, stat, skewed, g, dil, tmp):
    nc = c.nc
    qk = c.sb("qk_dil", [P, 4, T], tmp)
    v = c.sb("v_dil", [P, NB, DH * DE], tmp)
    bias = c.sb("bias_dil", [P, 2, DH, P], tmp)
    copy_tiles(c, w_in, O_DIL + g * 256, 2, xnT, qk[:, 0:2, :])
    copy_tiles(c, w_in, O_DIL + 768 + g * 256, 2, xnT, qk[:, 2:4, :])

    def tokens(b):
        if dil == 1:
            return lambda ap: ap[:, b * P:(b + 1) * P], b > 0
        if dil == 4:
            at = b // 2 + BANK * (b % 2)
            return lambda ap: ap[:, at:at + BANK - 3:4], b % 2 > 0
        return lambda ap: ap[:, b:T - 7 + b:8], False

    cut = [tokens(b) for b in range(NB)]
    token_major(c, f"v_dil{g}", [(0, w_in[:, :, O_DIL + 1536 + g * 256:O_DIL + 1536 + (g + 1) * 256])], DH * DE, xnT,
                [lambda src, k, b=b: cut[b][0](src[:, k, :]) for b in range(NB)], lambda b: v[:, b, :])
    row = skewed.tensor
    pairs = []
    for m in range(DH):
        head = 2 * (m % 2) + m // 2
        at = (g * DH + head) * P * SKEW
        pairs += [(bias[:, 0, m, :], bass.AP(row, at + 127 + P, [[SKEW - 1, P], [1, P]])),
                  (bias[:, 1, m, :], bass.AP(row, at + 127, [[SKEW - 1, P], [1, P]]))]
    load_all(c, f"bias_loaded{g}", pairs)

    lg = c.sb("lg_dil", [P, 2, 2, DH * P], tmp)
    pt = c.sb("pt_dil", [P, 2, 2, DH * P], tmp)
    (sc_ready, sc_read, max_ready, exp_ready, t_ready, t_copied, pv_ready, o_ready, t2_copied) = (
        c.sem(f"d{g}_{n}") for n in ("scores", "scores_read", "max", "exp", "t", "t_dve", "pv", "o", "t_act"))
    with nc.Block() as block:
        @block.tensor
        def _(pe):
            def scores(b):
                if b:
                    pe.wait_ge(sc_read, b)
                mine, prev = cut[b]
                for part in range(1 + prev):
                    for h in range(DH):
                        r, t = slice(64 * (h % 2), 64 * (h % 2) + 64), h // 2
                        last = nc.tensor.matmul(c.ps[:, 2 * part + h % 2, t * P:(t + 1) * P], mine(qk[r, t, :]),
                                                cut[b - part][0](qk[r, 2 + t, :]), start=True, stop=True)
                last.then_inc(sc_ready, 1)
            scores(0)
            for b in range(NB):
                if b + 1 < NB:
                    scores(b + 1)
                prev = cut[b][1]
                pe.wait_ge(exp_ready, b + 1)
                if b:
                    pe.wait_ge(t_copied, b)
                    pe.wait_ge(t2_copied, b)
                for part in range(1 + prev):
                    for m in range(DH):
                        last = nc.tensor.transpose(c.ps[:, 4 + part, m * P:(m + 1) * P], lg[:, b % 2, part, m * P:(m + 1) * P], ident[:, :])
                last.then_inc(t_ready, 1)
                pe.wait_ge(t_copied, b + 1)
                pe.wait_ge(t2_copied, b + 1)
                if b >= 2:
                    pe.wait_ge(o_ready, b - 1)
                for m in range(DH):
                    h = 2 * (m % 2) + m // 2
                    for part in range(1 + prev):
                        last = nc.tensor.matmul(c.ps[:, 6 + b % 2, h * DE:(h + 1) * DE], pt[:, b % 2, part, m * P:(m + 1) * P],
                                                v[:, b - part, h * DE:(h + 1) * DE], start=(part == 0), stop=(part == prev))
                last.then_inc(pv_ready, 1)

        @block.vector
        def _(dve):
            step = c.dve.on(dve)

            def head_out(b):
                s = b % 2
                dve.wait_ge(pv_ready, b + 1)
                step(nc.vector.tensor_tensor(o[:, g, b, 0:DH * DE].rearrange("p (h r e) -> p r h e", r=2, e=DE),
                                             c.ps[:, 6 + s, 0:DH * DE].rearrange("p (h r e) -> p r h e", r=2, e=DE),
                                             stat[:, g, b, 2, :].rearrange("p (r h) -> p r h", r=2).unsqueeze(3).to_broadcast([P, 2, 2, DE]), ALU.mult))
                dve.nop().then_inc(o_ready, 1)
            for b in range(NB):
                s, parts = b % 2, 1 + cut[b][1]
                dve.wait_ge(sc_ready, b + 1)
                if b >= 2:
                    dve.wait_ge(t_ready, b - 1)
                for part in range(parts):
                    step(nc.vector.scalar_tensor_tensor(lg[:, s, part, :].rearrange("p (r x) -> p r x", r=2),
                                                        c.ps[:, 2 * part:2 * part + 2, 0:2 * P], 0.125,
                                                        bias[:, part].rearrange("p (r h) t -> p r (h t)", r=2), ALU.mult, ALU.add))
                dve.nop().then_inc(sc_read, 1)
                view = lg[:, s, 0:parts, :].rearrange("p a (m t) -> p m a t", m=DH)
                step(nc.vector.tensor_reduce(stat[:, g, b, 0, :], view, AX.XY, ALU.max))
                step(nc.vector.tensor_scalar(stat[:, g, b, 0, :], stat[:, g, b, 0, :], -1.0, None, ALU.mult))
                dve.nop().then_inc(max_ready, 1)
                dve.wait_ge(exp_ready, b + 1)
                step(nc.vector.reciprocal(stat[:, g, b, 2, :], stat[:, g, b, 1, :]))
                dve.wait_ge(t_ready, b + 1)
                if b >= 2:
                    dve.wait_ge(pv_ready, b - 1)
                step(nc.vector.tensor_copy(pt[:, s, 0, :], c.ps[:, 4, :]))
                dve.nop().then_inc(t_copied, 1)
                head_out(b)

        @block.scalar
        def _(act):
            step = c.act.on(act)
            for b in range(NB):
                s, parts = b % 2, 1 + cut[b][1]
                act.wait_ge(max_ready, b + 1)
                for m in range(DH):
                    e = lg[:, s, 0:parts, m * P:(m + 1) * P]
                    step(nc.scalar.activation(e, e, ACT.Exp, bias=stat[:, g, b, 0, m:m + 1], accum_out=stat[:, g, b, 1, m:m + 1]))
                act.nop().then_inc(exp_ready, 1)
                act.wait_ge(t_ready, b + 1)
                if b >= 2:
                    act.wait_ge(pv_ready, b - 1)
                if parts == 2:
                    step(nc.scalar.copy(pt[:, s, 1, :], c.ps[:, 5, :]))
                act.nop().then_inc(t2_copied, 1)


def stick_branch(c, io, w_in, xnT, yT, ones, s2):
    nc = c.nc
    H = 4
    qk = c.sb("qk_sb", [P, 2 * H, T], s2)
    v = c.sb("v_sb", [P, NB, H * SB_E], s2)
    copy_tiles(c, w_in, O_SB, H, xnT, qk[:, 0:H, :], scale=float(SB_E) ** -0.5)
    copy_tiles(c, w_in, O_SB + 512, H, xnT, qk[:, H:2 * H, :])
    token_major(c, "v_sb", [(0, w_in[:, :, O_SB + 1024:O_SB + 1536])], 512, xnT, plain_blocks(NB), lambda b: v[:, b, :])
    tri = c.sb("sb_tri", [P, 3, P], s2)
    load_all(c, "sb_tri_loaded", [(tri[:, :, :], c.io["k_stick"])])
    l, sp, dlt, acc, w = (c.sb("sb_" + n, [P, 2, BANK], s2) for n in ("l", "sp", "dlt", "acc", "w"))
    units = []
    for h in range(H):
        for half in range(2):
            kbs = list(range(4 * half + 3, -1, -1))
            units += [(h, half, kb, max(0, kb * P - half * BANK), n, len(kbs)) for n, kb in enumerate(kbs)]
    N = len(units)
    z_ready, l_ready, sp_ready, between, arg_ready, w_ready, pv_ready, y_ready, acc_zero = (
        c.sem("sb_" + n + "_done") for n in ("z", "l", "sp", "between", "arg", "w", "pv", "y", "zero"))

    def pair(u):
        return 2 * units[u][0] + units[u][1]

    with nc.Block() as block:
        @block.tensor
        def _(pe):
            def logits(u):
                h, half, kb, q0, n, _ = units[u]
                if u >= 2:
                    pe.wait_ge(sp_ready, u - 1)
                nc.tensor.matmul(c.ps[:, u % 2, q0:BANK], qk[:, H + h, kb * P:(kb + 1) * P],
                                 qk[:, h, half * BANK + q0:(half + 1) * BANK], start=True, stop=True).then_inc(z_ready, 1)

            def sums(u):
                h, half, kb, q0, n, _ = units[u]
                pe.wait_ge(sp_ready, u + 1)
                if u >= 2:
                    pe.wait_ge(arg_ready, u - 1)
                last = nc.tensor.matmul(c.ps[:, 2 + u % 2, q0:BANK], tri[:, 0, :], sp[:, u % 2, q0:BANK], start=True, stop=(n == 0))
                if n:
                    last = nc.tensor.matmul(c.ps[:, 2 + u % 2, q0:BANK], ones[:, :], acc[:, n % 2, q0:BANK], start=False, stop=True)
                last.then_inc(between, 1)

            def values(u):
                h, half, kb, q0, n, total = units[u]
                pe.wait_ge(w_ready, u + 1)
                if n == 0 and pair(u) >= 2:
                    pe.wait_ge(y_ready, pair(u) - 1)
                nc.tensor.matmul(c.ps[:, 4 + pair(u) % 2, q0:BANK], v[:, kb, h * SB_E:(h + 1) * SB_E], w[:, u % 2, q0:BANK],
                                 start=(n == 0), stop=(n == total - 1), skip_group_check=True).then_inc(pv_ready, 1)
            logits(0)
            for u in range(N + 1):
                if u + 1 < N:
                    logits(u + 1)
                if u < N:
                    sums(u)
                if u >= 1:
                    values(u - 1)

        @block.scalar
        def _(act):
            step = c.act.on(act)

            def soft(u):
                q0 = units[u][3]
                act.wait_ge(z_ready, u + 1)
                if u >= 2:
                    act.wait_ge(sp_ready, u - 1)
                t = l[:, u % 2, q0:BANK]
                step(nc.scalar.activation(t, c.ps[:, u % 2, q0:BANK], ACT.Abs))
                step(nc.scalar.activation(t, t, ACT.Exp, scale=-1.0))
                nc.scalar.activation(t, t, ACT.Ln, bias=1.0).then_inc(l_ready, 1)
            soft(0)
            for u in range(N):
                if u + 1 < N:
                    soft(u + 1)
                h, half, kb, q0, n, total = units[u]
                act.wait_ge(arg_ready, u + 1)
                if u >= 2:
                    act.wait_ge(pv_ready, u - 1)
                nc.scalar.activation(w[:, u % 2, q0:BANK], dlt[:, u % 2, q0:BANK], ACT.Exp).then_inc(w_ready, 1)
                if n == total - 1:
                    act.wait_ge(pv_ready, u + 1)
                    nc.scalar.copy(yT[:, Y_SB + h, half * BANK:(half + 1) * BANK], c.ps[:, 4 + pair(u) % 2, :]).then_inc(y_ready, 1)

        @block.vector
        def _(dve):
            step = c.dve.on(dve)

            def soft(u):
                h, half, kb, q0, n, total = units[u]
                s, q = u % 2, slice(q0, BANK)
                z, diag = c.ps[:, s, q], slice(q0, q0 + P)
                own = kb >= 4 * half
                dve.wait_ge(l_ready, u + 1)
                if u >= 2:
                    dve.wait_ge(between, u - 1)
                    dve.wait_ge(w_ready, u - 1)
                step(nc.vector.scalar_tensor_tensor(sp[:, s, q], z, 0.0, l[:, s, q], ALU.max, ALU.add))
                step(nc.vector.tensor_tensor(dlt[:, s, q], z, sp[:, s, q], ALU.subtract))
                if own:
                    step(nc.vector.tensor_tensor(sp[:, s, diag], sp[:, s, diag], tri[:, 1, :], ALU.mult))
                    step(nc.vector.tensor_tensor(dlt[:, s, diag], dlt[:, s, diag], tri[:, 2, :], ALU.add))
                if n == 0:
                    if u >= 1:
                        dve.wait_ge(between, u)
                    step(nc.vector.memset(acc[:, :, :], 0.0))
                if n + 1 < total:
                    if u >= 1:
                        dve.wait_ge(between, u)
                    step(nc.vector.tensor_tensor(acc[:, (n + 1) % 2, q], acc[:, n % 2, q], sp[:, s, q], ALU.add))
                dve.nop().then_inc(sp_ready, 1)
            soft(0)
            for u in range(N):
                if u + 1 < N:
                    soft(u + 1)
                q = slice(units[u][3], BANK)
                dve.wait_ge(between, u + 1)
                nc.vector.tensor_tensor(dlt[:, u % 2, q], dlt[:, u % 2, q], c.ps[:, 2 + u % 2, q], ALU.subtract).then_inc(arg_ready, 1)


def s5_branch(c, io, w_in, xnT, yT, ident, s2):
    nc = c.nc
    uT = c.sb("uT", [P, 4, T], s2)
    copy_tiles(c, w_in, O_S5, 4, xnT, uT)
    TWO_PI = float(2 * np.pi)
    C1 = 6.28125
    C2 = TWO_PI - C1
    SAFE = TWO_PI * (1 - 2.0 ** -21)
    small = c.sb("s5_small", [P, 14, QT], s2)
    re, im, dt, r, th, n_, ab, cr, ci, t0, t1, frac, f32_, lbr = (small[:, j, :] for j in range(14))
    bt = c.sb("s5_b", [P, 2, QT, SC], s2)
    bb = c.sb("s5_bb", [P, 2, QT, SC], s2)
    cc = c.sb("s5_c", [P, 2, 4, 64], s2)
    coarse, fine, rnd = (c.sb("s5_" + n, [P, QT, 32], s2) for n in ("coarse", "fine", "rnd"))
    ramp = c.sb("s5_ramp", [P, 32], s2)
    masks = c.sb("s5_masks", [P, 4, 10], s2)
    dsk = c.sb("s5_d", [P, 4], s2)
    half_pi = c.sb("half_pi", [P, 1], s2)
    gl = lambda ap: ap.rearrange("(q g) s -> g s q", g=2)
    pairs = []
    for gg in range(2):
        rows = slice(64 * gg, 64 * gg + 64)
        pairs += [(re[rows], gl(io["s5_a_re_2"][0])[gg]), (im[rows], gl(io["s5_a_im_2"][0])[gg]),
                  (dt[rows], bass.AP(io["s5_log_dt_2"].tensor, gg, [[0, 64], [2, QT]]))]
        pairs += [(bt[rows, j, :, :], io[n][0].rearrange("(q g) s ch -> g s q ch", g=2)[gg]) for j, n in enumerate(("s5_b_re_2", "s5_b_im_2"))]
    pairs += [(cc[:, j, :, :], io[n][0].rearrange("(y g) ch s -> (g ch) y s", y=4)) for j, n in enumerate(("s5_c_re_2", "s5_c_im_2"))]
    pairs += [(ramp[:, :], io["k_ramp"]), (masks[:, :, :], io["k_s5mask"]), (dsk[:, :], col(io["s5_d_2"][0]))]
    load_all(c, "s5_loaded", pairs)

    with nc.Block() as block:
        a_ready, v_ready = c.sem("s5_prep_act"), c.sem("s5_prep_dve")

        @block.scalar
        def _(act):
            step = c.act.on(act)
            step(nc.scalar.activation(dt, dt, ACT.Exp))
            act.nop().then_inc(a_ready, 1)
            act.wait_ge(v_ready, 1)
            step(nc.scalar.activation(r, t0, ACT.Exp))
            step(nc.scalar.activation(ab, th, ACT.Abs))
            step(nc.scalar.activation(t1, th, ACT.Sin))
            step(nc.scalar.activation(lbr, ab, ACT.Sin, scale=-1.0, bias=half_pi[:, 0:1]))
            act.nop().then_inc(a_ready, 1)

        @block.vector
        def _(dve):
            step = c.dve.on(dve)
            tt = lambda out, a, b, op: step(nc.vector.tensor_tensor(out, a, b, op))
            ts = lambda out, a, x, y, op0, op1=ALU.bypass: step(nc.vector.tensor_scalar(out, a, x, y, op0, op1))
            step(nc.vector.memset(half_pi[:, :], float(np.pi / 2)))
            dve.wait_ge(a_ready, 1)
            tt(t0, re, dt, ALU.mult)
            tt(th, im, dt, ALU.mult)
            ts(n_, th, 1 / TWO_PI, ROUND, ALU.mult, ALU.add)
            ts(n_, n_, ROUND, None, ALU.subtract)
            step(nc.vector.scalar_tensor_tensor(th, n_, -C1, th, ALU.mult, ALU.add))
            step(nc.vector.scalar_tensor_tensor(th, n_, -C2, th, ALU.mult, ALU.add))
            ts(th, th, float(np.float32(3.1415925)), float(np.float32(-3.1415925)), ALU.min, ALU.max)
            dve.nop().then_inc(v_ready, 1)
            ts(frac, th, 1 / TWO_PI, None, ALU.mult)
            ts(f32_, frac, 32.0, None, ALU.mult)
            ts(n_, f32_, ROUND, None, ALU.add)
            ts(n_, n_, ROUND, None, ALU.subtract)
            tt(f32_, f32_, n_, ALU.subtract)
            for dst, src in ((coarse, f32_), (fine, frac)):
                tt(dst[:, :, :], src.unsqueeze(2).to_broadcast([P, QT, 32]), ramp[:, :].unsqueeze(1).to_broadcast([P, QT, 32]), ALU.mult)
                ts(rnd[:, :, :], dst[:, :, :], ROUND, None, ALU.add)
                ts(rnd[:, :, :], rnd[:, :, :], ROUND, None, ALU.subtract)
                tt(dst[:, :, :], dst[:, :, :], rnd[:, :, :], ALU.subtract)
            dve.wait_ge(a_ready, 2)
            tt(lbr, lbr, r, ALU.mult)
            ts(lbr, lbr, -1.0, None, ALU.add)
            tt(t1, t1, r, ALU.mult)
            tt(cr, lbr, re, ALU.mult)
            tt(t0, t1, im, ALU.mult)
            tt(cr, cr, t0, ALU.add)
            tt(ci, t1, re, ALU.mult)
            tt(t0, lbr, im, ALU.mult)
            tt(ci, ci, t0, ALU.subtract)
            tt(t0, re, re, ALU.mult)
            tt(t1, im, im, ALU.mult)
            tt(t0, t0, t1, ALU.add)
            step(nc.vector.reciprocal(t0, t0))
            tt(cr, cr, t0, ALU.mult)
            tt(ci, ci, t0, ALU.mult)
            wide = lambda a: a.unsqueeze(2).to_broadcast([P, QT, SC])
            tt(bb[:, 0], bt[:, 0], wide(cr), ALU.mult)
            tt(bb[:, 1], bt[:, 1], wide(cr), ALU.mult)
            tt(bt[:, 0], bt[:, 0], wide(ci), ALU.mult)
            tt(bt[:, 1], bt[:, 1], wide(ci), ALU.mult)
            tt(bb[:, 0], bb[:, 0], bt[:, 1], ALU.subtract)
            tt(bb[:, 1], bb[:, 1], bt[:, 0], ALU.add)
            ts(cc[:, 1], cc[:, 1], -1.0, None, ALU.mult)

    yg = c.sb("s5_y", [P, 4, T], s2)
    with ExitStack() as tmp:
        padded = c.sb("s5_pad", [P, 4, P], tmp)
        mats = c.sb("s5_mats", [P, 2, 4, P], tmp)
        cs = yT[:, Y_S5:Y_S5 + 2, :]
        g = c.sb("s5_g", [P, 2, T], tmp)
        hh = yT[:, Y_S5 + 2:Y_S5 + 4, :]
        x1 = c.sb("s5_x1", [P, T], tmp)
        x2 = c.sb("s5_x2", [P, T], tmp)
        y1 = c.sb("s5_y1", [P, T], tmp)
        pads, turned, mats_ready, bu_ready, ph_ready, cs_ready, g_ready, h_ready, y_sum, y_out, bu_read, g_read = (
            c.sem("s5_" + n) for n in ("pads", "turned", "mats", "bu", "ph", "cs", "g", "h", "ysum", "yout", "bu_read", "g_read"))
        re_ps = c.ps[:, 0:2, :].rearrange("p b t -> p (b t)")
        im_ps = c.ps[:, 2:4, :].rearrange("p b t -> p (b t)")
        with nc.Block() as block:
            @block.tensor
            def _(pe):
                for q in range(QT):
                    pe.wait_ge(pads, q + 1)
                    if q:
                        pe.wait_ge(mats_ready, q)
                    for j in range(4):
                        last = nc.tensor.transpose(c.ps[:, 6, j * P:(j + 1) * P], padded[:, j, :], ident[:, :])
                    last.then_inc(turned, 1)
                    pe.wait_ge(mats_ready, q + 1)
                    if q:
                        pe.wait_ge(bu_read, q)
                    for j in range(2):
                        for n in range(2):
                            last = nc.tensor.matmul(c.ps[:, 2 * j + n, :], mats[:, q % 2, j, :], uT[:, q // 4, n * BANK:(n + 1) * BANK],
                                                    start=True, stop=True)
                    last.then_inc(bu_ready, 1)
                    pe.wait_ge(h_ready, q + 1)
                    if q % 4 == 0 and q:
                        pe.wait_ge(y_out, q // 4)
                    for n in range(2):
                        for j in range(2):
                            last = nc.tensor.matmul(c.ps[:, 4 + n, :], mats[:, q % 2, 2 + j, :], hh[:, j, n * BANK:(n + 1) * BANK],
                                                    start=(q % 4 == 0 and j == 0), stop=(q % 4 == 3 and j == 1))
                    last.then_inc(y_sum, 1)

            @block.gpsimd
            def _(pool):
                step = c.pool.on(pool)
                tt = lambda out, a, b, op: step(nc.gpsimd.tensor_tensor(out, a, b, op))
                for q in range(QT):
                    if q:
                        pool.wait_ge(turned, q)
                    for j in range(2):
                        tt(padded[:, j, :].rearrange("p (g ch) -> p g ch", g=8), bb[:, j, q, :].unsqueeze(1).to_broadcast([P, 8, SC]),
                           masks[:, q % 4, 0:8].unsqueeze(2).to_broadcast([P, 8, SC]), ALU.mult)
                        tt(padded[:, 2 + j, :].rearrange("p (g s) -> p g s", g=2), cc[:, j, q // 4, :].unsqueeze(1).to_broadcast([P, 2, 64]),
                           masks[:, q % 4, 8:10].unsqueeze(2).to_broadcast([P, 2, 64]), ALU.mult)
                    pool.nop().then_inc(pads, 1)
                    pool.wait_ge(g_ready, q + 1)
                    if q:
                        pool.wait_ge(y_sum, q)
                    tt(hh[:, 0, :], g[:, 0, :], cs[:, 0, :], ALU.mult)
                    tt(y1[:, :], g[:, 1, :], cs[:, 1, :], ALU.mult)
                    tt(hh[:, 0, :], hh[:, 0, :], y1[:, :], ALU.subtract)
                    tt(hh[:, 1, :], g[:, 0, :], cs[:, 1, :], ALU.mult)
                    tt(y1[:, :], g[:, 1, :], cs[:, 0, :], ALU.mult)
                    tt(hh[:, 1, :], hh[:, 1, :], y1[:, :], ALU.add)
                    pool.nop().then_inc(h_ready, 1)

            @block.vector
            def _(dve):
                step = c.dve.on(dve)
                tt = lambda out, a, b, op: step(nc.vector.tensor_tensor(out, a, b, op))
                for q in range(QT):
                    if q:
                        dve.wait_ge(h_ready, q)
                    ph = cs[:, 0, :]
                    tt(ph.rearrange("p (a b) -> p a b", b=32), coarse[:, q, :].unsqueeze(2).to_broadcast([P, 32, 32]),
                       fine[:, q, :].unsqueeze(1).to_broadcast([P, 32, 32]), ALU.add)
                    step(nc.vector.tensor_scalar(x1[:, :], ph, ROUND, None, ALU.add))
                    step(nc.vector.tensor_scalar(x1[:, :], x1[:, :], ROUND, None, ALU.subtract))
                    tt(ph, ph, x1[:, :], ALU.subtract)
                    dve.nop().then_inc(ph_ready, 1)
                    dve.wait_ge(bu_ready, q + 1)
                    dve.wait_ge(cs_ready, q + 1)
                    tt(x1[:, :], re_ps, cs[:, 0, :], ALU.mult)
                    tt(x2[:, :], im_ps, cs[:, 1, :], ALU.mult)
                    tt(x1[:, :], x1[:, :], x2[:, :], ALU.add)
                    step(nc.vector.tensor_tensor_scan(g[:, 0, :], r[:, q:q + 1].to_broadcast([P, T]), x1[:, :], 0.0, ALU.mult, ALU.add))
                    tt(x1[:, :], im_ps, cs[:, 0, :], ALU.mult)
                    tt(x2[:, :], re_ps, cs[:, 1, :], ALU.mult)
                    dve.nop().then_inc(bu_read, 1)
                    tt(x1[:, :], x1[:, :], x2[:, :], ALU.subtract)
                    step(nc.vector.tensor_tensor_scan(g[:, 1, :], r[:, q:q + 1].to_broadcast([P, T]), x1[:, :], 0.0, ALU.mult, ALU.add))
                    dve.nop().then_inc(g_ready, 1)
                    if q % 4 == 3:
                        m = q // 4
                        dve.wait_ge(y_sum, q + 1)
                        step(nc.vector.scalar_tensor_tensor(yg[:, m, :], uT[:, m, :], dsk[:, m:m + 1],
                                                            c.ps[:, 4:6, :].rearrange("p b t -> p (b t)"), ALU.mult, ALU.add))
                        dve.nop().then_inc(y_out, 1)

            @block.scalar
            def _(act):
                step = c.act.on(act)
                for q in range(QT):
                    act.wait_ge(turned, q + 1)
                    if q >= 2:
                        act.wait_ge(y_sum, q - 1)
                    step(nc.scalar.copy(mats[:, q % 2].rearrange("p j x -> p (j x)"), c.ps[:, 6, :]))
                    act.nop().then_inc(mats_ready, 1)
                    act.wait_ge(ph_ready, q + 1)
                    step(nc.scalar.activation(cs[:, 1, :], cs[:, 0, :], ACT.Sin, scale=SAFE))
                    step(nc.scalar.activation(cs[:, 0, :], cs[:, 0, :], ACT.Abs))
                    step(nc.scalar.activation(cs[:, 0, :], cs[:, 0, :], ACT.Sin, scale=-TWO_PI, bias=half_pi[:, 0:1]))
                    act.nop().then_inc(cs_ready, 1)
    with nc.Block() as block:
        @block.scalar
        def _(act):
            step = c.act.on(act)
            step(nc.scalar.activation(yg[:, :, :], yg[:, :, :], ACT.Gelu_apprx_tanh))
    with ExitStack() as tmp:
        wbuf = c.sb("wbuf", [P, 2, 2, 4, P], tmp)
        sig = c.sb("s5_sig", [P, 2, T], tmp)
        sig_ready = c.sem("s5_sig_ready")
        wv = io["s5_w_glu_2"][0].rearrange("(k p) n -> p k n", p=P)

        def act_part(eng, tile, s, i):
            c.act(nc.scalar.activation(sig[:, s, :], c.ps[:, 4 * s + 2:4 * s + 4, :].rearrange("p b t -> p (b t)"), ACT.Sigmoid))
            eng.nop().then_inc(sig_ready, 1)

        def dve_part(eng, tile, s, i):
            eng.wait_ge(sig_ready, i * 2 + s + 1)
            c.dve(nc.vector.tensor_tensor(yT[:, bass.ds(tile + Y_S5, 1), :].rearrange("p o t -> p (o t)"),
                                          c.ps[:, 4 * s:4 * s + 2, :].rearrange("p b t -> p (b t)"), sig[:, s, :], ALU.mult))
        project(c, 4, 2, 4, lambda part, t: wv[:, :, bass.ds(t * P + part * 512, P)], lambda part: yg, HALVES,
                lambda s, part, n: c.ps[:, 4 * s + 2 * part + n, :], act_part, dve_part, 1, 1, wbuf)


def merge(c, io, xnT, yT, merged, s2):
    nc = c.nc
    wg = c.sb("w_gate", [P, 2, DK, P], s2)
    wb = c.sb("w_branch", [P, 2, 4, P], s2)
    sig = c.sb("sig", [P, 2, T], s2)
    first = [sum(BRANCH_TILES[:b]) for b in range(4)]
    gate = io["w_gate_2"][0].rearrange("b (k p) n -> p b k n", p=P)
    wide = io["w_branch_2"][0].rearrange("(k p) n -> p k n", p=P)
    loaded = [c.sem(f"mg_loaded{s}") for s in range(2)]
    summed = [c.sem(f"mg_sum{s}") for s in range(2)]
    sig_ready = [c.sem(f"mg_sig{s}") for s in range(2)]
    used = [c.sem(f"mg_used{s}") for s in range(2)]
    flat = lambda b: c.ps[:, b:b + 2, :].rearrange("p b t -> p (b t)")
    with nc.Block() as block:
        @block.sync
        def _(sp):
            with sp.Fori(0, DK) as m:
                for b in range(4):
                    s, done = b % 2, m * 2 + b // 2
                    sp.wait_ge(summed[s], done + 1)
                    sp.dma_start(wg[:, s], gate[:, b, :, bass.ds(m * P, P)]).then_inc(loaded[s], 16)
                    n = BRANCH_TILES[b]
                    sp.dma_start(wb[:, s, 0:n], wide[:, first[b]:first[b] + n, bass.ds(m * P, P)]).then_inc(loaded[s], 16)

        @block.tensor
        def _(pe):
            for s in range(2):
                pe.nop().then_inc(summed[s], 1)
            with pe.Fori(0, DK) as m:
                for b in range(4):
                    s, done = b % 2, m * 2 + b // 2
                    pe.wait_ge(loaded[s], (done + 1) * 32)
                    pe.wait_ge(used[s], done + 1)
                    for n in range(2):
                        cols = slice(n * BANK, (n + 1) * BANK)
                        for k in range(DK):
                            nc.tensor.matmul(c.ps[:, 4 * s + n, :], wg[:, s, k, :], xnT[:, k, cols], start=(k == 0), stop=(k == DK - 1))
                    for n in range(2):
                        cols = slice(n * BANK, (n + 1) * BANK)
                        for k in range(BRANCH_TILES[b]):
                            last = nc.tensor.matmul(c.ps[:, 4 * s + 2 + n, :], wb[:, s, k, :], yT[:, first[b] + k, cols],
                                                    start=(k == 0), stop=(k == BRANCH_TILES[b] - 1))
                    last.then_inc(summed[s], 1)

        @block.scalar
        def _(act):
            with act.Fori(0, DK) as m:
                for b in range(4):
                    s, done = b % 2, m * 2 + b // 2
                    act.wait_ge(summed[s], done + 2)
                    act.wait_ge(used[s], done + 1)
                    nc.scalar.activation(sig[:, s, :], flat(4 * s), ACT.Sigmoid).then_inc(sig_ready[s], 1)

        @block.vector
        def _(dve):
            def tile(m):
                dst = merged[:, bass.ds(m, 1), :].rearrange("p o t -> p (o t)")
                for b in range(4):
                    s, done = b % 2, m * 2 + b // 2
                    dve.wait_ge(sig_ready[s], done + 1)
                    if b == 0:
                        c.dve(nc.vector.tensor_tensor(dst, flat(4 * s + 2), sig[:, s, :], ALU.mult))
                    else:
                        c.dve(nc.vector.tensor_tensor(sig[:, s, :], flat(4 * s + 2), sig[:, s, :], ALU.mult))
                        c.dve(nc.vector.tensor_tensor(dst, dst, sig[:, s, :], ALU.add))
                    dve.nop().then_inc(used[s], 1)
            for s in range(2):
                dve.nop().then_inc(used[s], 1)
            c.dve.on(dve).loop(DK, 7, tile)


def shape_constants():
    f = np.float32
    sel = np.zeros((MH, MH, P), f)
    for h in range(MH):
        sel[h, h] = 1
    first = np.arange(TA) % P == 0
    reset = np.stack([np.where(first, 0, 1), np.where(first, NEG, 0)]).astype(f)
    j, i = np.arange(NBA)[:, None], np.arange(NBA)[None]
    later = np.stack([(i - 1 > j) * 1.0, (i > 0) * np.ones((NBA, 1))]).astype(f)
    s, t = np.arange(P)[:, None], np.arange(P)[None]
    tri = np.stack([np.where(s <= t, 0, NEG), np.where(s >= t, 0, NEG)], 1).astype(f)
    q, k = np.arange(P)[:, None], np.arange(3 * P)[None]
    band = np.where((k >= q) & (k <= q + 2 * P), 0, NEG).astype(f)
    e = np.arange(P) % 64
    pairs = 16
    inv = (f(10000.0) ** (-np.arange(pairs, dtype=f) / f(pairs))).astype(f)
    tok = np.arange(T)
    pos = np.where((e < 32)[:, None], (tok // 64)[None], (tok % 64)[None]).astype(f)
    ang = (pos * inv[e % pairs][:, None]).astype(f)
    rope = np.stack([np.cos(ang), np.sin(ang)], 1).astype(f)
    swap = np.zeros((P, P), f)
    for m in range(P):
        if (m % 32) < 16:
            swap[m + 16, m] = -1
        else:
            swap[m - 16, m] = 1
    return {"k_ident": np.eye(P, dtype=f), "k_ones": np.ones((P, P), f), "k_sel": sel,
            "k_reset": np.broadcast_to(reset, (MH, 2, TA)).copy(),
            "k_later": np.broadcast_to(later, (MH, 2, NBA, NBA)).copy(), "k_tri": tri, "k_band": band,
            "k_rope": rope, "k_swap": swap, **second_constants()}


def second_constants():
    f = np.float32
    pool = np.zeros((P, len(POOLS), 3, P), f)
    for g, w in enumerate(POOLS):
        for t in range(P):
            lo = max(t + 1 - w, 0)
            pool[lo:t + 1, g, 0, t] = f(1) / f(t + 1 - lo)
            pool[lo:t + 1, g, 1, t] = f(1) / f(w)
            if t + 1 - w < 0:
                pool[P + t + 1 - w:P, g, 2, t] = f(1) / f(w)
            pool[t, g, 0:2, t] -= 1
    x = np.arange(SKEW)
    dist = 255 - x
    valid = (dist >= 0) & (dist <= P)
    onehot, skewmask = np.zeros((32, 3, SKEW), f), np.zeros((DH, 3, SKEW), f)
    for g, dil in enumerate(DIL):
        ok = valid if dil < 16 else valid & (dist % 2 == 0) & (dist < P)
        skewmask[:, g] = np.where(ok, 0, NEG)
        d = np.clip(dist, 0, P) * (dil if dil < 16 else 8)
        large = 16 + (np.log(np.maximum(d, 1).astype(f) / f(16)) / f(np.log(2048 / 16)) * f(16)).astype(np.int32)
        bucket = np.where(d < 16, d, np.minimum(large, 31))
        onehot[bucket, g, x] = ok
    a, b = np.arange(P)[:, None], np.arange(P)[None]
    stick = np.stack([(a > b) * 1.0, (a < b) * 1.0, np.where(a < b, 0, NEG)], 1).astype(f)
    m = np.zeros((P, 4, 10), f)
    p = np.arange(P)
    for q in range(4):
        m[p, q, 2 * q + p // 64] = 1
        for gg in range(2):
            m[p // SC == 2 * q + gg, q, 8 + gg] = 1
    return {"k_pool": pool, "k_onehot": onehot, "k_skewmask": skewmask, "k_stick": stick,
            "k_ramp": np.broadcast_to(np.arange(32, dtype=f), (P, 32)).copy(), "k_s5mask": m}


_INS = ["x", "c", "ctx", "c_ctx", "w_ada", "b_ada", "norm_mix", "norm_ffn", "w_in", "gate_b", "qk_conv_w",
        "qk_conv_b", "mlstm_norm", "attn_sink", "w_out", "w_up", "ffn_conv_w", "ffn_conv_b", "w_down",
        "final_norm", "attn_norm_g_2", "w_in_2", "pool_w_2", "pool_scale_2", "rel_bias_2", "s5_a_re_2",
        "s5_a_im_2", "s5_log_dt_2", "s5_b_re_2", "s5_b_im_2", "s5_c_re_2", "s5_c_im_2", "s5_d_2",
        "s5_w_glu_2", "w_branch_2", "w_gate_2", "w_out_2", "ffn_norm_g_2", "w_up_2", "w_down_2",
        "final_norm_g_2"]


def launch_arrays(inputs):
    arrays = {f"in_{n}": np.ascontiguousarray(inputs[n]) for n in _INS}
    arrays.update({f"in_{n}": a for n, a in shape_constants().items()})
    return arrays


def declare_and_build(nc, arrays):
    io = {n[3:]: nc.dram_tensor(n, a.shape, mybir.dt.from_np(a.dtype), kind="ExternalInput").ap()
          for n, a in arrays.items()}
    io["out"] = nc.dram_tensor("out_0", (1, T, D), F32, kind="ExternalOutput").ap()
    build(nc, io)


def kernel(**inputs):
    import concourse.bacc as _bacc
    from concourse.bass_utils import run_bass_kernel_spmd as _run

    nc = _bacc.Bacc("TRN2", target_bir_lowering=False, num_devices=1)
    arrays = launch_arrays(inputs)
    declare_and_build(nc, arrays)
    r = _run(nc, [arrays], core_ids=[0])
    return r.results[0]["out_0"]
```

```python
from contextlib import ExitStack

import numpy as np

import concourse.bass as bass
from concourse import mybir

F32 = mybir.dt.float32
F32R = mybir.dt.float32r
ALU = mybir.AluOpType
ACT = mybir.ActivationFunctionType
AX = mybir.AxisListType

P = 128
D = 1024
DK = D // P
T = 1024
TC = 256
TA = T + TC
NB = T // P
NBA = TA // P
BANK = 512
EPS = 1e-6
NEG = -1e30
FF = 2816
FK = FF // P
MH, AH, KVH, GRP = 4, 8, 2, 4
OFF_QK, OFF_V, OFF_O, OFF_G, OFF_QA, OFF_KA, OFF_VA = 0, 1024, 1536, 2048, 2064, 2576, 2704
NG = 16
HALVES = [(0, BANK), (BANK, BANK)]
XCHUNKS = HALVES + [(T, TC)]


class Count:

    def __init__(self, sem):
        self.sem, self.base = sem, 0


class Chain:

    def __init__(self, sem):
        self.sem, self.eng, self.base, self.n = sem, None, 0, 0

    def on(self, eng):
        self.eng = eng
        return self

    def __call__(self, ins):
        self.n += 1
        ins.then_inc(self.sem, 1)
        self.eng.wait_ge(self.sem, self.base + self.n)

    def take_waits(self):
        self.n += 1
        self.eng.nop().then_inc(self.sem, 1)

    def loop(self, count, per, body):
        start = self.base + self.n
        with self.eng.Fori(0, count) as i:
            self.base, self.n = start + i * per, 0
            body(i)
            assert self.n == per, (self.n, per)
        self.base, self.n = start + count * per, 0


class Core:

    def __init__(self, nc, ctx):
        self.nc, self.ctx, self.names, self.lasting = nc, ctx, {}, True
        self.dve, self.act, self.pool, self.pe = (Chain(self.sem(n)) for n in
                                        ("dve_steps", "act_steps", "pool_steps", "pe_steps"))
        self.ps = ctx.enter_context(nc.psum_tensor("ps", [P, 8, BANK], F32))
        self.w_loaded = [Count(self.sem(f"w_loaded{s}")) for s in range(2)]
        self.w_split = [Count(self.sem(f"w_split{s}")) for s in range(2)]
        self.split_used = Count(self.sem("split_used"))
        self.w_used = [Count(self.sem(f"w_used{s}")) for s in range(2)]
        self.acc_ready = [Count(self.sem(f"acc_ready{s}")) for s in range(2)]
        self.act_emptied = [Count(self.sem(f"act_emptied{s}")) for s in range(2)]
        self.dve_emptied = [Count(self.sem(f"dve_emptied{s}")) for s in range(2)]

        self.lasting, self.stage_sems = False, []

    def sem(self, name):
        sem = self.nc.alloc_semaphore(name=name)
        if not self.lasting:
            self.stage_sems.append(sem)
        return sem

    def end_stage(self):
        self.nc.clear_and_free_semaphores(self.stage_sems)
        self.nc.all_engine_barrier()
        self.stage_sems = []

    def sb(self, name, shape, ctx=None, dtype=F32):
        self.names[name] = self.names.get(name, 0) + 1
        if self.names[name] > 1:
            name = f"{name}_{self.names[name]}"
        return (ctx or self.ctx).enter_context(self.nc.sbuf_tensor(name, shape, dtype))


def project(c, tiles, parts, k_tiles, w_cols, rhs, chunks, bank_of, act_part, dve_part, act_steps,
            dve_steps, wbuf, w_parts=None):
    nc = c.nc
    half = tiles // 2
    n_loads = parts

    def split_slot(part, s, i):
        return (part, i * 2 + s) if parts == 2 else (s, i)

    with nc.Block() as block:

        def both_slots(eng, body):
            with eng.Fori(0, half) as i:
                for s in range(2):
                    body(i * 2 + s, s, i)

        @block.sync
        def _(sp):
            def load(tile, s, i):
                used = c.acc_ready[s] if w_parts is None else c.w_used[s]
                sp.wait_ge(used.sem, used.base + i)
                for part in range(parts):
                    sp.dma_start(wbuf[:, s, part, 0:k_tiles, :], w_cols(part, tile)).then_inc(c.w_loaded[s].sem, 16)
            both_slots(sp, load)

        @block.tensor
        def _(pe):
            def products(tile, s, i):
                pe.wait_ge(c.act_emptied[s].sem, c.act_emptied[s].base + i)
                pe.wait_ge(c.dve_emptied[s].sem, c.dve_emptied[s].base + i)
                if w_parts is None:
                    pe.wait_ge(c.w_loaded[s].sem, c.w_loaded[s].base + (i + 1) * (16 * n_loads))
                for part in range(parts):
                    if w_parts is None:
                        passes = [(wbuf[:, s, part], rhs(part))]
                    else:
                        q, uses = split_slot(part, s, i)
                        pe.wait_ge(c.w_split[q].sem, c.w_split[q].base + uses + 1)
                        (w_hi, w_lo), (hi, lo) = w_parts, rhs(part)
                        passes = [(w_hi[:, q], hi), (w_hi[:, q], lo), (w_lo[:, q], hi)]
                    for n, (at, size) in enumerate(chunks):
                        for k in range(k_tiles):
                            for j, (w, r) in enumerate(passes):
                                last = nc.tensor.matmul(bank_of(s, part, n)[:, 0:size], w[:, k, :], r[:, k, at:at + size],
                                                        start=(k == 0 and j == 0),
                                                        stop=(k == k_tiles - 1 and j == len(passes) - 1))
                    if part == parts - 1:
                        last.then_inc(c.acc_ready[s].sem, 1)
                    elif w_parts is not None:
                        last.then_inc(c.split_used.sem, 1)
            both_slots(pe, products)

        if w_parts is not None:
            @block.gpsimd
            def _(pool):
                def split_weights(i):
                    for s in range(2):
                        pool.wait_ge(c.w_loaded[s].sem, c.w_loaded[s].base + (i + 1) * (16 * n_loads))
                        for part in range(parts):
                            q, uses = split_slot(part, s, i)
                            if parts == 1:
                                pool.wait_ge(c.acc_ready[s].sem, c.acc_ready[s].base + i)
                            elif part == 0:
                                pool.wait_ge(c.split_used.sem, c.split_used.base + uses)
                            else:
                                pool.wait_ge(c.acc_ready[1 - s].sem, c.acc_ready[1 - s].base + i + s)
                            w, hi, lo = wbuf[:, s, part, 0:k_tiles, :], w_parts[0][:, q, 0:k_tiles, :], w_parts[1][:, q, 0:k_tiles, :]
                            c.pool.take_waits()
                            c.pool(nc.gpsimd.tensor_copy(hi, w))
                            c.pool(nc.gpsimd.tensor_tensor(lo, w, hi.bitcast(F32), ALU.subtract))
                            pool.nop().then_inc(c.w_split[q].sem, 1)
                        pool.nop().then_inc(c.w_used[s].sem, 1)
                c.pool.on(pool).loop(half, 6 * parts, split_weights)

        @block.scalar
        def _(eng):
            def empty(i):
                for s in range(2):
                    eng.wait_ge(c.acc_ready[s].sem, c.acc_ready[s].base + i + 1)
                    act_part(eng, i * 2 + s, s, i)
                    eng.nop().then_inc(c.act_emptied[s].sem, 1)
            c.act.on(eng).loop(half, 2 * act_steps, empty)

        @block.vector
        def _(eng):
            def empty(i):
                for s in range(2):
                    eng.wait_ge(c.acc_ready[s].sem, c.acc_ready[s].base + i + 1)
                    dve_part(eng, i * 2 + s, s, i)
                    eng.nop().then_inc(c.dve_emptied[s].sem, 1)
            c.dve.on(eng).loop(half, 2 * dve_steps, empty)

    for s in range(2):
        c.w_loaded[s].base += half * 16 * n_loads
        if w_parts is not None:
            c.w_used[s].base += half
            c.w_split[s].base += half * parts
        c.acc_ready[s].base += half
        c.act_emptied[s].base += half
        c.dve_emptied[s].base += half
    if w_parts is not None and parts == 2:
        c.split_used.base += tiles


def modulation(c, io, ada, ident):
    nc = c.nc
    with ExitStack() as tmp:
        cc = c.sb("cc", [P, DK, 2], tmp)
        sc = c.sb("sc", [P, DK, 2], tmp)
        b = c.sb("b_ada_t", [P, 48], tmp)
        wa = c.sb("wa", [P, 3, DK, BANK], tmp)
        rows = c.sb("ada_rows", [2, 12, BANK], tmp)
        c_loaded, sc_ready, ada_sum = c.sem("c_loaded"), c.sem("sc_ready"), c.sem("ada_sum")
        wa_loaded = [c.sem(f"wa_loaded{s}") for s in range(3)]
        row_copied, turned = c.sem("ada_row_copied"), c.sem("ada_turned")
        wa_used = [c.sem(f"wa_used{s}") for s in range(3)]
        acc = c.ps[:, 0, 0:96].rearrange("p (m j) -> p m j", j=2)
        w = io["w_ada"][0].rearrange("(k p) n -> p k n", p=P)
        with nc.Block() as block:
            @block.sync
            def _(sp):
                with nc.allow_non_contiguous_dma("small"):
                    sp.dma_start(cc[:, :, 0], io["c"].rearrange("o (k p) -> p (o k)", p=P)).then_inc(c_loaded, 16)
                    sp.dma_start(cc[:, :, 1], io["c_ctx"].rearrange("(k p) -> p k", p=P)).then_inc(c_loaded, 16)
                    sp.dma_start(b[:, :], io["b_ada"].rearrange("o (m p) -> p (o m)", p=P)).then_inc(c_loaded, 16)
                with sp.Fori(0, 4) as i:
                    for s in range(3):
                        sp.wait_ge(wa_used[s], i + 1)
                        sp.dma_start(wa[:, s], w[:, :, bass.ds((i * 3 + s) * BANK, BANK)]).then_inc(wa_loaded[s], 16)

            @block.scalar
            def _(act):
                act.wait_ge(c_loaded, 48)
                nc.scalar.activation(sc[:, :, :], cc[:, :, :], ACT.Silu).then_inc(sc_ready, 1)

            @block.tensor
            def _(pe):
                for s in range(3):
                    pe.nop().then_inc(wa_used[s], 1)
                pe.wait_ge(sc_ready, 1)

                def turn(g):
                    pe.wait_ge(row_copied, g + 1)
                    for m in range(4):
                        ins = nc.tensor.transpose(acc[:, 4 * g + m, :], rows[:, g, m * P:(m + 1) * P], ident[0:2, 0:2])
                    ins.then_inc(turned, 1)

                for g in range(12):
                    pe.wait_ge(wa_loaded[g % 3], 16 * (g // 3 + 1))
                    for k in range(DK):
                        last = nc.tensor.matmul(c.ps[0:2, 1 + g % 4, :], sc[:, k, :], wa[:, g % 3, k, :],
                                                start=(k == 0), stop=(k == DK - 1))
                    last.then_inc(wa_used[g % 3], 1)
                    if g:
                        turn(g - 1)
                turn(11)

            @block.vector
            def _(dve):
                for g in range(12):
                    dve.wait_ge(wa_used[g % 3], g // 3 + 2)
                    nc.vector.tensor_copy(rows[:, g, :], c.ps[0:2, 1 + g % 4, :]).then_inc(row_copied, 1)
                dve.wait_ge(turned, 12)
                nc.vector.tensor_tensor(ada[:, :, :], acc, b[:, :].unsqueeze(2).to_broadcast([P, 48, 2]),
                                        ALU.add).then_inc(ada_sum, 1)


def turn_in(c, io, xT, cT, ident):
    nc = c.nc
    with ExitStack() as tmp:
        rows = c.sb("rows", [P, 2, D], tmp)
        loaded = [c.sem(f"rows_loaded{s}") for s in range(2)]
        turned, dve_copied, act_copied = c.sem("turned"), c.sem("turned_dve_copied"), c.sem("turned_act_copied")
        src = [io["x"][0, b * P:(b + 1) * P, :] for b in range(NB)] + \
              [io["ctx"][0, b * P:(b + 1) * P, :] for b in range(TC // P)]
        dst = [xT[:, :, b * P:(b + 1) * P] for b in range(NB)] + \
              [cT[:, :, b * P:(b + 1) * P] for b in range(TC // P)]
        with nc.Block() as block:
            @block.sync
            def _(sp):
                for b in range(NBA):
                    if b >= 2:
                        sp.wait_ge(turned, b - 1)
                    sp.dma_start(rows[:, b % 2, :], src[b]).then_inc(loaded[b % 2], 16)

            @block.tensor
            def _(pe):
                for b in range(NBA):
                    pe.wait_ge(loaded[b % 2], 16 * (b // 2 + 1))
                    if b >= 2:
                        pe.wait_ge(dve_copied, b - 1)
                        pe.wait_ge(act_copied, b - 1)
                    for k in range(DK):
                        last = nc.tensor.transpose(c.ps[:, 2 * (b % 2) + k // 4, (k % 4) * P:(k % 4 + 1) * P],
                                                   rows[:, b % 2, k * P:(k + 1) * P], ident[:, :])
                    last.then_inc(turned, 1)

            @block.vector
            def _(dve):
                for b in range(NBA):
                    dve.wait_ge(turned, b + 1)
                    nc.vector.tensor_copy(dst[b][:, 0:4, :], c.ps[:, 2 * (b % 2), :].rearrange("p (k t) -> p k t", k=4)).then_inc(dve_copied, 1)

            @block.scalar
            def _(act):
                for b in range(NBA):
                    act.wait_ge(turned, b + 1)
                    nc.scalar.copy(dst[b][:, 4:8, :], c.ps[:, 2 * (b % 2) + 1, :].rearrange("p (k t) -> p k t", k=4)).then_inc(act_copied, 1)


def norm(c, name, parts, ones, out, shift=True, save=None):
    nc = c.nc
    with ExitStack() as tmp:
        sq = c.sb("sq", [P, 2, BANK], tmp)
        rs = c.sb("rs", [P, 2, BANK], tmp)
        squared, sq_used = c.sem(name + "_squared"), c.sem(name + "_sq_used")
        mean_ready, root_ready, scaled = c.sem(name + "_mean"), c.sem(name + "_root"), c.sem(name + "_scaled")
        done = c.sem(name + "_done")
        with nc.Block() as block:
            if save is not None:
                saved = c.sem(name + "_saved")

                @block.sync
                def _(sp):
                    sp.dma_start(save[1], save[0][:, :, :]).then_inc(saved, 16)
                    sp.wait_ge(saved, 16)

            @block.scalar
            def _(act):
                for n, (src, at, size, g, b, to) in enumerate(parts):
                    for k in range(DK):
                        j = n * DK + k
                        if j >= 2:
                            act.wait_ge(sq_used, j - 1)
                        nc.scalar.activation(sq[:, j % 2, 0:size], src[:, k, at:at + size], ACT.Square).then_inc(squared, 1)
                for n, (src, at, size, g, b, to) in enumerate(parts):
                    act.wait_ge(mean_ready, n + 1)
                    nc.scalar.activation(rs[:, n % 2, 0:size], rs[:, n % 2, 0:size], ACT.Sqrt).then_inc(root_ready, 1)
                    if shift:
                        for k in range(DK):
                            act.wait_ge(scaled, n * DK + k + 1)
                            nc.scalar.activation(out[:, k, to:to + size], out[:, k, to:to + size], ACT.Identity,
                                                 bias=b(k), scale=1.0).then_inc(done, 1)

            @block.tensor
            def _(pe):
                for n, (src, at, size, g, b, to) in enumerate(parts):
                    for k in range(DK):
                        pe.wait_ge(squared, n * DK + k + 1)
                        nc.tensor.matmul(c.ps[:, n, 0:size], ones[:, :], sq[:, (n * DK + k) % 2, 0:size],
                                         start=(k == 0), stop=(k == DK - 1)).then_inc(sq_used, 1)

            @block.vector
            def _(dve):
                step = c.dve.on(dve)
                for n, (src, at, size, g, b, to) in enumerate(parts):
                    dve.wait_ge(sq_used, DK * (n + 1))
                    if n >= 2:
                        dve.wait_ge(scaled, DK * (n - 1))
                    nc.vector.tensor_scalar(rs[:, n % 2, 0:size], c.ps[:, n, 0:size], 1.0 / D, EPS,
                                            ALU.mult, ALU.add).then_inc(mean_ready, 1)
                    dve.wait_ge(root_ready, n + 1)
                    step(nc.vector.reciprocal(rs[:, n % 2, 0:size], rs[:, n % 2, 0:size]))
                    for k in range(DK):
                        nc.vector.scalar_tensor_tensor(out[:, k, to:to + size], src[:, k, at:at + size], g(k),
                                                       rs[:, n % 2, 0:size], ALU.mult, ALU.mult).then_inc(scaled, 1)


def load_all(c, name, pairs):
    nc = c.nc
    loaded = c.sem(name)
    with nc.Block() as block:
        @block.sync
        def _(sp):
            with nc.allow_non_contiguous_dma("small vectors, one element to a partition"):
                for dst, src in pairs:
                    sp.dma_start(dst, src).then_inc(loaded, 16)
            sp.wait_ge(loaded, 16 * len(pairs))


def col(ap):
    return ap.rearrange("(k p) -> p k", p=P)


def build(nc, io):
    with ExitStack() as ctx:
        c = Core(nc, ctx)
        c.io = io
        c.eps = c.sb("eps", [P, 1])
        xT = c.sb("xT", [P, DK, T])
        ident, ones = c.sb("ident", [P, P]), c.sb("ones", [P, P])
        ada = c.sb("ada", [P, 48, 2])
        gains = c.sb("gains", [P, 5, DK])
        gainx = c.sb("gainx", [P, 3, DK])
        final2 = c.sb("final2", [P, DK])
        load_all(c, "consts_loaded", [
            (ident[:, :], io["k_ident"]), (ones[:, :], io["k_ones"]),
            (gains[:, 0], col(io["norm_mix"][0])), (gains[:, 1], col(io["norm_ffn"][0])),
            (gains[:, 2], col(io["final_norm"])), (gains[:, 3], col(io["attn_norm_g_2"][0])),
            (gains[:, 4], col(io["ffn_norm_g_2"][0])), (final2[:, :], col(io["final_norm_g_2"]))])
        with nc.Block() as block:
            @block.vector
            def _(dve):
                c.dve.on(dve)(nc.vector.memset(c.eps[:, :], EPS))
                for emptied in c.dve_emptied:
                    dve.nop().then_inc(emptied.sem, 1)

            @block.scalar
            def _(act):
                for emptied in c.act_emptied:
                    act.nop().then_inc(emptied.sem, 1)

            @block.tensor
            def _(pe):
                for used in c.acc_ready + c.w_used + [c.split_used]:
                    pe.nop().then_inc(used.sem, 1)
        for count in c.acc_ready + c.w_used + [c.split_used] + c.act_emptied + c.dve_emptied:
            count.base += 1
        modulation(c, io, ada, ident)
        first_block(c, io, xT, ident, ones, ada, gains, gainx)
        second_block(c, io, xT, ident, ones, gains, final2)


def first_block(c, io, xT, ident, ones, ada, gains, gainx):
    nc = c.nc
    mix_ctx = ExitStack()
    with mix_ctx:
        mixT = c.sb("mixT", [P, DK, T], mix_ctx)
        with ExitStack() as s1:
            mixer(c, io, xT, ident, ones, ada, gains, gainx, mixT, s1)
        residual(c, io["w_out"][0], DK, mixT, xT, lambda k: ada[:, 16 + k, 0:1], "mix")
    c.end_stage()
    feed_forward_1(c, io, xT, ones, ada, gainx)
    norm(c, "final1", [(xT, at, n, lambda k: gains[:, 2, k:k + 1], None, at) for at, n in HALVES],
         ones, xT, shift=False)


def split(c, x, hi, lo, name):
    nc = c.nc
    hi_ready, lo_ready = c.sem(name + "_hi"), c.sem(name + "_lo")
    with nc.Block() as block:
        @block.scalar
        def _(act):
            for k in range(DK):
                nc.scalar.copy(hi[:, k, :], x[:, k, :]).then_inc(hi_ready, 1)

        @block.vector
        def _(dve):
            for k in range(DK):
                dve.wait_ge(hi_ready, k + 1)
                nc.vector.tensor_tensor(lo[:, k, :], x[:, k, :], hi[:, k, :].bitcast(F32),
                                        ALU.subtract).then_inc(lo_ready, 1)


def split_pair(c, name, shape, ctx):
    return [c.sb(f"{name}_{n}", shape, ctx, F32R) for n in ("hi", "lo")]


def wide_product(c, name, tiles, k_tiles, w, w_cuts, src, dve_banks, act_banks, take, load_first=None):
    nc = c.nc
    steps, passes = k_tiles // 2, tiles // 4
    width, subs = T // passes, 8 // tiles
    with ExitStack() as tmp:
        w_raw = c.sb("w_raw", [P, 2, tiles * P], tmp)
        w_hi, w_lo = split_pair(c, "w", [P, 2, tiles * P], tmp)
        s_hi, s_lo = split_pair(c, "src", [P, 2, width], tmp)
        loaded, hi_ready, lo_ready, used = ([c.sem(f"{name}_{n}{s}") for s in range(2)]
                                            for n in ("loaded", "hi", "lo", "used"))
        summed, dve_taken, act_taken, first_loaded = (c.sem(f"{name}_{n}") for n in ("summed", "dve_taken", "act_taken", "first"))
        source = lambda n, k: src[:, bass.ds(k, 1), n * width:(n + 1) * width].rearrange("p o t -> p (o t)")

        def all_steps(eng, chain, per, body, between=None):
            for n in range(passes):
                body(n, 0, 0, n * steps)
                if n and between:
                    between(n - 1)
                body(n, 1, 1, n * steps)
                rest = lambda i: [body(n, i * 2 + (2 + s), s, i + (n * steps + 1)) for s in range(2)]
                if chain:
                    chain.loop(steps - 1, 2 * per, rest)
                else:
                    with eng.Fori(0, steps - 1) as i:
                        rest(i)
            if between:
                between(passes - 1)

        with nc.Block() as block:
            @block.sync
            def _(sp):
                def load(n, k, s, use):
                    if type(use) is not int or use:
                        sp.wait_ge(lo_ready[s], use)
                    at = 0
                    for lo, hi in w_cuts:
                        sp.dma_start(w_raw[:, s, at:at + hi - lo],
                                     w[:, bass.ds(k, 1), lo:hi].rearrange("p o t -> p (o t)")).then_inc(loaded[s], 16)
                        at += hi - lo
                all_steps(sp, None, 0, load)

            @block.scalar
            def _(act):
                def split_hi(n, k, s, use):
                    act.wait_ge(loaded[s], (use + 1) * (16 * len(w_cuts)))
                    if type(use) is not int or use:
                        act.wait_ge(used[s], use)
                    c.act(nc.scalar.copy(w_hi[:, s, :], w_raw[:, s, :]))
                    c.act(nc.scalar.copy(s_hi[:, s, :], source(n, k)))
                    act.nop().then_inc(hi_ready[s], 1)

                def empty(n):
                    if act_banks:
                        act.wait_ge(summed, n + 1)
                    for b in act_banks:
                        take(nc.scalar, n, b // subs, n * width + b % subs * BANK, c.ps[:, b, :]).then_inc(act_taken, 1)
                if load_first is not None:
                    act.dma_start(load_first[0][:, :, :], load_first[1]).then_inc(first_loaded, 16)
                all_steps(act, c.act.on(act), 2, split_hi, empty)

            @block.vector
            def _(dve):
                def split_lo(n, k, s, use):
                    dve.wait_ge(hi_ready[s], use + 1)
                    c.dve(nc.vector.tensor_tensor(w_lo[:, s, :], w_raw[:, s, :], w_hi[:, s, :].bitcast(F32), ALU.subtract))
                    c.dve(nc.vector.tensor_tensor(s_lo[:, s, :], source(n, k), s_hi[:, s, :].bitcast(F32), ALU.subtract))
                    dve.nop().then_inc(lo_ready[s], 1)

                def empty(n):
                    if not dve_banks:
                        return
                    dve.wait_ge(summed, n + 1)
                    if n == 0 and load_first is not None:
                        dve.wait_ge(first_loaded, 16)
                    for b in dve_banks:
                        take(nc.vector, n, b // subs, n * width + b % subs * BANK, c.ps[:, b, :]).then_inc(dve_taken, 1)
                all_steps(dve, c.dve.on(dve), 2, split_lo, empty)

            @block.tensor
            def _(pe):
                def products(n, first, last, s, use):
                    pe.wait_ge(hi_ready[s], use + 1)
                    for j, (wp, sp) in enumerate(((w_hi, s_hi), (w_hi, s_lo), (w_lo, s_hi))):
                        if j == 1:
                            pe.wait_ge(lo_ready[s], use + 1)
                        for b in range(8):
                            if n and first and j == 0:
                                if b in dve_banks:
                                    pe.wait_ge(dve_taken, len(dve_banks) * (n - 1) + dve_banks.index(b) + 1)
                                else:
                                    pe.wait_ge(act_taken, len(act_banks) * (n - 1) + act_banks.index(b) + 1)
                            m, at = b // subs, b % subs * BANK
                            ins = nc.tensor.matmul(c.ps[:, b, :], wp[:, s, m * P:(m + 1) * P], sp[:, s, at:at + BANK],
                                                   start=(first and j == 0), stop=(last and j == 2))
                    ins.then_inc(used[s], 1)
                for n in range(passes):
                    for s in range(2):
                        products(n, s == 0, False, s, n * steps)
                    if steps > 2:
                        with pe.Fori(0, steps - 2) as i:
                            for s in range(2):
                                products(n, False, False, s, i + (n * steps + 1))
                    for s in range(2):
                        products(n, False, s == 1, s, n * steps + steps - 1)
                    pe.wait_ge(used[1], (n + 1) * steps)
                    pe.nop().then_inc(summed, 1)


def residual(c, w, k_tiles, src, xT, gate, name, saved=None):
    nc = c.nc

    def add(eng, n, m, at, acc):
        dst = xT[:, m, at:at + BANK]
        if gate is None:
            return eng.tensor_tensor(dst, acc, dst, ALU.add)
        return eng.scalar_tensor_tensor(dst, acc, gate(m), dst, ALU.mult, ALU.add)
    wide_product(c, name, DK, k_tiles, w.rearrange("(k p) n -> p k n", p=P), [(0, D)], src, list(range(8)), [], add,
                 None if saved is None else (xT, saved))


def copy_wide(c, name, w, w_cuts, tiles, src, dst, scale=lambda m: 1.0):
    def copy(eng, n, m, at, acc):
        if eng is c.nc.vector:
            return eng.tensor_scalar(dst[:, m, at:at + BANK], acc, scale(m), None, ALU.mult)
        return eng.mul(dst[:, m, at:at + BANK], acc, scale(m))
    wide_product(c, name, tiles, DK, w, w_cuts, src, [0, 2, 4, 6], [1, 3, 5, 7], copy)


def ffn_buffers(xT):
    flat = xT[:, :, :].rearrange("p k t -> p (k t)")
    return (flat[:, 0:4 * DK * P].rearrange("p (s a k n) -> p s a k n", s=2, a=2, k=DK),
            *(flat[:, at * T:(at + 2) * T].rearrange("p (s t) -> p s t", s=2) for at in (4, 6)))


def feed_forward_1(c, io, xT, ones, ada, gainx):
    nc = c.nc
    saved = nc.dram_tensor("x_saved1", (P, DK, T), F32, kind="Internal").ap()
    with ExitStack() as s2:
        hid = c.sb("hid", [P, FK, T], s2)
        with ExitStack() as s3:
            h_hi, h_lo = split_pair(c, "h", [P, DK, T], s3)
            cw = c.sb("cw", [P, 4, FK], s3)
            load_all(c, "ffn_conv_loaded", [(cw[:, j], col(io["ffn_conv_w"][0, j])) for j in range(3)]
                     + [(cw[:, 3], col(io["ffn_conv_b"][0]))])
            norm(c, "norm_ffn1", [(xT, at, n, lambda k: gainx[:, 2, k:k + 1], lambda k: ada[:, 24 + k, 0:1], at)
                                  for at, n in HALVES], ones, hid, save=(xT, saved))
            split(c, hid, h_hi, h_lo, "h1")
            w_parts = split_pair(c, "w", [P, 2, DK, P], s3)
            wbuf, a, tap = ffn_buffers(xT)
            a_copied, conv_ready, gelu_ready = c.sem("a_copied"), c.sem("conv_ready"), c.sem("gelu_ready")
            wv = io["w_up"][0].rearrange("(k p) n -> p k n", p=P)

            def act_part(eng, tile, s, i):
                n = i * 2 + s + 1
                c.act(nc.scalar.copy(a[:, s, :], c.ps[:, 4 * s:4 * s + 2, :].rearrange("p b t -> p (b t)")))
                eng.nop().then_inc(a_copied, 1)
                eng.wait_ge(conv_ready, n)
                c.act(nc.scalar.activation(tap[:, s, :], tap[:, s, :], ACT.Gelu_apprx_tanh))
                eng.nop().then_inc(gelu_ready, 1)

            def dve_part(eng, tile, s, i):
                n = i * 2 + s + 1
                w = [cw[:, j, bass.ds(tile, 1)] for j in range(4)]
                eng.wait_ge(a_copied, n)
                c.dve(nc.vector.tensor_scalar(tap[:, s, :], a[:, s, :], w[1], w[3], ALU.mult, ALU.add))
                c.dve(nc.vector.scalar_tensor_tensor(tap[:, s, 1:T], a[:, s, 0:T - 1], w[0], tap[:, s, 1:T], ALU.mult, ALU.add))
                c.dve(nc.vector.scalar_tensor_tensor(tap[:, s, 0:T - 1], a[:, s, 1:T], w[2], tap[:, s, 0:T - 1], ALU.mult, ALU.add))
                eng.nop().then_inc(conv_ready, 1)
                eng.wait_ge(gelu_ready, n)
                c.dve(nc.vector.tensor_tensor(hid[:, bass.ds(tile, 1), :].rearrange("p o t -> p (o t)"),
                                              c.ps[:, 4 * s + 2:4 * s + 4, :].rearrange("p b t -> p (b t)"),
                                              tap[:, s, :], ALU.mult))
            project(c, FK, 2, DK, lambda part, t: wv[:, :, bass.ds(t * P + part * FF, P)], lambda part: (h_hi, h_lo), HALVES,
                    lambda s, part, n: c.ps[:, 4 * s + 2 * part + n, :], act_part, dve_part, 2, 4, wbuf, w_parts)
        residual(c, io["w_down"][0], FK, hid, xT, lambda k: ada[:, 40 + k, 0:1], "down1", saved)


def token_major(c, name, w, cols, src, lhs_cols, dst):
    nc = c.nc
    blocks = len(lhs_cols)
    with ExitStack() as tmp:
        wbuf = c.sb("w_tok", [P, DK, cols], tmp)
        loaded = [c.sem(f"{name}_w{j}") for j in range(4)]
        summed, emptied = c.sem(name + "_sum"), c.sem(name + "_out")
        with nc.Block() as block:
            @block.sync
            def _(sp):
                for j in range(4):
                    for at, view in w:
                        sp.dma_start(wbuf[:, 2 * j:2 * j + 2, at:at + view.shape[2]], view[:, 2 * j:2 * j + 2, :]).then_inc(loaded[j], 16)

            @block.tensor
            def _(pe):
                for b in range(blocks):
                    if b >= 8:
                        pe.wait_ge(emptied, b - 7)
                    for k in range(DK):
                        if b == 0 and k % 2 == 0:
                            pe.wait_ge(loaded[k // 2], 16 * len(w))
                        last = nc.tensor.matmul(c.ps[:, b % 8, 0:cols], lhs_cols[b](src, k), wbuf[:, k, :],
                                                start=(k == 0), stop=(k == DK - 1))
                    last.then_inc(summed, 1)

            @block.vector
            def _(dve):
                for b in range(blocks):
                    dve.wait_ge(summed, b + 1)
                    nc.vector.tensor_copy(dst(b), c.ps[:, b % 8, 0:cols]).then_inc(emptied, 1)


def mixer(c, io, xT, ident, ones, ada, gains, gainx, mixT, s1):
    nc = c.nc
    hT = c.sb("hT", [P, DK, TA], s1)
    with ExitStack() as s2:
        cT = c.sb("cT", [P, DK, TC], s2)
        turn_in(c, io, xT, cT, ident)
        with nc.Block() as block:
            @block.vector
            def _(dve):
                for j, (at, who, g) in enumerate([(8, 0, 0), (8, 1, 0), (32, 0, 1)]):
                    c.dve.on(dve)(nc.vector.scalar_tensor_tensor(gainx[:, j, :], ada[:, at:at + DK, who], 1.0,
                                                                 gains[:, g, :], ALU.add, ALU.mult))
        norm(c, "norm_mix", [(xT, at, n, lambda k: gainx[:, 0, k:k + 1], lambda k: ada[:, k, 0:1], at) for at, n in HALVES]
             + [(cT, 0, TC, lambda k: gainx[:, 1, k:k + 1], lambda k: ada[:, k, 1:2], T)], ones, hT)
    w_in = io["w_in"][0].rearrange("(k p) n -> p k n", p=P)
    with ExitStack() as s2:
        window(c, io, w_in, hT, ident, mixT, s2)
    c.end_stage()
    with ExitStack() as s2:
        mlstm(c, io, w_in, hT, ident, ones, mixT, s2)


def plain_blocks(n):
    return [lambda src, k, b=b: src[:, k, b * P:(b + 1) * P] for b in range(n)]


def mlstm(c, io, w_in, hT, ident, ones, mixT, s2):
    nc = c.nc
    qkT = c.sb("qkT", [P, 2 * MH, TA], s2)
    between = c.sb("between", [MH, 2, NBA, NBA], s2)
    keyw = c.sb("keyw", [P, 2, 2, NBA, MH], s2)
    sel = c.sb("sel", [MH, MH, P], s2)
    mgain = c.sb("mgain", [P, MH], s2)

    with ExitStack() as tmp:
        PADW = TA + 3
        wbuf = c.sb("wbuf", [P, 2, 1, DK, P], tmp)
        pad = c.sb("pad", [P, 2, PADW], tmp)
        tap = c.sb("tap", [P, 2, PADW], tmp)
        cw = c.sb("cw", [P, 4, DK], tmp)
        load_all(c, "qk_conv_loaded", [(cw[:, j], col(io["qk_conv_w"][0, j])) for j in range(3)]
                 + [(cw[:, 3], col(io["qk_conv_b"][0])), (sel[:, :, :], io["k_sel"]),
                    (mgain[:, :], col(io["mlstm_norm"][0]))])
        with nc.Block() as block:
            @block.vector
            def _(dve):
                c.dve.on(dve)(nc.vector.memset(pad[:, :, :], 0.0))
        copied, conv_ready = c.sem("qk_copied"), c.sem("qk_conv")
        W3 = PADW - 2

        def act_part(eng, tile, s, i):
            c.act(nc.scalar.copy(pad[:, s, 1:T + 1], c.ps[:, 4 * s:4 * s + 2, :].rearrange("p b t -> p (b t)")))
            c.act(nc.scalar.copy(pad[:, s, T + 2:TA + 2], c.ps[:, 4 * s + 2, 0:TC]))
            eng.nop().then_inc(copied, 1)
            eng.wait_ge(conv_ready, i * 2 + s + 1)
            c.act(nc.scalar.activation(qkT[:, bass.ds(tile, 1), 0:T].rearrange("p o t -> p (o t)"), tap[:, s, 0:T], ACT.Silu))
            c.act(nc.scalar.activation(qkT[:, bass.ds(tile, 1), T:TA].rearrange("p o t -> p (o t)"), tap[:, s, T + 1:TA + 1], ACT.Silu))

        def dve_part(eng, tile, s, i):
            w = [cw[:, j, bass.ds(tile, 1)] for j in range(4)]
            eng.wait_ge(copied, i * 2 + s + 1)
            c.dve(nc.vector.tensor_scalar(tap[:, s, 0:W3], pad[:, s, 1:W3 + 1], w[1], w[3], ALU.mult, ALU.add))
            c.dve(nc.vector.scalar_tensor_tensor(tap[:, s, 0:W3], pad[:, s, 0:W3], w[0], tap[:, s, 0:W3], ALU.mult, ALU.add))
            c.dve(nc.vector.scalar_tensor_tensor(tap[:, s, 0:W3], pad[:, s, 2:W3 + 2], w[2], tap[:, s, 0:W3], ALU.mult, ALU.add))
            eng.nop().then_inc(conv_ready, 1)
        project(c, 2 * MH, 1, DK, lambda part, t: w_in[:, :, bass.ds(t * P, P)], lambda part: hT, XCHUNKS,
                lambda s, part, n: c.ps[:, 4 * s + n, :], act_part, dve_part, 4, 3, wbuf)

    oT = c.sb("oT", [P, MH, T], s2)

    def gate(eng, n, m, at, acc):
        return eng.activation(oT[:, m, at:at + BANK], acc, ACT.Sigmoid)
    wide_product(c, "o_gate", MH, DK, w_in, [(OFF_O, OFF_O + 512)], hT, [], list(range(8)), gate)
    v = c.sb("v_m", [P, NBA, 512], s2)
    token_major(c, "v_m", [(0, w_in[:, :, OFF_V:OFF_V + 512])], 512, hT, plain_blocks(NBA), lambda b: v[:, b, :])
    negM = c.sb("negM", [MH, 2, T], s2)
    floor = c.sb("floor", [MH, 2, T], s2)
    with ExitStack() as s3:
        g = c.sb("g", [P, NBA, NG], s3)
        token_major(c, "gates", [(0, w_in[:, :, OFF_G:OFF_G + NG])], NG, hT, plain_blocks(NBA), lambda b: g[:, b, :])
        gates(c, io, g, hT, ident, negM, floor, between, keyw)
    mlstm_heads(c, hT, qkT, oT, v, negM, floor, between, keyw, sel, mgain, ones, mixT)


def carve(tile, parts, sizes):
    flat = tile[0:parts].rearrange("p k t -> p (k t)")
    at, views = 0, []
    for n in sizes:
        views.append(flat[:, at:at + n])
        at += n
    assert at <= flat.shape[1]
    return views


def gates(c, io, g, hT, ident, negM, floor, between, keyw):
    nc = c.nc
    with ExitStack() as s3:
        rows, reset, t1, t2 = carve(hT, MH, [4 * TA, 2 * TA, TA, TA])
        rows = rows.rearrange("p (k t) -> p k t", k=4)
        reset = reset.rearrange("p (k t) -> p k t", k=2)
        gb = c.sb("gb", [MH, 4], s3)
        later = c.sb("later", [MH, 2, NBA, NBA], s3)
        t3 = c.sb("t3", [MH, TA], s3)
        nat = rows.rearrange("p (d w) t -> p d w t", d=2)
        small = c.sb("small", [MH, 4, NBA], s3)
        grid = g[0:MH].rearrange("p b n -> p (b n)")[:, 0:NBA * NBA].rearrange("p (j i) -> p j i", j=NBA)
        load_all(c, "gate_consts", [(gb[:, :], io["gate_b"][0].rearrange("(k h) -> h k", h=MH)),
                                    (reset[:, :, :], io["k_reset"]), (later[:, :, :, :], io["k_later"])])
        turned, taken = c.sem("gates_turned"), c.sem("gates_taken")
        spans = [(slice(T, TA), slice(0, TC)), (slice(0, T), slice(TC, TA))]

        def rev(ap, d):
            return ap[:, ::-1] if d else ap

        with nc.Block() as block:
            @block.tensor
            def _(pe):
                for kind in range(4):
                    if kind >= 2:
                        pe.wait_ge(taken, kind - 1)
                    for b in range(NBA):
                        last = nc.tensor.transpose(c.ps[0:MH, 4 * (kind % 2) + b // 4, (b % 4) * P:(b % 4 + 1) * P],
                                                   g[:, b, kind * MH:(kind + 1) * MH], ident[:, :])
                    last.then_inc(turned, 1)

            @block.vector
            def _(dve):
                step = c.dve.on(dve)
                for kind in range(4):
                    dve.wait_ge(turned, kind + 1)
                    flat = c.ps[0:MH, 4 * (kind % 2):4 * (kind % 2) + 3, :].rearrange("p b t -> p (b t)")
                    for nat_s, proc_s in spans:
                        step(nc.vector.tensor_scalar(rows[:, kind, proc_s], rev(flat[:, nat_s], kind // 2),
                                                     gb[:, kind:kind + 1], None, ALU.add))
                    dve.nop().then_inc(taken, 1)

        with nc.Block() as block:
            abs_ready, soft_ready = c.sem("gate_abs"), c.sem("gate_soft")

            @block.scalar
            def _(act):
                step = c.act.on(act)
                for d in range(2):
                    t = (t1, t2)[d]
                    step(nc.scalar.activation(t[:, :], rows[:, 2 * d + 1, :], ACT.Abs))
                    step(nc.scalar.activation(t[:, :], t[:, :], ACT.Exp, scale=-1.0))
                    nc.scalar.activation(t[:, :], t[:, :], ACT.Ln, bias=1.0).then_inc(soft_ready, 1)

            @block.vector
            def _(dve):
                step = c.dve.on(dve)
                for d in range(2):
                    dve.wait_ge(soft_ready, d + 1)
                    step(nc.vector.scalar_tensor_tensor(rows[:, 2 * d + 1, :], rows[:, 2 * d + 1, :], 0.0,
                                                        (t1, t2)[d][:, :], ALU.min, ALU.subtract))

        with nc.Block() as block:
            m_ready = c.sem("gate_m")

            @block.vector
            def _(dve):
                step = c.dve.on(dve)
                blk = lambda ap: ap.rearrange("p (b t) -> p b t", t=P)
                for d in range(2):
                    li, lf = rows[:, 2 * d, :], rows[:, 2 * d + 1, :]
                    L, U, C = t1[:, :], t2[:, :], t3[:, :]
                    step(nc.vector.tensor_tensor_scan(L, reset[:, 0, :], lf, 0.0, ALU.mult, ALU.add))
                    step(nc.vector.tensor_tensor(U, li, L, ALU.subtract))
                    step(nc.vector.tensor_tensor_scan(C, reset[:, 1, :], U, NEG, ALU.add, ALU.max))
                    step(nc.vector.tensor_copy(small[:, 0, :], blk(L)[:, :, P - 1]))
                    step(nc.vector.tensor_tensor(small[:, 1, :], blk(C)[:, :, P - 1], small[:, 0, :], ALU.add))
                    step(nc.vector.tensor_tensor_scan(small[:, 2, :], small[:, 0, :], small[:, 1, :], NEG, ALU.add, ALU.max))
                    step(nc.vector.memset(grid[:, :, :], 0.0))
                    step(nc.vector.tensor_tensor(grid[:, :, 1:NBA], later[:, 0, :, 1:NBA],
                                                 small[:, 0, 0:NBA - 1].unsqueeze(1).to_broadcast([MH, NBA, NBA - 1]), ALU.mult))
                    step(nc.vector.tensor_tensor_scan(between[:, d].rearrange("p j i -> p (j i)"),
                                                      later[:, 1].rearrange("p j i -> p (j i)"),
                                                      grid[:, :, :].rearrange("p j i -> p (j i)"), 0.0, ALU.mult, ALU.add))
                    step(nc.vector.tensor_tensor(blk(C)[:, 2:NBA, :], blk(C)[:, 2:NBA, :],
                                                 small[:, 2, 1:NBA - 1].unsqueeze(2).to_broadcast([MH, NB, P]), ALU.max))
                    step(nc.vector.tensor_tensor(L[:, TC:TA], L[:, TC:TA], C[:, TC:TA], ALU.add))
                    for nat_s, proc_s in spans:
                        step(nc.vector.tensor_copy(nat[:, d, 1, nat_s], rev(U[:, proc_s], d)))
                    step(nc.vector.tensor_tensor(blk(U), blk(U), small[:, 0, :].unsqueeze(2).to_broadcast([MH, NBA, P]), ALU.add))
                    for nat_s, proc_s in spans:
                        step(nc.vector.tensor_copy(nat[:, d, 0, nat_s], rev(U[:, proc_s], d)))
                    step(nc.vector.tensor_scalar(negM[:, d, :], rev(C[:, TC:TA], d), -1.0, None, ALU.mult))
                    step(nc.vector.tensor_scalar(floor[:, d, :], rev(L[:, TC:TA], d), -1.0, 88.0, ALU.mult, ALU.min))
                    dve.nop().then_inc(m_ready, 1)

            @block.scalar
            def _(act):
                step = c.act.on(act)
                for d in range(2):
                    act.wait_ge(m_ready, d + 1)
                    step(nc.scalar.activation(floor[:, d, :], floor[:, d, :], ACT.Exp))

        with nc.Block() as block:
            cols_ready = c.sem("gate_cols")
            flat = c.ps[:, 0, 0:2 * 2 * NBA * MH].rearrange("p (d w b h) -> p d w b h", d=2, w=2, b=NBA)

            @block.tensor
            def _(pe):
                for d in range(2):
                    for w in range(2):
                        for b in range(NBA):
                            last = nc.tensor.transpose(flat[:, d, w, b, :], nat[:, d, w, b * P:(b + 1) * P], ident[0:MH, 0:MH])
                last.then_inc(cols_ready, 1)

            @block.vector
            def _(dve):
                dve.wait_ge(cols_ready, 1)
                c.dve.on(dve)(nc.vector.tensor_copy(keyw[:, :, :, :, :].rearrange("p d w b h -> p (d w b h)"),
                                                    c.ps[:, 0, 0:2 * 2 * NBA * MH]))


NORM_AFTER = 6


def mlstm_heads(c, hT, qkT, oT, v, negM, floor, between, keyw, sel, mgain, ones, mixT):
    nc = c.nc
    SCALE = float(P) ** -0.5
    units = []
    for h in range(MH):
        for d in range(2):
            units += [("negM", h, d, None), ("floor", h, d, None)]
            for j in range(NBA):
                if j < 2:
                    b, t0, t1, diag = (NB + j, NB + 1 - j)[d], 0, T, None
                else:
                    b = (j - 2, NBA - 1 - j)[d]
                    t0, t1 = ((b * P, T), (0, (b + 1) * P))[d]
                    diag = b * P
                units.append(("key", h, d, (j, b, t0, t1, diag)))
    for h in range(MH):
        after = [i for i, u in enumerate(units) if u[:3] == ("key", h + 1, 0)]
        units.insert(after[NORM_AFTER] + 1 if after else len(units), ("norm", h, None, None))
    with ExitStack() as tmp:
        bias, low, S, mask, w, h_sum, num_copy = carve(hT, P, [2 * T, 2 * T, MH * 2 * NBA * NBA, 2 * P, 2 * T, T, T])
        bias = bias.rearrange("p (d t) -> p d t", d=2)
        low = low.rearrange("p (d t) -> p d t", d=2)
        S = S.rearrange("p (h d x) -> p h d x", h=MH, d=2)
        mask = mask.rearrange("p (d t) -> p d t", d=2)
        w = w.rearrange("p (s t) -> p s t", s=2)
        load_all(c, "tri_loaded", [(mask[:, :, :], c.io["k_tri"])])
        scores_ready, args_ready = c.sem("scores_ready"), c.sem("args_ready")
        weights_ready, probs_ready, summed = c.sem("weights_ready"), c.sem("probs_ready"), c.sem("summed")
        pair_summed, den_copied, pair_done = c.sem("pair_summed"), c.sem("den_copied"), c.sem("pair_done")
        banks_free = c.sem("pair_banks_free")
        sq_ready, root_ready = c.sem("hn_squared"), c.sem("hn_root")

        def slices(t0, t1):
            return [(b, max(t0, b * BANK), min(t1, (b + 1) * BANK)) for b in range(2)
                    if max(t0, b * BANK) < min(t1, (b + 1) * BANK)]

        with nc.Block() as block:
            bet_ready = c.sem("between_ready")

            @block.tensor
            def _(pe):
                for h in range(MH):
                    last = nc.tensor.matmul(c.ps[:, h, 0:200], sel[:, h, :], between[:, :, :, :].rearrange("p d j i -> p (d j i)"),
                                            start=True, stop=True)
                last.then_inc(bet_ready, 1)

            @block.vector
            def _(dve):
                dve.wait_ge(bet_ready, 1)
                c.dve.on(dve)(nc.vector.tensor_copy(S[:, :, :, :].rearrange("p h d x -> p h (d x)"), c.ps[:, 0:MH, 0:200]))
        S4 = S[:, :, :, :].rearrange("p h d (j i) -> p h d j i", j=NBA)

        key_no, pair_no, n, m = [], [], 0, 0
        for kind, h, d, x in units:
            key_no.append(n)
            n += kind == "key"
            if kind == "negM":
                m += 1
            pair_no.append(m)

        norms = [[p for p in range(u) if units[p][0] == "norm"] for u in range(len(units))]

        with nc.Block() as block:
            num = lambda b: c.ps[:, 4 + b, :]
            den = lambda b: c.ps[:, 6 + b, :]

            @block.tensor
            def _(pe):
                def first(u):
                    kind, h, d, x = units[u]
                    if u >= 2:
                        pe.wait_ge(probs_ready, u - 1)
                    for b, lo, hi in (slices(x[2], x[3]) if kind == "key" else slices(0, T)):
                        dst = c.ps[:, 2 * (u % 2) + b, lo - b * BANK:hi - b * BANK]
                        if kind == "key":
                            last = nc.tensor.matmul(dst, qkT[:, MH + h, x[1] * P:(x[1] + 1) * P], qkT[:, h, lo:hi],
                                                    start=True, stop=True)
                        elif kind == "norm":
                            if b == 0:
                                pe.wait_ge(sq_ready, h + 1)
                            last = nc.tensor.matmul(dst, ones[:, :], w[:, u % 2, lo:hi], start=True, stop=True)
                        else:
                            last = nc.tensor.matmul(dst, sel[:, h, :], (negM if kind == "negM" else floor)[:, d, lo:hi],
                                                    start=True, stop=True)
                    last.then_inc(scores_ready, 1)

                def second(u):
                    kind, h, d, x = units[u]
                    if kind != "key":
                        return
                    j, kb, t0, t1, diag = x
                    if j == 0 and pair_no[u] > 1:
                        pe.wait_ge(banks_free, pair_no[u] - 1)
                    pe.wait_ge(probs_ready, u + 1)
                    for b, lo, hi in slices(t0, t1):
                        cols = slice(lo - b * BANK, hi - b * BANK)
                        nc.tensor.matmul(num(b)[:, cols], v[:, kb, h * P:(h + 1) * P], w[:, u % 2, lo:hi],
                                         start=(j == 0), stop=False, skip_group_check=True)
                        last = nc.tensor.matmul(den(b)[:, cols], ones[:, :], w[:, u % 2, lo:hi],
                                                start=(j == 0), stop=False, skip_group_check=True)
                    last.then_inc(summed, 1)
                    if j == NBA - 1:
                        pe.wait_ge(summed, key_no[u] + 1)
                        pe.nop().then_inc(pair_summed, 1)
                first(0)
                for u in range(len(units)):
                    if u + 1 < len(units) and units[u + 1][0] != "norm":
                        first(u + 1)
                    second(u)
                    if u + 1 < len(units) and units[u + 1][0] == "norm":
                        first(u + 1)

            @block.gpsimd
            def _(pool):
                step = c.pool.on(pool)
                for u, (kind, h, d, x) in enumerate(units):
                    if kind != "key":
                        continue
                    j, kb, t0, t1, diag = x
                    if j == 0:
                        pool.wait_ge(probs_ready, u - 1)
                    if u >= 2:
                        prev = [p for p in range(u - 1) if (u - p) % 2 == 0 and units[p][0] != "negM" and units[p][0] != "floor"]
                        if prev and units[prev[-1]][0] == "key":
                            pool.wait_ge(summed, key_no[prev[-1]] + 1)
                        elif prev:
                            pool.wait_ge(probs_ready, prev[-1] + 1)
                            if key_no[prev[-1]]:
                                pool.wait_ge(summed, key_no[prev[-1]])
                    B = bias[:, d, :]
                    far = (t0, t1) if diag is None else ((diag + P, t1) if d == 0 else (t0, diag))
                    if diag is not None:
                        nc.gpsimd.tensor_tensor(w[:, u % 2, diag:diag + P], B[:, diag:diag + P], mask[:, d, :], ALU.add).then_inc(args_ready, 1)
                    if far[0] < far[1]:
                        q0, q1 = far[0] // P, far[1] // P
                        i0 = (q0 + 2, NBA - 1 - q0)[d]
                        i1 = i0 + (q1 - q0) * (1, -1)[d]
                        s = S4[:, h, d, j, i0:i1] if d == 0 else S4[:, h, d, j, i0:(i1 if i1 >= 0 else None):-1]
                        nc.gpsimd.tensor_tensor(w[:, u % 2, far[0]:far[1]].rearrange("p (q t) -> p q t", t=P),
                                                B[:, far[0]:far[1]].rearrange("p (q t) -> p q t", t=P),
                                                s.unsqueeze(2).to_broadcast([P, q1 - q0, P]), ALU.add).then_inc(args_ready, 1)

            @block.scalar
            def _(act):
                step = c.act.on(act)
                n = 0
                for u, (kind, h, d, x) in enumerate(units):
                    if kind == "norm":
                        act.wait_ge(pair_done, 2 * h + 2)
                        prev = [p for p in range(u) if (u - p) % 2 == 0 and units[p][0] == "key"]
                        act.wait_ge(summed, key_no[prev[-1]] + 1)
                        nc.scalar.activation(w[:, u % 2, :], h_sum[:, :], ACT.Square).then_inc(sq_ready, 1)
                        act.wait_ge(args_ready, n)
                        act.wait_ge(scores_ready, u + 1)
                        step(nc.scalar.activation(num_copy[:, :], c.ps[:, 2 * (u % 2):2 * (u % 2) + 2, :].rearrange("p b t -> p (b t)"),
                                                  ACT.Sqrt, scale=1.0 / P, bias=c.eps[:, 0:1]))
                        act.nop().then_inc(root_ready, 1)
                        continue
                    if kind != "key":
                        continue
                    j, kb, t0, t1, diag = x
                    far = (t0, t1) if diag is None else ((diag + P, t1) if d == 0 else (t0, diag))
                    if diag is not None:
                        n += 1
                        act.wait_ge(args_ready, n)
                        last = step(nc.scalar.activation(w[:, u % 2, diag:diag + P], w[:, u % 2, diag:diag + P], ACT.Exp,
                                                         bias=keyw[:, d, 1, kb, h:h + 1]))
                    if far[0] < far[1]:
                        n += 1
                        act.wait_ge(args_ready, n)
                        step(nc.scalar.activation(w[:, u % 2, far[0]:far[1]], w[:, u % 2, far[0]:far[1]], ACT.Exp,
                                                  bias=keyw[:, d, 0, kb, h:h + 1]))
                    act.nop().then_inc(weights_ready, 1)
                    if j == NBA - 1:
                        act.wait_ge(pair_summed, pair_no[u])
                        nc.scalar.activation(bias[:, d, :], c.ps[:, 6:8, :].rearrange("p b t -> p (b t)"), ACT.Abs).then_inc(den_copied, 1)
                        if pair_no[u] > 1:
                            act.wait_ge(pair_done, pair_no[u] - 1)
                        if norms[u]:
                            act.wait_ge(probs_ready, norms[u][-1] + 1)
                        step(nc.scalar.copy(num_copy[:, :], c.ps[:, 4:6, :].rearrange("p b t -> p (b t)")))
                        act.nop().then_inc(banks_free, 1)

            @block.vector
            def _(dve):
                step = c.dve.on(dve)

                def divide(pair):
                    d = (pair - 1) % 2
                    dve.wait_ge(den_copied, pair)
                    step(nc.vector.tensor_tensor(bias[:, d, :], bias[:, d, :], low[:, d, :], ALU.max))
                    step(nc.vector.reciprocal(bias[:, d, :], bias[:, d, :]))
                    dve.wait_ge(banks_free, pair)
                    if d == 0:
                        step(nc.vector.tensor_tensor(h_sum[:, :], num_copy[:, :], bias[:, d, :], ALU.mult))
                    else:
                        step(nc.vector.tensor_tensor(bias[:, d, :], num_copy[:, :], bias[:, d, :], ALU.mult))
                        step(nc.vector.tensor_tensor(h_sum[:, :], h_sum[:, :], bias[:, d, :], ALU.add))
                    dve.nop().then_inc(pair_done, 1)

                for u, (kind, h, d, x) in enumerate(units):
                    if kind == "norm" and h == MH - 1:
                        divide(2 * MH)
                    dve.wait_ge(scores_ready, u + 1)
                    flat = c.ps[:, 2 * (u % 2):2 * (u % 2) + 2, :].rearrange("p b t -> p (b t)")
                    if kind in ("negM", "floor"):
                        dst = (bias if kind == "negM" else low)[:, d, :]
                        nc.vector.tensor_copy(dst, flat).then_inc(probs_ready, 1)
                    elif kind == "key":
                        j, kb, t0, t1, diag = x
                        dve.wait_ge(weights_ready, key_no[u] + 1)
                        nc.vector.scalar_tensor_tensor(w[:, u % 2, t0:t1], flat[:, t0:t1], SCALE, w[:, u % 2, t0:t1],
                                                       ALU.mult, ALU.mult).then_inc(probs_ready, 1)
                        if j == 1 and pair_no[u] > 1:
                            divide(pair_no[u] - 1)
                    else:
                        dve.wait_ge(root_ready, h + 1)
                        step(nc.vector.reciprocal(num_copy[:, :], num_copy[:, :]))
                        step(nc.vector.scalar_tensor_tensor(h_sum[:, :], h_sum[:, :], mgain[:, h:h + 1], num_copy[:, :], ALU.mult, ALU.mult))
                        step(nc.vector.tensor_tensor(mixT[:, h, :], h_sum[:, :], oT[:, h, :], ALU.mult))
                        dve.nop().then_inc(probs_ready, 1)


def window(c, io, w_in, hT, ident, mixT, s2):
    nc = c.nc
    AT = AH // 2
    qT = c.sb("qaT", [P, AT, T], s2)
    kT = c.sb("kaT", [P, KVH, TA], s2)
    va = c.sb("v_a", [P, NBA, P], s2)
    with ExitStack() as tmp:
        rope = c.sb("rope", [P, 2, T], tmp)
        swap = c.sb("swap", [P, P], tmp)
        wq = c.sb("w_qa", [P, DK, 5 * P], tmp)
        raw = c.sb("raw", [P, 2, TA], tmp)
        loaded, summed, raw_ready, swapped, roped = (c.sem("rope_" + n) for n in ("w", "sum", "raw", "swap", "done"))
        wq_loaded = [c.sem(f"wq_loaded{m}") for m in range(5)]
        dup = c.sem("k_dup")
        with nc.Block() as block:
            @block.sync
            def _(sp):
                for m in range(5):
                    sp.dma_start(wq[:, :, m * P:(m + 1) * P], w_in[:, :, OFF_QA + m * P:OFF_QA + (m + 1) * P]).then_inc(wq_loaded[m], 16)
                    if m == 0:
                        sp.dma_start(swap[:, :], io["k_swap"]).then_inc(loaded, 16)
                        sp.dma_start(rope[:, :, :], io["k_rope"]).then_inc(loaded, 16)
                sp.wait_ge(roped, 5)
                sp.dma_start(kT[64:128, 0, :], kT[0:64, 0, :]).then_inc(dup, 16)
                sp.dma_start(kT[0:64, 1, :], kT[64:128, 1, :]).then_inc(dup, 16)
                sp.wait_ge(dup, 32)

            @block.tensor
            def _(pe):
                def products(m):
                    pe.wait_ge(wq_loaded[m], 16)
                    if m >= 2:
                        pe.wait_ge(raw_ready, m - 1)
                    for n, (at, size) in enumerate(HALVES if m < 4 else XCHUNKS):
                        if n == 2:
                            pe.wait_ge(raw_ready, m)
                        for k in range(DK):
                            last = nc.tensor.matmul(c.ps[:, 2 * (m % 2) + n, 0:size], wq[:, k, m * P:(m + 1) * P], hT[:, k, at:at + size],
                                                    start=(k == 0), stop=(k == DK - 1))
                    last.then_inc(summed, 1)

                products(0)
                pe.wait_ge(loaded, 32)
                for m in range(5):
                    if m < 4:
                        products(m + 1)
                    pe.wait_ge(raw_ready, m + 1)
                    if m >= 2:
                        pe.wait_ge(roped, m - 1)
                    for n in range(2):
                        last = nc.tensor.matmul(c.ps[:, 4 + 2 * (m % 2) + n, :], swap[:, :], raw[:, m % 2, n * BANK:(n + 1) * BANK],
                                                start=True, stop=True)
                    last.then_inc(swapped, 1)

            @block.scalar
            def _(act):
                step = c.act.on(act)
                for m in range(5):
                    act.wait_ge(summed, m + 1)
                    if m >= 2:
                        act.wait_ge(roped, m - 1)
                    at = 2 * (m % 2)
                    step(nc.scalar.copy(raw[:, m % 2, 0:T], c.ps[:, at:at + 2, :].rearrange("p b t -> p (b t)")))
                    if m == 4:
                        step(nc.scalar.mul(kT[0:64, 0, T:TA], c.ps[0:64, 2, 0:TC], 0.125))
                        step(nc.scalar.mul(kT[64:128, 1, T:TA], c.ps[64:128, 2, 0:TC], 0.125))
                    act.nop().then_inc(raw_ready, 1)

            @block.vector
            def _(dve):
                step = c.dve.on(dve)
                for m in range(5):
                    dve.wait_ge(swapped, m + 1)
                    sw = c.ps[:, 4 + 2 * (m % 2):6 + 2 * (m % 2), :].rearrange("p b t -> p (b t)")
                    for lo, hi, dst, s in ([(0, P, qT[:, m, :], 1.0)] if m < 4 else
                                           [(0, 64, kT[0:64, 0, 0:T], 0.125), (64, P, kT[64:128, 1, 0:T], 0.125)]):
                        step(nc.vector.scalar_tensor_tensor(dst, sw[lo:hi, :], s, rope[lo:hi, 1, :], ALU.mult, ALU.mult))
                        step(nc.vector.scalar_tensor_tensor(raw[lo:hi, m % 2, 0:T], raw[lo:hi, m % 2, 0:T], s, rope[lo:hi, 0, :],
                                                            ALU.mult, ALU.mult))
                        step(nc.vector.tensor_tensor(dst, dst, raw[lo:hi, m % 2, 0:T], ALU.add))
                    dve.nop().then_inc(roped, 1)
    token_major(c, "v_a", [(0, w_in[:, :, OFF_VA:OFF_VA + P])], P, hT, plain_blocks(NBA), lambda b: va[:, b, :])
    with ExitStack() as tmp:
        W = 3 * P
        mask = c.sb("band", [P, W], tmp)
        sink = c.sb("sink", [P, AH], tmp)
        lg = c.sb("lg", [P, 2, 2, W + TC + 1], tmp)
        st = c.sb("st", [P, 2, 3, 2], tmp)
        pt = c.sb("pt", [P, 2, 2, 5, P], tmp)
        load_all(c, "band_loaded", [(mask[:, :], io["k_band"]), (sink[:, :], bass.AP(io["attn_sink"].tensor, 0, [[0, P], [1, AH]]))])
        units = [(n, g) for n in range(NB) for g in range(AH // 2)]
        sc_ready, sc_band_read, sc_ctx_read = c.sem("aw_scores"), c.sem("aw_band_read"), c.sem("aw_ctx_read")
        max_ready, exp_ready, p_ready, t_ready = c.sem("aw_max"), c.sem("aw_exp"), c.sem("aw_p"), c.sem("aw_t")
        t_dve, t_act, pv_ready, y_ready = c.sem("aw_t_dve"), c.sem("aw_t_act"), c.sem("aw_pv"), c.sem("aw_y")

        def band(n):
            lo, hi = max(0, (n - 1) * P), min(T, (n + 2) * P)
            return lo, hi, lo - (n - 1) * P

        with nc.Block() as block:
            @block.tensor
            def _(pe):
                def scores(u):
                    n, g = units[u]
                    lo, hi, off = band(n)
                    if u >= 1:
                        pe.wait_ge(sc_band_read, u)
                        pe.wait_ge(sc_ctx_read, u)
                    for h in range(2):
                        r = slice(64 * h, 64 * h + 64)
                        q = qT[r, g, n * P:(n + 1) * P]
                        nc.tensor.matmul(c.ps[:, h, 0:hi - lo], q, kT[r, g // 2, lo:hi], start=True, stop=True)
                        last = nc.tensor.matmul(c.ps[:, 2 + h, 0:TC], q, kT[r, g // 2, T:TA], start=True, stop=True)
                    last.then_inc(sc_ready, 1)
                def turn(u):
                    lo, hi, off = band(units[u][0])
                    nk = (hi - lo) // P + 2
                    pe.wait_ge(p_ready, u + 1)
                    if u >= 1:
                        pe.wait_ge(t_dve, u)
                        pe.wait_ge(t_act, u)
                    for x in range(2 * nk):
                        last = nc.tensor.transpose(c.ps[:, 4 + x // 4, (x % 4) * P:(x % 4 + 1) * P],
                                                   lg[:, u % 2, x // nk, (x % nk) * P:(x % nk + 1) * P], ident[:, :])
                    last.then_inc(t_ready, 1)

                def outputs(u):
                    n, g = units[u]
                    lo, hi, off = band(n)
                    nk = (hi - lo) // P + 2
                    pe.wait_ge(t_dve, u + 1)
                    pe.wait_ge(t_act, u + 1)
                    if u >= 1:
                        pe.wait_ge(y_ready, u)
                    for h in range(2):
                        for x in range(nk):
                            kb = lo // P + x if x < nk - 2 else NB + x - (nk - 2)
                            last = nc.tensor.matmul(c.ps[64 * h:64 * h + 64, 7, 0:P], va[:, kb, (g // 2) * 64:(g // 2) * 64 + 64],
                                                    pt[:, u % 2].rearrange("p h x q -> p (h x) q")[:, h * nk + x, :],
                                                    start=(x == 0), stop=(x == nk - 1))
                    last.then_inc(pv_ready, 1)
                scores(0)
                for u in range(len(units)):
                    if u + 1 < len(units):
                        scores(u + 1)
                    if u:
                        outputs(u - 1)
                    turn(u)
                outputs(len(units) - 1)

            @block.vector
            def _(dve):
                step = c.dve.on(dve)

                def top(u):
                    n, g = units[u]
                    lo, hi, off = band(n)
                    bw, s = hi - lo, u % 2
                    dve.wait_ge(sc_ready, u + 1)
                    if u >= 2:
                        dve.wait_ge(t_ready, u - 1)
                    step(nc.vector.tensor_tensor(lg[:, s, :, 0:bw], c.ps[:, 0:2, 0:bw],
                                                 mask[:, off:off + bw].unsqueeze(1).to_broadcast([P, 2, bw]), ALU.add))
                    dve.nop().then_inc(sc_band_read, 1)
                    step(nc.vector.tensor_copy(lg[:, s, :, bw + TC], sink[:, 2 * g:2 * g + 2]))
                    dve.wait_ge(sc_ctx_read, u + 1)
                    step(nc.vector.tensor_reduce(st[:, s, 0, :], lg[:, s, :, 0:bw + TC + 1], AX.X, ALU.max))
                    step(nc.vector.tensor_scalar(st[:, s, 0, :], st[:, s, 0, :], -1.0, None, ALU.mult))
                    dve.nop().then_inc(max_ready, 1)

                def divide(u):
                    lo, hi, off = band(units[u][0])
                    bw, s = hi - lo, u % 2
                    dve.wait_ge(exp_ready, u + 1)
                    step(nc.vector.reciprocal(st[:, s, 2, :], st[:, s, 1, :]))
                    for h in range(2):
                        step(nc.vector.tensor_scalar(lg[:, s, h, 0:bw + TC], lg[:, s, h, 0:bw + TC], st[:, s, 2, h:h + 1], None, ALU.mult))
                    dve.nop().then_inc(p_ready, 1)

                def turned(u):
                    dve.wait_ge(t_ready, u + 1)
                    if u >= 2:
                        dve.wait_ge(pv_ready, u - 1)
                    step(nc.vector.tensor_copy(pt[:, u % 2].rearrange("p h x q -> p (h x q)")[:, 0:BANK], c.ps[:, 4, :]))
                    dve.nop().then_inc(t_dve, 1)

                def output(u):
                    n, g = units[u]
                    dve.wait_ge(pv_ready, u + 1)
                    step(nc.vector.tensor_copy(mixT[:, 4 + g, n * P:(n + 1) * P], c.ps[:, 7, 0:P]))
                    dve.nop().then_inc(y_ready, 1)
                top(0)
                for u in range(len(units)):
                    if u:
                        turned(u - 1)
                    divide(u)
                    if u + 1 < len(units):
                        top(u + 1)
                    if u:
                        output(u - 1)
                turned(len(units) - 1)
                output(len(units) - 1)

            @block.scalar
            def _(act):
                step = c.act.on(act)

                def exps(u):
                    lo, hi, off = band(units[u][0])
                    bw, s = hi - lo, u % 2
                    act.wait_ge(sc_ready, u + 1)
                    if u >= 2:
                        act.wait_ge(t_ready, u - 1)
                    step(nc.scalar.copy(lg[:, s, :, bw:bw + TC], c.ps[:, 2:4, 0:TC]))
                    act.nop().then_inc(sc_ctx_read, 1)
                    act.wait_ge(max_ready, u + 1)
                    for h in range(2):
                        step(nc.scalar.activation(lg[:, s, h, 0:bw + TC + 1], lg[:, s, h, 0:bw + TC + 1], ACT.Exp,
                                                  bias=st[:, s, 0, h:h + 1], accum_out=st[:, s, 1, h:h + 1]))
                    act.nop().then_inc(exp_ready, 1)

                def turned(u):
                    lo, hi, off = band(units[u][0])
                    nk = (hi - lo) // P + 2
                    act.wait_ge(t_ready, u + 1)
                    if u >= 2:
                        act.wait_ge(pv_ready, u - 1)
                    flat = pt[:, u % 2].rearrange("p h x q -> p (h x q)")
                    rest = 2 * nk * P - BANK
                    step(nc.scalar.copy(flat[:, BANK:BANK + rest], c.ps[:, 5:7, :].rearrange("p b t -> p (b t)")[:, 0:rest]))
                    act.nop().then_inc(t_act, 1)
                exps(0)
                for u in range(len(units)):
                    if u:
                        turned(u - 1)
                    if u + 1 < len(units):
                        exps(u + 1)
                turned(len(units) - 1)


POOLS = (2, 4, 8, 16)
DIL, DH, DE = (1, 4, 16), 4, 64
SB_E = 128
O_POOL, O_DIL, O_SB, O_S5 = 0, 512, 2816, 4352
Y_POOL, Y_DIL, Y_SB, Y_S5, Y_TILES = 0, 4, 6, 10, 14
BRANCH_TILES = (4, 2, 4, 4)
SKEW = 384
ROUND = 1.5 * 2.0 ** 23
QT = 16
SC = 16


def second_block(c, io, xT, ident, ones, gains, final2):
    nc = c.nc
    with ExitStack() as s1:
        saved = nc.dram_tensor("x_saved2", (P, DK, T), F32, kind="Internal").ap()
        xnT = c.sb("xnT", [P, DK, T], s1)
        norm(c, "norm2", [(xT, at, n, lambda k: gains[:, 3, k:k + 1], None, at) for at, n in HALVES],
             ones, xnT, shift=False, save=(xT, saved))
        yT = c.sb("yT", [P, Y_TILES, T], s1)
        w_in = io["w_in_2"][0].rearrange("(k p) n -> p k n", p=P)
        with ExitStack() as s2:
            pool_branch(c, io, w_in, xnT, yT, s2)
        c.end_stage()
        with ExitStack() as s2:
            dilated_branch(c, io, w_in, xnT, yT, ident, s2)
        c.end_stage()
        with ExitStack() as s2:
            stick_branch(c, io, w_in, xnT, yT, ones, s2)
        c.end_stage()
        with ExitStack() as s2:
            s5_branch(c, io, w_in, xnT, yT, ident, xT, s2)
        c.end_stage()
        with ExitStack() as s2:
            merged = c.sb("merged", [P, DK, T], s2)
            with ExitStack() as s3:
                merge(c, io, xnT, yT, merged, s3)
            residual(c, io["w_out_2"][0], DK, merged, xT, None, "out2", saved)
    with ExitStack() as s2:
        hid = c.sb("hid2", [P, FK, T], s2)
        saved = nc.dram_tensor("x_saved3", (P, DK, T), F32, kind="Internal").ap()
        with ExitStack() as s3:
            h_hi, h_lo = split_pair(c, "h", [P, DK, T], s3)
            norm(c, "norm_ffn2", [(xT, at, n, lambda k: gains[:, 4, k:k + 1], None, at) for at, n in HALVES],
                 ones, hid, shift=False, save=(xT, saved))
            split(c, hid, h_hi, h_lo, "h2")
            w_parts = split_pair(c, "w", [P, 2, DK, P], s3)
            wbuf, act_out, _ = ffn_buffers(xT)
            silu_ready = c.sem("silu_ready")
            wv = io["w_up_2"][0].rearrange("(k p) n -> p k n", p=P)

            def act_part(eng, tile, s, i):
                c.act(nc.scalar.activation(act_out[:, s, :], c.ps[:, 4 * s:4 * s + 2, :].rearrange("p b t -> p (b t)"), ACT.Silu))
                eng.nop().then_inc(silu_ready, 1)

            def dve_part(eng, tile, s, i):
                eng.wait_ge(silu_ready, i * 2 + s + 1)
                c.dve(nc.vector.tensor_tensor(hid[:, bass.ds(tile, 1), :].rearrange("p o t -> p (o t)"),
                                              c.ps[:, 4 * s + 2:4 * s + 4, :].rearrange("p b t -> p (b t)"),
                                              act_out[:, s, :], ALU.mult))
            project(c, FK, 2, DK, lambda part, t: wv[:, :, bass.ds(t * P + part * FF, P)], lambda part: (h_hi, h_lo), HALVES,
                    lambda s, part, n: c.ps[:, 4 * s + 2 * part + n, :], act_part, dve_part, 1, 1, wbuf, w_parts)
        residual(c, io["w_down_2"][0], FK, hid, xT, None, "down2", saved)
    norm(c, "final2", [(xT, at, n, lambda k: final2[:, k:k + 1], None, at) for at, n in HALVES],
         ones, xT, shift=False)
    turn_out(c, io, xT, ident)


def turn_out(c, io, xT, ident):
    nc = c.nc
    with ExitStack() as tmp:
        rows = c.sb("out_rows", [P, 2, D], tmp)
        turned, dve_copied, act_copied = c.sem("out_turned"), c.sem("out_dve"), c.sem("out_act")
        stored = [c.sem(f"out_stored{s}") for s in range(2)]
        with nc.Block() as block:
            @block.tensor
            def _(pe):
                for b in range(NB):
                    if b >= 2:
                        pe.wait_ge(dve_copied, b - 1)
                        pe.wait_ge(act_copied, b - 1)
                    for k in range(DK):
                        last = nc.tensor.transpose(c.ps[:, 2 * (b % 2) + k // 4, (k % 4) * P:(k % 4 + 1) * P],
                                                   xT[:, k, b * P:(b + 1) * P], ident[:, :])
                    last.then_inc(turned, 1)

            @block.vector
            def _(dve):
                for b in range(NB):
                    dve.wait_ge(turned, b + 1)
                    if b >= 2:
                        dve.wait_ge(stored[b % 2], 16 * (b // 2))
                    nc.vector.tensor_copy(rows[:, b % 2, 0:BANK], c.ps[:, 2 * (b % 2), :]).then_inc(dve_copied, 1)

            @block.scalar
            def _(act):
                for b in range(NB):
                    act.wait_ge(turned, b + 1)
                    if b >= 2:
                        act.wait_ge(stored[b % 2], 16 * (b // 2))
                    nc.scalar.copy(rows[:, b % 2, BANK:D], c.ps[:, 2 * (b % 2) + 1, :]).then_inc(act_copied, 1)

            @block.sync
            def _(sp):
                for b in range(NB):
                    sp.wait_ge(dve_copied, b + 1)
                    sp.wait_ge(act_copied, b + 1)
                    sp.dma_start(io["out"][0, b * P:(b + 1) * P, :], rows[:, b % 2, :]).then_inc(stored[b % 2], 16)
                for s in range(2):
                    sp.wait_ge(stored[s], 16 * (NB // 2))


def pool_branch(c, io, w_in, xnT, yT, s2):
    nc = c.nc
    G = len(POOLS)
    u = c.sb("u_pool", [P, NB, G * P], s2)
    token_major(c, "u_pool", [(0, w_in[:, :, O_POOL:O_POOL + G * P])], G * P, xnT, plain_blocks(NB), lambda b: u[:, b, :])
    band, wg, sc = c.sb("pool_band", [P, G, 3, P], s2), c.sb("pool_w", [P, G, P], s2), c.sb("pool_sc", [P, G], s2)
    p = c.sb("pool_p", [P, 2, T], s2)
    load_all(c, "pool_loaded", [(band[:, :, :, :], io["k_pool"]), (wg[:, :, :], io["pool_w_2"][0].rearrange("g c d -> c g d")),
                                (sc[:, :], col(io["pool_scale_2"][0]))])
    meaned, p_ready, mixed, y_ready = (c.sem("pool_" + n) for n in ("mean", "p", "mix", "y"))
    flat = lambda b: c.ps[:, b:b + 2, :].rearrange("p b t -> p (b t)")
    with nc.Block() as block:
        @block.tensor
        def _(pe):
            def means(g):
                if g >= 2:
                    pe.wait_ge(p_ready, g - 1)
                for b in range(NB):
                    dst = c.ps[:, 2 * (g % 2) + b // 4, (b % 4) * P:(b % 4 + 1) * P]
                    last = nc.tensor.matmul(dst, u[:, b, g * P:(g + 1) * P], band[:, g, 0 if b == 0 else 1, :],
                                            start=True, stop=(b == 0))
                    if b:
                        last = nc.tensor.matmul(dst, u[:, b - 1, g * P:(g + 1) * P], band[:, g, 2, :], start=False, stop=True)
                last.then_inc(meaned, 1)
            means(0)
            for g in range(G):
                if g + 1 < G:
                    means(g + 1)
                pe.wait_ge(p_ready, g + 1)
                if g >= 2:
                    pe.wait_ge(y_ready, g - 1)
                for n in range(2):
                    last = nc.tensor.matmul(c.ps[:, 4 + 2 * (g % 2) + n, :], wg[:, g, :], p[:, g % 2, n * BANK:(n + 1) * BANK],
                                            start=True, stop=True)
                last.then_inc(mixed, 1)

        @block.vector
        def _(dve):
            for g in range(G):
                dve.wait_ge(meaned, g + 1)
                if g >= 2:
                    dve.wait_ge(mixed, g - 1)
                nc.vector.tensor_copy(p[:, g % 2, :], flat(2 * (g % 2))).then_inc(p_ready, 1)

        @block.scalar
        def _(act):
            for g in range(G):
                act.wait_ge(mixed, g + 1)
                nc.scalar.activation(yT[:, Y_POOL + g, :], flat(4 + 2 * (g % 2)), ACT.Copy, scale=sc[:, g:g + 1]).then_inc(y_ready, 1)


def dilated_branch(c, io, w_in, xnT, yT, ident, s2):
    nc = c.nc
    ROW = DH * DE + DH
    o = c.sb("o_dil", [P, 3, NB, ROW], s2)
    stat = c.sb("stat", [P, 3, NB, 3, DH], s2)
    scratch = nc.dram_tensor("dil_scratch", (2, T, ROW), F32, kind="Internal").ap()
    skewed = nc.dram_tensor("bias_scratch", (3, DH, P, SKEW), F32, kind="Internal").ap()
    with ExitStack() as tmp:
        rel, oh = c.sb("rel", [32, 3 * DH], tmp), c.sb("onehot", [32, 3, SKEW], tmp)
        off = c.sb("bias_off", [DH, 3, SKEW], tmp)
        load_all(c, "rel_loaded", [(rel[:, :], io["rel_bias_2"]), (oh[:, :, :], io["k_onehot"]), (off[:, :, :], io["k_skewmask"])])
        summed, ready, stored = c.sem("rel_sum"), c.sem("rel_ready"), c.sem("rel_stored")
        with nc.Block() as block:
            @block.tensor
            def _(pe):
                for g in range(3):
                    last = nc.tensor.matmul(c.ps[0:DH, g, 0:SKEW], rel[:, g * DH:(g + 1) * DH], oh[:, g, :], start=True, stop=True)
                last.then_inc(summed, 1)

            @block.vector
            def _(dve):
                dve.wait_ge(summed, 1)
                nc.vector.tensor_tensor(off[:, :, :], off[:, :, :], c.ps[0:DH, 0:3, 0:SKEW], ALU.add).then_inc(ready, 1)

            @block.sync
            def _(sp):
                sp.wait_ge(ready, 1)
                for g in range(3):
                    sp.dma_start(skewed[g], off[:, g, :].unsqueeze(1).to_broadcast([DH, P, SKEW])).then_inc(stored, 16)
                sp.wait_ge(stored, 48)

    for g, dil in enumerate(DIL):
        c.end_stage()
        with ExitStack() as tmp:
            dilated_group(c, w_in, xnT, ident, o, stat, skewed, g, dil, tmp)

    c.end_stage()
    lse = o[:, :, :, DH * DE:ROW]
    with nc.Block() as block:
        ln_ready, lse_ready, stored, back = (c.sem("dil_" + n) for n in ("ln", "lse", "stored", "back"))

        @block.scalar
        def _(act):
            nc.scalar.activation(stat[:, :, :, 1, :], stat[:, :, :, 1, :], ACT.Ln).then_inc(ln_ready, 1)

        @block.vector
        def _(dve):
            step = c.dve.on(dve)
            dve.wait_ge(ln_ready, 1)
            for g in range(3):
                for par in range(2):
                    step(nc.vector.tensor_tensor(lse[:, g].rearrange("p b (h r) -> p b r h", r=2)[:, :, par, :],
                                                 stat[:, g, :, 1, 2 * par:2 * par + 2], stat[:, g, :, 0, 2 * par:2 * par + 2], ALU.subtract))
            dve.nop().then_inc(lse_ready, 1)

        @block.sync
        def _(sp):
            sp.wait_ge(lse_ready, 1)
            for r in range(4):
                sp.dma_start(scratch[0].rearrange("(b l r) x -> r l b x", b=2, r=4)[r], o[:, 1, 2 * r:2 * r + 2, :]).then_inc(stored, 16)
            sp.dma_start(scratch[1].rearrange("(l a) x -> l a x", a=NB), o[:, 2, :, :]).then_inc(stored, 16)
            sp.wait_ge(stored, 80)
            for g in range(2):
                sp.dma_start(o[:, 1 + g, :, :], scratch[g].rearrange("(b p) x -> p b x", p=P)).then_inc(back, 16)
            sp.wait_ge(back, 32)

    with ExitStack() as tmp:
        top = c.sb("dil_top", [P, NB, DH], tmp)
        with nc.Block() as block:
            sub_ready, e_ready, y_ready, turned = (c.sem("dily_" + n) for n in ("sub", "exp", "y", "turned"))

            @block.vector
            def _(dve):
                step = c.dve.on(dve)
                step(nc.vector.tensor_tensor(top[:, :, :], lse[:, 0], lse[:, 1], ALU.max))
                step(nc.vector.tensor_tensor(top[:, :, :], top[:, :, :], lse[:, 2], ALU.max))
                for g in range(3):
                    step(nc.vector.tensor_tensor(lse[:, g], lse[:, g], top[:, :, :], ALU.subtract))
                dve.nop().then_inc(sub_ready, 1)
                dve.wait_ge(e_ready, 1)
                step(nc.vector.tensor_tensor(top[:, :, :], lse[:, 0], lse[:, 1], ALU.add))
                step(nc.vector.tensor_tensor(top[:, :, :], top[:, :, :], lse[:, 2], ALU.add))
                step(nc.vector.reciprocal(top[:, :, :], top[:, :, :]))
                for b in range(NB):
                    for g in range(3):
                        v = o[:, g, b, 0:DH * DE].rearrange("p (h e) -> p h e", h=DH)
                        step(nc.vector.tensor_tensor(v, v, lse[:, g, b, :].unsqueeze(2).to_broadcast([P, DH, DE]), ALU.mult))
                        if g:
                            step(nc.vector.tensor_tensor(o[:, 0, b, 0:DH * DE], o[:, 0, b, 0:DH * DE], o[:, g, b, 0:DH * DE], ALU.add))
                    v = o[:, 0, b, 0:DH * DE].rearrange("p (h e) -> p h e", h=DH)
                    step(nc.vector.tensor_tensor(v, v, top[:, b, :].unsqueeze(2).to_broadcast([P, DH, DE]), ALU.mult))
                    dve.nop().then_inc(y_ready, 1)

            @block.tensor
            def _(pe):
                for b in range(NB):
                    pe.wait_ge(y_ready, b + 1)
                    for m in range(2):
                        last = nc.tensor.transpose(c.ps[:, 2 * m + b // 4, (b % 4) * P:(b % 4 + 1) * P],
                                                   o[:, 0, b, m * P:(m + 1) * P], ident[:, :])
                last.then_inc(turned, 1)

            @block.scalar
            def _(act):
                step = c.act.on(act)
                act.wait_ge(sub_ready, 1)
                for g in range(3):
                    step(nc.scalar.activation(lse[:, g], lse[:, g], ACT.Exp))
                act.nop().then_inc(e_ready, 1)
                act.wait_ge(turned, 1)
                for m in range(2):
                    step(nc.scalar.copy(yT[:, Y_DIL + m, :], c.ps[:, 2 * m:2 * m + 2, :].rearrange("p b t -> p (b t)")))


def dilated_group(c, w_in, xnT, ident, o, stat, skewed, g, dil, tmp):
    nc = c.nc
    qk = c.sb("qk_dil", [P, 4, T], tmp)
    v = c.sb("v_dil", [P, NB, DH * DE], tmp)
    bias = c.sb("bias_dil", [P, 2, DH, P], tmp)
    at = O_DIL + g * 256
    copy_wide(c, f"qk_dil{g}", w_in, [(at, at + 256), (at + 768, at + 1024)], 4, xnT, qk)

    def tokens(b):
        if dil == 1:
            return lambda ap: ap[:, b * P:(b + 1) * P], b > 0
        if dil == 4:
            at = b // 2 + BANK * (b % 2)
            return lambda ap: ap[:, at:at + BANK - 3:4], b % 2 > 0
        return lambda ap: ap[:, b:T - 7 + b:8], False

    cut = [tokens(b) for b in range(NB)]
    token_major(c, f"v_dil{g}", [(0, w_in[:, :, O_DIL + 1536 + g * 256:O_DIL + 1536 + (g + 1) * 256])], DH * DE, xnT,
                [lambda src, k, b=b: cut[b][0](src[:, k, :]) for b in range(NB)], lambda b: v[:, b, :])
    row = skewed.tensor
    pairs = []
    for m in range(DH):
        head = 2 * (m % 2) + m // 2
        at = (g * DH + head) * P * SKEW
        pairs += [(bias[:, 0, m, :], bass.AP(row, at + 127 + P, [[SKEW - 1, P], [1, P]])),
                  (bias[:, 1, m, :], bass.AP(row, at + 127, [[SKEW - 1, P], [1, P]]))]
    load_all(c, f"bias_loaded{g}", pairs)

    lg = c.sb("lg_dil", [P, 2, 2, DH * P], tmp)
    pt = c.sb("pt_dil", [P, 2, 2, DH * P], tmp)
    (sc_ready, sc_read, max_ready, exp_ready, t_ready, t_copied, pv_ready, o_ready, t2_copied) = (
        c.sem(f"d{g}_{n}") for n in ("scores", "scores_read", "max", "exp", "t", "t_dve", "pv", "o", "t_act"))
    with nc.Block() as block:
        @block.tensor
        def _(pe):
            def scores(b):
                if b:
                    pe.wait_ge(sc_read, b)
                mine, prev = cut[b]
                for part in range(1 + prev):
                    for h in range(DH):
                        r, t = slice(64 * (h % 2), 64 * (h % 2) + 64), h // 2
                        last = nc.tensor.matmul(c.ps[:, 2 * part + h % 2, t * P:(t + 1) * P], mine(qk[r, t, :]),
                                                cut[b - part][0](qk[r, 2 + t, :]), start=True, stop=True)
                last.then_inc(sc_ready, 1)
            def turn(b):
                pe.wait_ge(exp_ready, b + 1)
                if b:
                    pe.wait_ge(t_copied, b)
                    pe.wait_ge(t2_copied, b)
                for part in range(1 + cut[b][1]):
                    for m in range(DH):
                        last = nc.tensor.transpose(c.ps[:, 4 + part, m * P:(m + 1) * P], lg[:, b % 2, part, m * P:(m + 1) * P], ident[:, :])
                last.then_inc(t_ready, 1)

            def outputs(b):
                prev = cut[b][1]
                pe.wait_ge(t_copied, b + 1)
                pe.wait_ge(t2_copied, b + 1)
                if b >= 2:
                    pe.wait_ge(o_ready, b - 1)
                for m in range(DH):
                    h = 2 * (m % 2) + m // 2
                    for part in range(1 + prev):
                        last = nc.tensor.matmul(c.ps[:, 6 + b % 2, h * DE:(h + 1) * DE], pt[:, b % 2, part, m * P:(m + 1) * P],
                                                v[:, b - part, h * DE:(h + 1) * DE], start=(part == 0), stop=(part == prev))
                last.then_inc(pv_ready, 1)
            scores(0)
            for b in range(NB):
                if b + 1 < NB:
                    scores(b + 1)
                if b:
                    outputs(b - 1)
                turn(b)
            outputs(NB - 1)

        @block.vector
        def _(dve):
            step = c.dve.on(dve)

            def top(b):
                s, parts = b % 2, 1 + cut[b][1]
                dve.wait_ge(sc_ready, b + 1)
                if b >= 2:
                    dve.wait_ge(t_ready, b - 1)
                for part in range(parts):
                    step(nc.vector.scalar_tensor_tensor(lg[:, s, part, :].rearrange("p (r x) -> p r x", r=2),
                                                        c.ps[:, 2 * part:2 * part + 2, 0:2 * P], 0.125,
                                                        bias[:, part].rearrange("p (r h) t -> p r (h t)", r=2), ALU.mult, ALU.add))
                dve.nop().then_inc(sc_read, 1)
                view = lg[:, s, 0:parts, :].rearrange("p a (m t) -> p m a t", m=DH)
                step(nc.vector.tensor_reduce(stat[:, g, b, 0, :], view, AX.XY, ALU.max))
                step(nc.vector.tensor_scalar(stat[:, g, b, 0, :], stat[:, g, b, 0, :], -1.0, None, ALU.mult))
                dve.nop().then_inc(max_ready, 1)

            def turned(b):
                dve.wait_ge(t_ready, b + 1)
                if b >= 2:
                    dve.wait_ge(pv_ready, b - 1)
                step(nc.vector.tensor_copy(pt[:, b % 2, 0, :], c.ps[:, 4, :]))
                dve.nop().then_inc(t_copied, 1)
                step(nc.vector.reciprocal(stat[:, g, b, 2, :], stat[:, g, b, 1, :]))

            def output(b):
                dve.wait_ge(pv_ready, b + 1)
                step(nc.vector.tensor_tensor(o[:, g, b, 0:DH * DE].rearrange("p (h r e) -> p r h e", r=2, e=DE),
                                             c.ps[:, 6 + b % 2, 0:DH * DE].rearrange("p (h r e) -> p r h e", r=2, e=DE),
                                             stat[:, g, b, 2, :].rearrange("p (r h) -> p r h", r=2).unsqueeze(3).to_broadcast([P, 2, 2, DE]), ALU.mult))
                dve.nop().then_inc(o_ready, 1)
            top(0)
            for b in range(NB):
                if b:
                    turned(b - 1)
                if b + 1 < NB:
                    top(b + 1)
                if b:
                    output(b - 1)
            turned(NB - 1)
            output(NB - 1)

        @block.scalar
        def _(act):
            step = c.act.on(act)

            def exps(b):
                s, parts = b % 2, 1 + cut[b][1]
                act.wait_ge(max_ready, b + 1)
                for m in range(DH):
                    e = lg[:, s, 0:parts, m * P:(m + 1) * P]
                    step(nc.scalar.activation(e, e, ACT.Exp, bias=stat[:, g, b, 0, m:m + 1], accum_out=stat[:, g, b, 1, m:m + 1]))
                act.nop().then_inc(exp_ready, 1)

            def turned(b):
                act.wait_ge(t_ready, b + 1)
                if b >= 2:
                    act.wait_ge(pv_ready, b - 1)
                if cut[b][1]:
                    step(nc.scalar.copy(pt[:, b % 2, 1, :], c.ps[:, 5, :]))
                act.nop().then_inc(t2_copied, 1)
            exps(0)
            for b in range(NB):
                if b:
                    turned(b - 1)
                if b + 1 < NB:
                    exps(b + 1)
            turned(NB - 1)


def stick_branch(c, io, w_in, xnT, yT, ones, s2):
    nc = c.nc
    H = 4
    qk = c.sb("qk_sb", [P, 2 * H, T], s2)
    v = c.sb("v_sb", [P, NB, H * SB_E], s2)
    copy_wide(c, "qk_sb", w_in, [(O_SB, O_SB + 1024)], 2 * H, xnT, qk, lambda m: float(SB_E) ** -0.5 if m < H else 1.0)
    token_major(c, "v_sb", [(0, w_in[:, :, O_SB + 1024:O_SB + 1536])], 512, xnT, plain_blocks(NB), lambda b: v[:, b, :])
    tri = c.sb("sb_tri", [P, 3, P], s2)
    load_all(c, "sb_tri_loaded", [(tri[:, :, :], c.io["k_stick"])])
    l, sp, dlt, acc, w = (c.sb("sb_" + n, [P, 2, BANK], s2) for n in ("l", "sp", "dlt", "acc", "w"))
    units = []
    for h in range(H):
        for half in range(2):
            kbs = list(range(4 * half + 3, -1, -1))
            units += [(h, half, kb, max(0, kb * P - half * BANK), n, len(kbs)) for n, kb in enumerate(kbs)]
    N = len(units)
    z_ready, l_ready, sp_ready, between, arg_ready, w_ready, pv_ready, y_ready, acc_zero = (
        c.sem("sb_" + n + "_done") for n in ("z", "l", "sp", "between", "arg", "w", "pv", "y", "zero"))

    def pair(u):
        return 2 * units[u][0] + units[u][1]

    with nc.Block() as block:
        @block.tensor
        def _(pe):
            def logits(u):
                h, half, kb, q0, n, _ = units[u]
                if u >= 2:
                    pe.wait_ge(sp_ready, u - 1)
                nc.tensor.matmul(c.ps[:, u % 2, q0:BANK], qk[:, H + h, kb * P:(kb + 1) * P],
                                 qk[:, h, half * BANK + q0:(half + 1) * BANK], start=True, stop=True).then_inc(z_ready, 1)

            def sums(u):
                h, half, kb, q0, n, _ = units[u]
                pe.wait_ge(sp_ready, u + 1)
                if u >= 2:
                    pe.wait_ge(arg_ready, u - 1)
                last = nc.tensor.matmul(c.ps[:, 2 + u % 2, q0:BANK], tri[:, 0, :], sp[:, u % 2, q0:BANK], start=True, stop=(n == 0))
                if n:
                    last = nc.tensor.matmul(c.ps[:, 2 + u % 2, q0:BANK], ones[:, :], acc[:, n % 2, q0:BANK], start=False, stop=True)
                last.then_inc(between, 1)

            def values(u):
                h, half, kb, q0, n, total = units[u]
                pe.wait_ge(w_ready, u + 1)
                if n == 0 and pair(u) >= 2:
                    pe.wait_ge(y_ready, pair(u) - 1)
                nc.tensor.matmul(c.ps[:, 4 + pair(u) % 2, q0:BANK], v[:, kb, h * SB_E:(h + 1) * SB_E], w[:, u % 2, q0:BANK],
                                 start=(n == 0), stop=(n == total - 1), skip_group_check=True).then_inc(pv_ready, 1)
            logits(0)
            for u in range(N + 1):
                if u + 1 < N:
                    logits(u + 1)
                if u < N:
                    sums(u)
                if u >= 1:
                    values(u - 1)

        @block.scalar
        def _(act):
            step = c.act.on(act)

            def soft(u):
                q0 = units[u][3]
                act.wait_ge(z_ready, u + 1)
                if u >= 2:
                    act.wait_ge(sp_ready, u - 1)
                t = l[:, u % 2, q0:BANK]
                step(nc.scalar.activation(t, c.ps[:, u % 2, q0:BANK], ACT.Abs))
                step(nc.scalar.activation(t, t, ACT.Exp, scale=-1.0))
                nc.scalar.activation(t, t, ACT.Ln, bias=1.0).then_inc(l_ready, 1)
            soft(0)
            for u in range(N):
                if u + 1 < N:
                    soft(u + 1)
                h, half, kb, q0, n, total = units[u]
                act.wait_ge(arg_ready, u + 1)
                if u >= 2:
                    act.wait_ge(pv_ready, u - 1)
                nc.scalar.activation(w[:, u % 2, q0:BANK], dlt[:, u % 2, q0:BANK], ACT.Exp).then_inc(w_ready, 1)
                if n == total - 1:
                    act.wait_ge(pv_ready, u + 1)
                    nc.scalar.copy(yT[:, Y_SB + h, half * BANK:(half + 1) * BANK], c.ps[:, 4 + pair(u) % 2, :]).then_inc(y_ready, 1)

        @block.vector
        def _(dve):
            step = c.dve.on(dve)

            def soft(u):
                h, half, kb, q0, n, total = units[u]
                s, q = u % 2, slice(q0, BANK)
                z, diag = c.ps[:, s, q], slice(q0, q0 + P)
                own = kb >= 4 * half
                dve.wait_ge(l_ready, u + 1)
                if u >= 2:
                    dve.wait_ge(between, u - 1)
                    dve.wait_ge(w_ready, u - 1)
                step(nc.vector.scalar_tensor_tensor(sp[:, s, q], z, 0.0, l[:, s, q], ALU.max, ALU.add))
                step(nc.vector.tensor_tensor(dlt[:, s, q], z, sp[:, s, q], ALU.subtract))
                if own:
                    step(nc.vector.tensor_tensor(sp[:, s, diag], sp[:, s, diag], tri[:, 1, :], ALU.mult))
                    step(nc.vector.tensor_tensor(dlt[:, s, diag], dlt[:, s, diag], tri[:, 2, :], ALU.add))
                if n == 0:
                    if u >= 1:
                        dve.wait_ge(between, u)
                    step(nc.vector.memset(acc[:, :, :], 0.0))
                if n + 1 < total:
                    if u >= 1:
                        dve.wait_ge(between, u)
                    step(nc.vector.tensor_tensor(acc[:, (n + 1) % 2, q], acc[:, n % 2, q], sp[:, s, q], ALU.add))
                dve.nop().then_inc(sp_ready, 1)
            soft(0)
            for u in range(N):
                if u + 1 < N:
                    soft(u + 1)
                q = slice(units[u][3], BANK)
                dve.wait_ge(between, u + 1)
                nc.vector.tensor_tensor(dlt[:, u % 2, q], dlt[:, u % 2, q], c.ps[:, 2 + u % 2, q], ALU.subtract).then_inc(arg_ready, 1)


def s5_branch(c, io, w_in, xnT, yT, ident, spare, s2):
    nc = c.nc
    uT = c.sb("uT", [P, 4, T], s2)
    copy_wide(c, "u_s5", w_in, [(O_S5, O_S5 + 512)], 4, xnT, uT)
    TWO_PI = float(2 * np.pi)
    C1 = 6.28125
    C2 = TWO_PI - C1
    SAFE = TWO_PI * (1 - 2.0 ** -21)
    small = c.sb("s5_small", [P, 14, QT], s2)
    re, im, dt, r, th, n_, ab, cr, ci, t0, t1, frac, f32_, lbr = (small[:, j, :] for j in range(14))
    bt = c.sb("s5_b", [P, 2, QT, SC], s2)
    bb = c.sb("s5_bb", [P, 2, QT, SC], s2)
    cc = c.sb("s5_c", [P, 2, 4, 64], s2)
    coarse, fine, rnd = (c.sb("s5_" + n, [P, QT, 32], s2) for n in ("coarse", "fine", "rnd"))
    ramp = c.sb("s5_ramp", [P, 32], s2)
    masks = c.sb("s5_masks", [P, 4, 10], s2)
    dsk = c.sb("s5_d", [P, 4], s2)
    half_pi = c.sb("half_pi", [P, 1], s2)
    gl = lambda ap: ap.rearrange("(q g) s -> g s q", g=2)
    pairs = []
    for gg in range(2):
        rows = slice(64 * gg, 64 * gg + 64)
        pairs += [(re[rows], gl(io["s5_a_re_2"][0])[gg]), (im[rows], gl(io["s5_a_im_2"][0])[gg]),
                  (dt[rows], bass.AP(io["s5_log_dt_2"].tensor, gg, [[0, 64], [2, QT]]))]
        pairs += [(bt[rows, j, :, :], io[n][0].rearrange("(q g) s ch -> g s q ch", g=2)[gg]) for j, n in enumerate(("s5_b_re_2", "s5_b_im_2"))]
    pairs += [(cc[:, j, :, :], io[n][0].rearrange("(y g) ch s -> (g ch) y s", y=4)) for j, n in enumerate(("s5_c_re_2", "s5_c_im_2"))]
    pairs += [(ramp[:, :], io["k_ramp"]), (masks[:, :, :], io["k_s5mask"]), (dsk[:, :], col(io["s5_d_2"][0]))]
    load_all(c, "s5_loaded", pairs)

    with nc.Block() as block:
        a_ready, v_ready = c.sem("s5_prep_act"), c.sem("s5_prep_dve")

        @block.scalar
        def _(act):
            step = c.act.on(act)
            step(nc.scalar.activation(dt, dt, ACT.Exp))
            act.nop().then_inc(a_ready, 1)
            act.wait_ge(v_ready, 1)
            step(nc.scalar.activation(r, t0, ACT.Exp))
            step(nc.scalar.activation(ab, th, ACT.Abs))
            step(nc.scalar.activation(t1, th, ACT.Sin))
            step(nc.scalar.activation(lbr, ab, ACT.Sin, scale=-1.0, bias=half_pi[:, 0:1]))
            act.nop().then_inc(a_ready, 1)

        @block.vector
        def _(dve):
            step = c.dve.on(dve)
            tt = lambda out, a, b, op: step(nc.vector.tensor_tensor(out, a, b, op))
            ts = lambda out, a, x, y, op0, op1=ALU.bypass: step(nc.vector.tensor_scalar(out, a, x, y, op0, op1))
            step(nc.vector.memset(half_pi[:, :], float(np.pi / 2)))
            dve.wait_ge(a_ready, 1)
            tt(t0, re, dt, ALU.mult)
            tt(th, im, dt, ALU.mult)
            ts(n_, th, 1 / TWO_PI, ROUND, ALU.mult, ALU.add)
            ts(n_, n_, ROUND, None, ALU.subtract)
            step(nc.vector.scalar_tensor_tensor(th, n_, -C1, th, ALU.mult, ALU.add))
            step(nc.vector.scalar_tensor_tensor(th, n_, -C2, th, ALU.mult, ALU.add))
            ts(th, th, float(np.float32(3.1415925)), float(np.float32(-3.1415925)), ALU.min, ALU.max)
            dve.nop().then_inc(v_ready, 1)
            ts(frac, th, 1 / TWO_PI, None, ALU.mult)
            ts(f32_, frac, 32.0, None, ALU.mult)
            ts(n_, f32_, ROUND, None, ALU.add)
            ts(n_, n_, ROUND, None, ALU.subtract)
            tt(f32_, f32_, n_, ALU.subtract)
            for dst, src in ((coarse, f32_), (fine, frac)):
                tt(dst[:, :, :], src.unsqueeze(2).to_broadcast([P, QT, 32]), ramp[:, :].unsqueeze(1).to_broadcast([P, QT, 32]), ALU.mult)
                ts(rnd[:, :, :], dst[:, :, :], ROUND, None, ALU.add)
                ts(rnd[:, :, :], rnd[:, :, :], ROUND, None, ALU.subtract)
                tt(dst[:, :, :], dst[:, :, :], rnd[:, :, :], ALU.subtract)
            dve.wait_ge(a_ready, 2)
            tt(lbr, lbr, r, ALU.mult)
            ts(lbr, lbr, -1.0, None, ALU.add)
            tt(t1, t1, r, ALU.mult)
            tt(cr, lbr, re, ALU.mult)
            tt(t0, t1, im, ALU.mult)
            tt(cr, cr, t0, ALU.add)
            tt(ci, t1, re, ALU.mult)
            tt(t0, lbr, im, ALU.mult)
            tt(ci, ci, t0, ALU.subtract)
            tt(t0, re, re, ALU.mult)
            tt(t1, im, im, ALU.mult)
            tt(t0, t0, t1, ALU.add)
            step(nc.vector.reciprocal(t0, t0))
            tt(cr, cr, t0, ALU.mult)
            tt(ci, ci, t0, ALU.mult)
            wide = lambda a: a.unsqueeze(2).to_broadcast([P, QT, SC])
            tt(bb[:, 0], bt[:, 0], wide(cr), ALU.mult)
            tt(bb[:, 1], bt[:, 1], wide(cr), ALU.mult)
            tt(bt[:, 0], bt[:, 0], wide(ci), ALU.mult)
            tt(bt[:, 1], bt[:, 1], wide(ci), ALU.mult)
            tt(bb[:, 0], bb[:, 0], bt[:, 1], ALU.subtract)
            tt(bb[:, 1], bb[:, 1], bt[:, 0], ALU.add)
            ts(cc[:, 1], cc[:, 1], -1.0, None, ALU.mult)

    yg = uT
    with ExitStack() as tmp:
        padded = c.sb("s5_pad", [P, 4, P], tmp)
        mats = c.sb("s5_mats", [P, 3, 4, P], tmp)
        cs = (yT[:, Y_S5:Y_S5 + 2, :], yT[:, Y_S5 + 2:Y_S5 + 4, :], spare[:, 4:6, :])
        g = c.sb("s5_g", [P, 2, 2, T], tmp)
        hh = spare[:, 0:4, :].rearrange("p (s j) t -> p s j t", s=2)
        x = c.sb("s5_x", [P, 4, T], tmp)
        y1 = c.sb("s5_y1", [P, T], tmp)
        pads, turned, mats_ready, bu_ready, ph_ready, cs_ready, g_ready, h_ready, y_sum, y_out, bu_read = (
            c.sem("s5_" + n) for n in ("pads", "turned", "mats", "bu", "ph", "cs", "g", "h", "ysum", "yout", "bu_read"))
        re_ps = c.ps[:, 0:2, :].rearrange("p b t -> p (b t)")
        im_ps = c.ps[:, 2:4, :].rearrange("p b t -> p (b t)")
        with nc.Block() as block:
            @block.tensor
            def _(pe):
                def turn(q):
                    pe.wait_ge(pads, q + 1)
                    if q:
                        pe.wait_ge(mats_ready, q)
                    for j in range(4):
                        last = nc.tensor.transpose(c.ps[:, 6, j * P:(j + 1) * P], padded[:, j, :], ident[:, :])
                    last.then_inc(turned, 1)

                def inputs(q):
                    pe.wait_ge(mats_ready, q + 1)
                    if q:
                        pe.wait_ge(bu_read, q)
                    for j in range(2):
                        for n in range(2):
                            last = nc.tensor.matmul(c.ps[:, 2 * j + n, :], mats[:, q % 3, j, :], uT[:, q // 4, n * BANK:(n + 1) * BANK],
                                                    start=True, stop=True)
                    last.then_inc(bu_ready, 1)

                def outputs(q):
                    pe.wait_ge(h_ready, q + 1)
                    if q % 4 == 0 and q:
                        pe.wait_ge(y_out, q // 4)
                    for n in range(2):
                        for j in range(2):
                            last = nc.tensor.matmul(c.ps[:, 4 + n, :], mats[:, q % 3, 2 + j, :], hh[:, q % 2, j, n * BANK:(n + 1) * BANK],
                                                    start=(q % 4 == 0 and j == 0), stop=(q % 4 == 3 and j == 1))
                    last.then_inc(y_sum, 1)

                turn(0)
                turn(1)
                inputs(0)
                for q in range(QT):
                    if q + 1 < QT:
                        inputs(q + 1)
                    if q + 2 < QT:
                        turn(q + 2)
                    if q:
                        outputs(q - 1)
                outputs(QT - 1)

            @block.gpsimd
            def _(pool):
                step = c.pool.on(pool)
                tt = lambda out, a, b, op: step(nc.gpsimd.tensor_tensor(out, a, b, op))

                def pad(q):
                    if q:
                        pool.wait_ge(turned, q)
                    for j in range(2):
                        tt(padded[:, j, :].rearrange("p (g ch) -> p g ch", g=8), bb[:, j, q, :].unsqueeze(1).to_broadcast([P, 8, SC]),
                           masks[:, q % 4, 0:8].unsqueeze(2).to_broadcast([P, 8, SC]), ALU.mult)
                        tt(padded[:, 2 + j, :].rearrange("p (g s) -> p g s", g=2), cc[:, j, q // 4, :].unsqueeze(1).to_broadcast([P, 2, 64]),
                           masks[:, q % 4, 8:10].unsqueeze(2).to_broadcast([P, 2, 64]), ALU.mult)
                    pool.nop().then_inc(pads, 1)
                for q in range(3):
                    pad(q)
                for q in range(QT):
                    s, w = q % 2, cs[q % 3]
                    pool.wait_ge(g_ready, q + 1)
                    if q >= 2:
                        pool.wait_ge(y_sum, q - 1)
                    tt(hh[:, s, 0, :], g[:, s, 0, :], w[:, 0, :], ALU.mult)
                    tt(y1[:, :], g[:, s, 1, :], w[:, 1, :], ALU.mult)
                    tt(hh[:, s, 0, :], hh[:, s, 0, :], y1[:, :], ALU.subtract)
                    tt(hh[:, s, 1, :], g[:, s, 0, :], w[:, 1, :], ALU.mult)
                    tt(y1[:, :], g[:, s, 1, :], w[:, 0, :], ALU.mult)
                    tt(hh[:, s, 1, :], hh[:, s, 1, :], y1[:, :], ALU.add)
                    pool.nop().then_inc(h_ready, 1)
                    if q + 3 < QT:
                        pad(q + 3)

            @block.vector
            def _(dve):
                step = c.dve.on(dve)
                tt = lambda out, a, b, op: step(nc.vector.tensor_tensor(out, a, b, op))

                def phase(q):
                    if q >= 3:
                        dve.wait_ge(h_ready, q - 2)
                    ph = cs[q % 3][:, 0, :]
                    tt(ph.rearrange("p (a b) -> p a b", b=32), coarse[:, q, :].unsqueeze(2).to_broadcast([P, 32, 32]),
                       fine[:, q, :].unsqueeze(1).to_broadcast([P, 32, 32]), ALU.add)
                    step(nc.vector.tensor_scalar(x[:, 0, :], ph, ROUND, None, ALU.add))
                    step(nc.vector.tensor_scalar(x[:, 0, :], x[:, 0, :], ROUND, None, ALU.subtract))
                    tt(ph, ph, x[:, 0, :], ALU.subtract)
                    dve.nop().then_inc(ph_ready, 1)

                def y_tile(m):
                    dve.wait_ge(y_sum, 4 * m + 4)
                    step(nc.vector.scalar_tensor_tensor(yg[:, m, :], uT[:, m, :], dsk[:, m:m + 1],
                                                        c.ps[:, 4:6, :].rearrange("p b t -> p (b t)"), ALU.mult, ALU.add))
                    dve.nop().then_inc(y_out, 1)
                phase(0)
                phase(1)
                for q in range(QT):
                    s, w = q % 2, cs[q % 3]
                    dve.wait_ge(bu_ready, q + 1)
                    dve.wait_ge(cs_ready, q + 1)
                    for j, (a, b) in enumerate(((re_ps, 0), (im_ps, 1), (im_ps, 0), (re_ps, 1))):
                        last = nc.vector.tensor_tensor(x[:, j, :], a, w[:, b, :], ALU.mult)
                        if j < 3:
                            last.then_inc(c.dve.sem, 1)
                            c.dve.n += 1
                    step(last)
                    dve.nop().then_inc(bu_read, 1)
                    last = nc.vector.tensor_tensor(x[:, 0, :], x[:, 0, :], x[:, 1, :], ALU.add)
                    last.then_inc(c.dve.sem, 1)
                    c.dve.n += 1
                    tt(x[:, 2, :], x[:, 2, :], x[:, 3, :], ALU.subtract)
                    if q >= 2:
                        dve.wait_ge(h_ready, q - 1)
                    for j in range(2):
                        step(nc.vector.tensor_tensor_scan(g[:, s, j, :], r[:, q:q + 1].to_broadcast([P, T]), x[:, 2 * j, :], 0.0,
                                                          ALU.mult, ALU.add))
                    dve.nop().then_inc(g_ready, 1)
                    if q + 2 < QT:
                        phase(q + 2)
                    if q % 4 == 1 and q > 1:
                        y_tile(q // 4 - 1)
                y_tile(3)

            @block.scalar
            def _(act):
                step = c.act.on(act)

                def matrices(q):
                    act.wait_ge(turned, q + 1)
                    if q >= 3:
                        act.wait_ge(y_sum, q - 2)
                    step(nc.scalar.copy(mats[:, q % 3].rearrange("p j x -> p (j x)"), c.ps[:, 6, :]))
                    act.nop().then_inc(mats_ready, 1)

                def tables(q):
                    act.wait_ge(ph_ready, q + 1)
                    w = cs[q % 3]
                    step(nc.scalar.activation(w[:, 1, :], w[:, 0, :], ACT.Sin, scale=SAFE))
                    step(nc.scalar.activation(w[:, 0, :], w[:, 0, :], ACT.Abs))
                    step(nc.scalar.activation(w[:, 0, :], w[:, 0, :], ACT.Sin, scale=-TWO_PI, bias=half_pi[:, 0:1]))
                    act.nop().then_inc(cs_ready, 1)
                for q in range(QT):
                    matrices(q)
                    tables(q)
    with nc.Block() as block:
        @block.scalar
        def _(act):
            step = c.act.on(act)
            step(nc.scalar.activation(yg[:, :, :], yg[:, :, :], ACT.Gelu_apprx_tanh))
    with ExitStack() as tmp:
        wbuf = c.sb("wbuf", [P, 2, 2, 4, P], tmp)
        sig = c.sb("s5_sig", [P, 2, T], tmp)
        sig_ready = c.sem("s5_sig_ready")
        wv = io["s5_w_glu_2"][0].rearrange("(k p) n -> p k n", p=P)

        def act_part(eng, tile, s, i):
            c.act(nc.scalar.activation(sig[:, s, :], c.ps[:, 4 * s + 2:4 * s + 4, :].rearrange("p b t -> p (b t)"), ACT.Sigmoid))
            eng.nop().then_inc(sig_ready, 1)

        def dve_part(eng, tile, s, i):
            eng.wait_ge(sig_ready, i * 2 + s + 1)
            c.dve(nc.vector.tensor_tensor(yT[:, bass.ds(tile + Y_S5, 1), :].rearrange("p o t -> p (o t)"),
                                          c.ps[:, 4 * s:4 * s + 2, :].rearrange("p b t -> p (b t)"), sig[:, s, :], ALU.mult))
        project(c, 4, 2, 4, lambda part, t: wv[:, :, bass.ds(t * P + part * 512, P)], lambda part: yg, HALVES,
                lambda s, part, n: c.ps[:, 4 * s + 2 * part + n, :], act_part, dve_part, 1, 1, wbuf)


def merge(c, io, xnT, yT, merged, s2):
    nc = c.nc
    M = DK // 2
    w_raw = c.sb("mg_raw", [P, 2, BANK], s2)
    w_hi, w_lo = split_pair(c, "mg_w", [P, 2, BANK], s2)
    s_hi, s_lo = split_pair(c, "mg_s", [P, 2, BANK], s2)
    sig = c.sb("sig", [P, M, BANK], s2)
    gate, wide = io["w_gate_2"][0], io["w_branch_2"][0]
    steps = [(b, k, g, k == 0, k == n - 1) for b in range(4) for g, n in ((True, DK), (False, BRANCH_TILES[b])) for k in range(n)]
    per = len(steps) // 2
    assert len(steps) % 2 == 0
    y_tile = [sum(BRANCH_TILES[:b]) for b in range(4)]
    loaded, hi_ready, lo_ready, used = ([c.sem(f"mg_{n}{s}") for s in range(2)] for n in ("loaded", "hi", "lo", "used"))
    gated, y_summed, y_taken, added = (c.sem("mg_" + n) for n in ("gated", "y_sum", "y_taken", "added"))

    def rounds(eng, body):
        with eng.Fori(0, 2) as n:
            with eng.Fori(0, 2) as h:
                body(n, h, n * 2 + h)

    def source(n, j):
        b, k, g, _, _ = steps[j]
        return (xnT[:, k] if g else yT[:, y_tile[b] + k])[:, bass.ds(n * BANK, BANK)]

    with nc.Block() as block:
        @block.sync
        def _(sp):
            def load(n, h, r):
                for j, (b, k, g, _, _) in enumerate(steps):
                    s = j % 2
                    sp.wait_ge(lo_ready[s], r * (2 * per) + (2 * (j // 2) + 2))
                    rows = gate[b, k * P:(k + 1) * P, bass.ds(h * BANK, BANK)] if g else \
                        wide[(y_tile[b] + k) * P:(y_tile[b] + k + 1) * P, bass.ds(h * BANK, BANK)]
                    sp.dma_start(w_raw[:, s, :], rows).then_inc(loaded[s], 16)
            rounds(sp, load)

        @block.scalar
        def _(act):
            act.nop().then_inc(gated, M)

            def split_and_gate(n, h, r):
                for j, (b, k, g, first, _) in enumerate(steps):
                    s = j % 2
                    act.wait_ge(used[s], r * per + (j // 2 + 1))
                    act.wait_ge(loaded[s], r * (16 * per) + 16 * (j // 2 + 1))
                    nc.scalar.copy(w_hi[:, s, :], w_raw[:, s, :]).then_inc(hi_ready[s], 1)
                    nc.scalar.copy(s_hi[:, s, :], source(n, j)).then_inc(hi_ready[s], 1)
                    if not g and first:
                        act.wait_ge(used[(j - 1) % 2], r * per + ((j - 1) // 2 + 2))
                        act.wait_ge(added, r * (4 * M) + (b * M + M))
                        for m in range(M):
                            nc.scalar.activation(sig[:, m, :], c.ps[:, m, :], ACT.Sigmoid).then_inc(gated, 1)
            rounds(act, split_and_gate)

        @block.vector
        def _(dve):
            for s in range(2):
                dve.nop().then_inc(lo_ready[s], 2)
            dve.nop().then_inc(y_taken, M)

            def split_and_take(n, h, r):
                def take(b):
                    for m in range(M):
                        dve.wait_ge(y_summed, r * (4 * M) + (b * M + m + 1))
                        dve.wait_ge(gated, r * (4 * M) + (b * M + m + 1 + M))
                        if b == 0:
                            if m == 0:
                                dve.wait_ge(added, r * (4 * M) + M)
                            dst = merged[:, bass.ds(h * M + m, 1), bass.ds(n * BANK, BANK)].rearrange("p o t -> p (o t)")
                        else:
                            dst = sig[:, m, :]
                        nc.vector.tensor_tensor(dst, c.ps[:, M + m, :], sig[:, m, :], ALU.mult).then_inc(y_taken, 1)

                for j, (b, k, g, first, _) in enumerate(steps):
                    s = j % 2
                    dve.wait_ge(hi_ready[s], r * (2 * per) + (2 * (j // 2) + 2))
                    nc.vector.tensor_tensor(s_lo[:, s, :], source(n, j), s_hi[:, s, :].bitcast(F32), ALU.subtract).then_inc(lo_ready[s], 1)
                    nc.vector.tensor_tensor(w_lo[:, s, :], w_raw[:, s, :], w_hi[:, s, :].bitcast(F32), ALU.subtract).then_inc(lo_ready[s], 1)
                    if g and first and b:
                        take(b - 1)
                take(3)
            rounds(dve, split_and_take)

        @block.gpsimd
        def _(pool):
            pool.nop().then_inc(added, M)
            waited = c.sem("mg_waited")

            def add(n, h, r):
                for b in range(4):
                    for m in range(M):
                        pool.wait_ge(y_taken, r * (4 * M) + (b * M + m + 1 + M))
                        if b == 0:
                            pool.nop().then_inc(added, 1)
                        else:
                            pool.wait_ge(added, r * (4 * M) + (b * M + m + 1))
                            pool.nop().then_inc(waited, 1)
                            dst = merged[:, bass.ds(h * M + m, 1), bass.ds(n * BANK, BANK)].rearrange("p o t -> p (o t)")
                            nc.gpsimd.tensor_tensor(dst, dst, sig[:, m, :], ALU.add).then_inc(added, 1)
            rounds(pool, add)

        @block.tensor
        def _(pe):
            for s in range(2):
                pe.nop().then_inc(used[s], 1)

            def products(n, h, r):
                for j, (b, k, g, first, last) in enumerate(steps):
                    s = j % 2
                    if first and g:
                        pe.wait_ge(gated, r * (4 * M) + (b * M + M))
                    elif first:
                        pe.wait_ge(y_taken, r * (4 * M) + (b * M + M))
                    pe.wait_ge(hi_ready[s], r * (2 * per) + (2 * (j // 2) + 2))
                    for i, (wp, sp) in enumerate(((w_hi, s_hi), (w_hi, s_lo), (w_lo, s_hi))):
                        if i:
                            pe.wait_ge(lo_ready[s], r * (2 * per) + (2 * (j // 2) + 2 + i))
                        for m in range(M):
                            bank, cols = c.ps[:, m if g else M + m, :], slice(m * P, (m + 1) * P)
                            ins = nc.tensor.matmul(bank, wp[:, s, cols], sp[:, s, :], start=(first and i == 0), stop=(last and i == 2))
                            if last and not g and i == 2 and m < M - 1:
                                ins.then_inc(y_summed, 1)
                    ins.then_inc(used[s], 1)
                    if last and not g:
                        pe.wait_ge(used[s], r * per + (j // 2 + 2))
                        pe.nop().then_inc(y_summed, 1)
            rounds(pe, products)


def shape_constants():
    f = np.float32
    sel = np.zeros((MH, MH, P), f)
    for h in range(MH):
        sel[h, h] = 1
    first = np.arange(TA) % P == 0
    reset = np.stack([np.where(first, 0, 1), np.where(first, NEG, 0)]).astype(f)
    j, i = np.arange(NBA)[:, None], np.arange(NBA)[None]
    later = np.stack([(i - 1 > j) * 1.0, (i > 0) * np.ones((NBA, 1))]).astype(f)
    s, t = np.arange(P)[:, None], np.arange(P)[None]
    tri = np.stack([np.where(s <= t, 0, NEG), np.where(s >= t, 0, NEG)], 1).astype(f)
    q, k = np.arange(P)[:, None], np.arange(3 * P)[None]
    band = np.where((k >= q) & (k <= q + 2 * P), 0, NEG).astype(f)
    e = np.arange(P) % 64
    pairs = 16
    inv = (f(10000.0) ** (-np.arange(pairs, dtype=f) / f(pairs))).astype(f)
    tok = np.arange(T)
    pos = np.where((e < 32)[:, None], (tok // 64)[None], (tok % 64)[None]).astype(f)
    ang = (pos * inv[e % pairs][:, None]).astype(f)
    rope = np.stack([np.cos(ang), np.sin(ang)], 1).astype(f)
    swap = np.zeros((P, P), f)
    for m in range(P):
        if (m % 32) < 16:
            swap[m + 16, m] = -1
        else:
            swap[m - 16, m] = 1
    return {"k_ident": np.eye(P, dtype=f), "k_ones": np.ones((P, P), f), "k_sel": sel,
            "k_reset": np.broadcast_to(reset, (MH, 2, TA)).copy(),
            "k_later": np.broadcast_to(later, (MH, 2, NBA, NBA)).copy(), "k_tri": tri, "k_band": band,
            "k_rope": rope, "k_swap": swap, **second_constants()}


def second_constants():
    f = np.float32
    pool = np.zeros((P, len(POOLS), 3, P), f)
    for g, w in enumerate(POOLS):
        for t in range(P):
            lo = max(t + 1 - w, 0)
            pool[lo:t + 1, g, 0, t] = f(1) / f(t + 1 - lo)
            pool[lo:t + 1, g, 1, t] = f(1) / f(w)
            if t + 1 - w < 0:
                pool[P + t + 1 - w:P, g, 2, t] = f(1) / f(w)
            pool[t, g, 0:2, t] -= 1
    x = np.arange(SKEW)
    dist = 255 - x
    valid = (dist >= 0) & (dist <= P)
    onehot, skewmask = np.zeros((32, 3, SKEW), f), np.zeros((DH, 3, SKEW), f)
    for g, dil in enumerate(DIL):
        ok = valid if dil < 16 else valid & (dist % 2 == 0) & (dist < P)
        skewmask[:, g] = np.where(ok, 0, NEG)
        d = np.clip(dist, 0, P) * (dil if dil < 16 else 8)
        large = 16 + (np.log(np.maximum(d, 1).astype(f) / f(16)) / f(np.log(2048 / 16)) * f(16)).astype(np.int32)
        bucket = np.where(d < 16, d, np.minimum(large, 31))
        onehot[bucket, g, x] = ok
    a, b = np.arange(P)[:, None], np.arange(P)[None]
    stick = np.stack([(a > b) * 1.0, (a < b) * 1.0, np.where(a < b, 0, NEG)], 1).astype(f)
    m = np.zeros((P, 4, 10), f)
    p = np.arange(P)
    for q in range(4):
        m[p, q, 2 * q + p // 64] = 1
        for gg in range(2):
            m[p // SC == 2 * q + gg, q, 8 + gg] = 1
    return {"k_pool": pool, "k_onehot": onehot, "k_skewmask": skewmask, "k_stick": stick,
            "k_ramp": np.broadcast_to(np.arange(32, dtype=f), (P, 32)).copy(), "k_s5mask": m}


_INS = ["x", "c", "ctx", "c_ctx", "w_ada", "b_ada", "norm_mix", "norm_ffn", "w_in", "gate_b", "qk_conv_w",
        "qk_conv_b", "mlstm_norm", "attn_sink", "w_out", "w_up", "ffn_conv_w", "ffn_conv_b", "w_down",
        "final_norm", "attn_norm_g_2", "w_in_2", "pool_w_2", "pool_scale_2", "rel_bias_2", "s5_a_re_2",
        "s5_a_im_2", "s5_log_dt_2", "s5_b_re_2", "s5_b_im_2", "s5_c_re_2", "s5_c_im_2", "s5_d_2",
        "s5_w_glu_2", "w_branch_2", "w_gate_2", "w_out_2", "ffn_norm_g_2", "w_up_2", "w_down_2",
        "final_norm_g_2"]


def launch_arrays(inputs):
    arrays = {f"in_{n}": np.ascontiguousarray(inputs[n]) for n in _INS}
    arrays.update({f"in_{n}": a for n, a in shape_constants().items()})
    return arrays


def declare_and_build(nc, arrays):
    io = {n[3:]: nc.dram_tensor(n, a.shape, mybir.dt.from_np(a.dtype), kind="ExternalInput").ap()
          for n, a in arrays.items()}
    io["out"] = nc.dram_tensor("out_0", (1, T, D), F32, kind="ExternalOutput").ap()
    build(nc, io)


def kernel(**inputs):
    import concourse.bacc as _bacc
    from concourse.bass_utils import run_bass_kernel_spmd as _run

    nc = _bacc.Bacc("TRN2", target_bir_lowering=False, num_devices=1)
    arrays = launch_arrays(inputs)
    declare_and_build(nc, arrays)
    r = _run(nc, [arrays], core_ids=[0])
    return r.results[0]["out_0"]
```
